# Optimizing a Trainium2 kernel written in Bass

```python
import jax, jax.numpy as jnp
from jax import lax
import numpy as np

D_MODEL = 1024
BATCH = 1
SEQ = 256
DEPTH = 2

GRID_W = 64
N_META = 16
HEAD_DIM = 64
N_Q_HEADS = D_MODEL // HEAD_DIM
N_KV_HEADS = 4
GROUP = N_Q_HEADS // N_KV_HEADS
QKV_WIDTH = (N_Q_HEADS + 2 * N_KV_HEADS) * HEAD_DIM
Q_BLOCK = 128
ROPE_AXIS = HEAD_DIM // 2
ROPE_THETA = 10000.0
D_RNN = D_MODEL
N_RG_BLOCKS = 4
RG_BW = D_RNN // N_RG_BLOCKS
CONV_W = 4
CONV_LEFT = 2
RG_C = 8.0
D_FF = 2816
N_ATTN = (DEPTH + 1) // 2
N_REC = DEPTH // 2
NORM_EPS = 1e-6

kernel_name = "hybrid_gqa_rglru_macaron_encoder"

def rms_norm(x, g):
    xf = x.astype(jnp.float32)
    y = xf * lax.rsqrt(jnp.mean(xf * xf, axis=-1, keepdims=True) + NORM_EPS)
    return (y * g.astype(jnp.float32)).astype(x.dtype)

def swiglu(x, w_in, w_out):
    h = x @ w_in
    return (jax.nn.silu(h[..., :D_FF]) * h[..., D_FF:]) @ w_out

def axial_rope_tables(n_tok):
    rows = n_tok // GRID_W
    row = jnp.repeat(jnp.arange(rows, dtype=jnp.float32), GRID_W)
    col = jnp.tile(jnp.arange(GRID_W, dtype=jnp.float32), rows)
    zeros = jnp.zeros((N_META,), jnp.float32)
    row = jnp.concatenate([zeros, row])
    col = jnp.concatenate([zeros, col])
    inv = 1.0 / (ROPE_THETA ** (jnp.arange(0, ROPE_AXIS, 2, dtype=jnp.float32) / ROPE_AXIS))
    theta = jnp.concatenate([row[:, None] * inv, col[:, None] * inv], axis=-1)
    return jnp.cos(theta), jnp.sin(theta)

def apply_rope(x, cos, sin):
    shape = (1, cos.shape[0]) + (1,) * (x.ndim - 3) + (ROPE_AXIS,)
    c = cos.reshape(shape).astype(x.dtype)
    s = sin.reshape(shape).astype(x.dtype)
    x1, x2 = x[..., :ROPE_AXIS], x[..., ROPE_AXIS:]
    return jnp.concatenate([x1 * c - x2 * s, x1 * s + x2 * c], axis=-1)

def attention_mixer(x, w_qkv, q_gain, k_gain, w_o, cos, sin):
    B, L, _ = x.shape
    qkv = x @ w_qkv
    q = qkv[..., :N_Q_HEADS * HEAD_DIM].reshape(B, L, N_KV_HEADS, GROUP, HEAD_DIM)
    k = qkv[..., N_Q_HEADS * HEAD_DIM:(N_Q_HEADS + N_KV_HEADS) * HEAD_DIM].reshape(B, L, N_KV_HEADS, HEAD_DIM)
    v = qkv[..., (N_Q_HEADS + N_KV_HEADS) * HEAD_DIM:].reshape(B, L, N_KV_HEADS, HEAD_DIM)
    q = apply_rope(rms_norm(q, q_gain), cos, sin) * (HEAD_DIM ** -0.5)
    k = apply_rope(rms_norm(k, k_gain), cos, sin)

    def attend(qb):
        s = jnp.einsum('bqhgd,bkhd->bhgqk', qb, k).astype(jnp.float32)
        p = jax.nn.softmax(s, axis=-1).astype(v.dtype)
        return jnp.einsum('bhgqk,bkhd->bqhgd', p, v)

    o_meta = attend(q[:, :N_META])
    n_real = L - N_META
    n_blk = n_real // Q_BLOCK
    qr = q[:, N_META:].reshape(B, n_blk, Q_BLOCK, N_KV_HEADS, GROUP, HEAD_DIM).swapaxes(0, 1)
    o_real = lax.map(attend, qr).swapaxes(0, 1).reshape(B, n_real, N_KV_HEADS, GROUP, HEAD_DIM)
    o = jnp.concatenate([o_meta, o_real], axis=1).reshape(B, L, N_Q_HEADS * HEAD_DIM)
    return o @ w_o

def _lin_combine(left, right):
    a1, b1 = left
    a2, b2 = right
    return a1 * a2, a2 * b1 + b2

def recurrent_mixer(x, w_in, conv_w, conv_b, gate_w, gate_b, lam, w_out):
    B, L, _ = x.shape
    u = x @ w_in
    gate = jax.nn.gelu(u[..., :D_RNN])
    xr = u[..., D_RNN:]
    xp = jnp.pad(xr, ((0, 0), (CONV_LEFT, CONV_W - 1 - CONV_LEFT), (0, 0)))
    xc = conv_b + sum(xp[:, j:j + L] * conv_w[j] for j in range(CONV_W))
    xb = xc.reshape(B, L, N_RG_BLOCKS, RG_BW)
    g = jnp.einsum('blhi,dghij->dgblhj', xb, gate_w).reshape(2, 2, B, L, D_RNN)
    g = jax.nn.sigmoid((g + gate_b[:, :, None, None, :]).astype(jnp.float32))
    r, i = g[:, 0], g[:, 1]
    log_a = -RG_C * r * jax.nn.softplus(-lam.astype(jnp.float32))[:, None, None, :]
    a = jnp.exp(log_a)
    b = jnp.sqrt(-jnp.expm1(2.0 * log_a)) * i * xc.astype(jnp.float32)[None]
    _, h_f = lax.associative_scan(_lin_combine, (a[0], b[0]), axis=1)
    _, h_b = lax.associative_scan(_lin_combine, (a[1], b[1]), axis=1, reverse=True)
    y = (h_f + h_b).astype(x.dtype) * gate
    return y @ w_out

def setup_inputs(seed: int = 0) -> dict:
    key = jax.random.key(seed)
    ks = jax.random.split(key, 20)
    nrm = lambda k, shape, fan_in: jax.random.normal(k, shape, jnp.float32) * (fan_in ** -0.5)
    a0 = jax.random.uniform(ks[14], (N_REC, 2, D_RNN), jnp.float32, 0.9, 0.999)
    return {
        "x": jax.random.normal(ks[0], (BATCH, SEQ, D_MODEL), jnp.float32),
        "meta_tokens": jax.random.normal(ks[1], (N_META, D_MODEL), jnp.float32),
        "norm_gains": 1.0 + 0.05 * jax.random.normal(ks[2], (DEPTH, 6, D_MODEL), jnp.float32),
        "ffn_w_in": nrm(ks[3], (DEPTH, 2, D_MODEL, 2 * D_FF), D_MODEL),
        "ffn_w_out": nrm(ks[4], (DEPTH, 2, D_FF, D_MODEL), D_FF),
        "attn_w_qkv": nrm(ks[5], (N_ATTN, D_MODEL, QKV_WIDTH), D_MODEL),
        "attn_q_gain": 1.0 + 0.05 * jax.random.normal(ks[6], (N_ATTN, HEAD_DIM), jnp.float32),
        "attn_k_gain": 1.0 + 0.05 * jax.random.normal(ks[7], (N_ATTN, HEAD_DIM), jnp.float32),
        "attn_w_o": nrm(ks[8], (N_ATTN, N_Q_HEADS * HEAD_DIM, D_MODEL), N_Q_HEADS * HEAD_DIM),
        "rec_w_in": nrm(ks[9], (N_REC, D_MODEL, 2 * D_RNN), D_MODEL),
        "rec_conv_w": nrm(ks[10], (N_REC, CONV_W, D_RNN), CONV_W),
        "rec_conv_b": 0.01 * jax.random.normal(ks[11], (N_REC, D_RNN), jnp.float32),
        "rec_gate_w": nrm(ks[12], (N_REC, 2, 2, N_RG_BLOCKS, RG_BW, RG_BW), RG_BW),
        "rec_gate_b": 0.01 * jax.random.normal(ks[13], (N_REC, 2, 2, D_RNN), jnp.float32),
        "rec_lambda": jnp.log(a0) - jnp.log1p(-a0),
        "rec_w_out": nrm(ks[15], (N_REC, D_RNN, D_MODEL), D_RNN),
    }

def reference(x, meta_tokens, norm_gains, ffn_w_in, ffn_w_out, attn_w_qkv, attn_q_gain,
              attn_k_gain, attn_w_o, rec_w_in, rec_conv_w, rec_conv_b, rec_gate_w,
              rec_gate_b, rec_lambda, rec_w_out):
    B, n_tok, _ = x.shape
    h = jnp.concatenate([jnp.broadcast_to(meta_tokens.astype(x.dtype)[None], (B, N_META, D_MODEL)), x], axis=1)
    cos, sin = axial_rope_tables(n_tok)
    for layer in range(DEPTH):
        g = norm_gains[layer]
        h = h + 0.5 * rms_norm(swiglu(rms_norm(h, g[0]), ffn_w_in[layer, 0], ffn_w_out[layer, 0]), g[1])
        hn = rms_norm(h, g[2])
        if layer % 2 == 0:
            j = layer // 2
            m = attention_mixer(hn, attn_w_qkv[j], attn_q_gain[j], attn_k_gain[j], attn_w_o[j], cos, sin)
        else:
            j = layer // 2
            m = recurrent_mixer(hn, rec_w_in[j], rec_conv_w[j], rec_conv_b[j], rec_gate_w[j],
                                rec_gate_b[j], rec_lambda[j], rec_w_out[j])
        h = h + rms_norm(m, g[3])
        h = h + 0.5 * rms_norm(swiglu(rms_norm(h, g[4]), ffn_w_in[layer, 1], ffn_w_out[layer, 1]), g[5])
    return h[:, N_META:]


_drawn_inputs = setup_inputs


def setup_inputs(seed=0):
    import zlib

    import numpy as np

    out = dict(_drawn_inputs(seed))
    spreads = {}
    factors = {'rec_conv_b': 4.296, 'rec_gate_b': 34.252}
    for name, (base, spread) in spreads.items():
        noise = np.random.default_rng([zlib.crc32(name.encode()), seed]).standard_normal(out[name].shape)
        drawn = base * np.exp(spread * noise) if base else spread * noise
        out[name] = __import__('jax').numpy.asarray(drawn.astype(out[name].dtype))
    for name, factor in factors.items():
        out[name] = (out[name] * factor).astype(out[name].dtype)
    return out
```

```python
from contextlib import ExitStack

import numpy as np

import concourse.bass as bass
from concourse import mybir

ALU = mybir.AluOpType
ACT = mybir.ActivationFunctionType
F32 = mybir.dt.float32
F32R = mybir.dt.float32r
AX_X = mybir.AxisListType.X

P = 128
D = 1024
KC = D // P
SEQ = 256
META = 16
L = SEQ + META
FF = 2816
FC = FF // P
HD = 64
NKV = 4
GROUP = 4
QT_N = D // P
KT_N = NKV * HD // P
QKT = KT_N + QT_N
CONVW = 4
CONVL = 2
NB = 4
GRID_W = 64
THETA = 10000.0
EPS = 1e-6
WEIGHT_SLOTS = 4
UNIT_TILES = 16
OUT_K = (6, 6, 5, 5)
TOK = [(0, P), (P, P), (2 * P, L - 2 * P)]
KTOK = [(0, 96), (96, 96), (192, 80)]

FFN_IN_UNITS = FC
FFN_OUT_UNITS = 4 * len(OUT_K)
FFN_UNITS = FFN_IN_UNITS + FFN_OUT_UNITS
U_QKV = FFN_UNITS
U_WO = U_QKV + 6
U_FFN = [0, U_WO + 4, U_WO + 4 + FFN_UNITS, 0]
U_REC = U_FFN[2] + FFN_UNITS
REC_ORDER = ["x0", "x1", "g0", "x2", "g1", "x3", "g2", "g3", "e0", "e1", "e2", "e3"]
U_ROUT = U_REC + len(REC_ORDER)
U_FFN[3] = U_ROUT + 4
UNITS = U_FFN[3] + FFN_UNITS

GAIN = lambda layer, i, c: (layer * 6 + i) * KC + c
V_CONVW, V_CONVB, V_GATEB, V_LAM, V_QG, V_KG = 0, 32, 40, 72, 88, 89
VB = 90
C_ID, C_ROT, C_BONES, C_ONES, C_COS, C_SIN = 0, P, 2 * P, 3 * P, 4 * P, 4 * P + L
C_N = 4 * P + 2 * L

NPROJ = 6
TILES_S = 9


def shape_constants():
    c = np.zeros((P, C_N), np.float32)
    c[:, C_ID:C_ID + P] = np.eye(P)
    half = HD // 2
    for m in range(P):
        if m % HD < half:
            c[m + half, C_ROT + m] = -1.0
        else:
            c[m - half, C_ROT + m] = 1.0
        b = m // HD * HD
        c[b:b + HD, C_BONES + m] = 1.0 / HD
    c[:, C_ONES:C_ONES + P] = 1.0 / D
    inv = (np.float32(1.0) / (np.float32(THETA) ** (np.arange(0, half, 2, dtype=np.float32) / np.float32(half)))).astype(np.float32)
    pos = np.arange(SEQ)
    zeros = np.zeros(META, np.float32)
    row = np.concatenate([zeros, (pos // GRID_W).astype(np.float32)])
    col = np.concatenate([zeros, (pos % GRID_W).astype(np.float32)])
    theta = np.concatenate([row[:, None] * inv, col[:, None] * inv], axis=-1).astype(np.float32)
    cos, sin = np.cos(theta).T, np.sin(theta).T
    for b in range(P // half):
        c[b * half:(b + 1) * half, C_COS:C_COS + L] = cos
        c[b * half:(b + 1) * half, C_SIN:C_SIN + L] = sin
    return c


def build(nc, x, meta, gains, ffn_in, ffn_out, w_qkv, q_gain, k_gain, w_o, rec_in, conv_w, conv_b,
          gate_w, gate_b, lam, rec_out, consts, out):
    ctx = ExitStack()
    with ctx:
        def sb(name, shape, dt=F32):
            return ctx.enter_context(nc.sbuf_tensor(name, shape, dt))

        def sem(name):
            return ctx.enter_context(nc.semaphore(name))

        h = sb("h", [P, KC, L])
        xh, xl = sb("xh", [P, KC, L], F32R), sb("xl", [P, KC, L], F32R)
        raw = sb("raw", [P, WEIGHT_SLOTS, UNIT_TILES * P])
        wh = sb("wh", [P, WEIGHT_SLOTS, UNIT_TILES * P], F32R)
        wl = sb("wl", [P, WEIGHT_SLOTS, UNIT_TILES * P], F32R)
        mg = sb("mg", [P, KC, L])
        cst = sb("cst", [P, C_N])
        vec_a = sb("vec_a", [P, 96])
        vec_h = sb("vec_h", [P, 96])
        vec_b = sb("vec_b", [P, VB])
        tmp = sb("tmp", [P, 8, L])
        pad = sb("pad", [P, 2, L + 4])
        sqb = sb("sqb", [P, 2, L])
        sqh = sb("sqh", [P, 2, L])
        acc = sb("acc", [P, L])
        hacc = sb("hacc", [P, L])
        rt = sb("rt", [P, L])
        r = sb("r", [P, L])
        small = sb("small", [P, 8, 16])
        c4 = sb("c4", [P, 2, KC])
        qg = sb("qg", [P, 2])
        rcol = sb("rcol", [P, 3])
        nmax = sb("nmax", [P, NKV * TILES_S])
        rsum = sb("rsum", [P, NKV * TILES_S])
        rinv = sb("rinv", [P, NKV * TILES_S])
        prow = sb("prow", [P, 3, L])

        with nc.sbuf_tensor("ah", [P, FC, L], F32R) as ah, nc.sbuf_tensor("al", [P, FC, L], F32R) as al:
            pass
        with nc.sbuf_tensor("tok_in", [P, 3, D], F32) as tok_in, nc.sbuf_tensor("vrow", [96, 2, P], F32) as vrow, \
                nc.sbuf_tensor("tok_out", [P, 2, D], F32) as tok_out:
            pass
        with nc.sbuf_tensor("qt", [P, QT_N, L], F32) as qt, nc.sbuf_tensor("kd", [P, NKV, L], F32) as kd, \
                nc.sbuf_tensor("vt", [P, 3, NKV * HD], F32) as vt, nc.sbuf_tensor("pt", [P, 2, 3, GROUP, L], F32) as pt:
            pass
        with nc.sbuf_tensor("xch", [P, 2, 2, L], F32R) as xch, nc.sbuf_tensor("xcl", [P, 2, 2, L], F32R) as xcl, \
                nc.sbuf_tensor("xc", [P, 2, 2, L], F32) as xc, nc.sbuf_tensor("gr", [P, 2, 2, 2, L], F32) as gr, \
                nc.sbuf_tensor("gi", [P, 2, 2, 2, L], F32) as gi, nc.sbuf_tensor("gw", [P, 2, 2, 2, L], F32) as gw, \
                nc.sbuf_tensor("gm", [P, 2, 2, 2, L], F32) as gm:
            pass
        ctx.enter_context(nc.sbuf_tensor("region", [P, 2 * FC * L], F32))

        bank = [ctx.enter_context(nc.psum_tensor(f"bank{i}", [P, 512], F32)) for i in range(8)]
        SUM_POST, SUM_PRE = bank[6], bank[7]
        QSUM, ROTB = bank[6], bank[7]

        ident = cst[:, C_ID:C_ID + P]
        rotm = cst[:, C_ROT:C_ROT + P]
        bones = cst[:, C_BONES:C_BONES + P]
        ones = cst[:, C_ONES:C_ONES + P]
        cos = cst[:, C_COS:C_COS + L]
        sin = cst[:, C_SIN:C_SIN + L]
        qp, qs, qn, qc = tmp[:, 0:2, :], tmp[:, 2:4, :], tmp[:, 4:6, :], tmp[:, 6:8, :]
        gp, sl, up, aa = qp, qs, qn, qc
        ys = tmp

        s_in = sem("inputs_landed")
        s_xin = sem("tokens_landed")
        landed = [sem(f"landed{i}") for i in range(WEIGHT_SLOTS)]
        wh_ready, w_ready, out_unit_used = sem("wh_ready"), sem("w_ready"), sem("out_unit_used")
        vecs_t, x_trans = sem("vecs_transposed"), sem("x_transposed")
        lam_a, lam_v = sem("lambda_act"), sem("lambda_dve")
        h_ready, xh_ready, x_ready = sem("h_ready"), sem("xh_ready"), sem("x_ready")
        hsq_ready, hacc_step, pre_sum, pre_root, r_ready = (sem(n) for n in ("hsq_ready", "hacc_step", "pre_sum", "pre_root", "r_ready"))
        gu_done, gate_scaled, silu_done, up_scaled, a_full, ah_ready, a_ready = (sem(n) for n in (
            "gu_done", "gate_scaled", "silu_done", "up_scaled", "a_full", "ah_ready", "a_ready"))
        proj_done, sq_ready, mg_ready, acc_step, post_sum, post_root, rt_ready, mg_scaled = (sem(n) for n in (
            "proj_done", "sq_ready", "mg_ready", "acc_step", "post_sum", "post_root", "rt_ready", "mg_scaled"))
        qk_done, q_scaled, q_squared, q_sum, q_root, q_rinv, q_normed, q_rot, q_cos, q_sin, q_final = (sem(n) for n in (
            "qk_done", "q_scaled", "q_squared", "q_sum", "q_root", "q_rinv", "q_normed", "q_rot", "q_cos", "q_sin", "q_final"))
        v_done, rcol_done, rcol_ready, v_ready, k_dup = (sem(n) for n in ("v_done", "rcol_done", "rcol_ready", "v_ready", "k_dup"))
        s_done, nmax_ready, p_exp, p_inv, p_norm, t_done, pt_main, pt_last, pv_done, oh_ready, o_ready = (sem(n) for n in (
            "s_done", "nmax_ready", "p_exp", "p_inv", "p_norm", "t_done", "pt_main", "pt_last", "pv_done", "oh_ready", "o_ready"))
        xr_done, pad_zero, xr_scaled, conv0, conv_step, xch_ready, xcl_ready = (sem(n) for n in (
            "xr_done", "pad_zero", "xr_scaled", "conv0", "conv_step", "xch_ready", "xcl_ready"))
        g_done, sig_done, tanh_done, rec_step, root_done, ix_done, b_done, scan_done, ysum_done = (sem(n) for n in (
            "g_done", "sig_done", "tanh_done", "rec_step", "root_done", "ix_done", "b_done", "scan_done", "ysum_done"))
        e_done, e_scaled, gelu_done, y_full, yh_ready, y_ready = (sem(n) for n in (
            "e_done", "e_scaled", "gelu_done", "y_full", "yh_ready", "y_ready"))
        out_t, s_out = sem("out_transposed"), sem("out_stored")
        out_copied = [sem("out_copied0"), sem("out_copied1")]
        vec_ready = sem("vec_ready")

        landed_at, count = [], [0] * WEIGHT_SLOTS
        for u in range(UNITS):
            gates = U_REC <= u < U_ROUT and REC_ORDER[u - U_REC][0] == "g"
            count[u % WEIGHT_SLOTS] += 64 if gates else 16
            landed_at.append(count[u % WEIGHT_SLOTS])

        def slot(u):
            return u % WEIGHT_SLOTS

        FFN_OF_PROJ = {0: 0, 2: 1, 3: 2, 5: 3}
        X_OF_FFN = (0, 2, 3, 5)
        PRE_GAIN = [(0, 0), (0, 2), (0, 4), (1, 0), (1, 2), (1, 4)]
        POST_GAIN = [(0, 1), (0, 3), (0, 5), (1, 1), (1, 3), (1, 5)]
        PROJ_BANKS = {n: ((4, 5), (0, 1), (0, 1), (2, 3)) if n in FFN_OF_PROJ else ((0, 1), (2, 3), (4, 5), (0, 1)) for n in range(NPROJ)}
        PROJ_T0 = [META if n >= 4 else 0 for n in range(NPROJ)]
        FFN_T0 = [0, 0, 0, META]
        ACC = 9

        def ffn_banks(m):
            return {0: (0, 1), 1: (2, 3), 2: (4, 5)}.get(m, (2, 3) if m % 2 == 0 else (0, 1))

        block = ctx.enter_context(nc.Block())

        @block.sync
        def _(sp):
            def load(u, it, kn, src):
                if u >= WEIGHT_SLOTS:
                    sp.wait_ge(w_ready, u - WEIGHT_SLOTS + 1 + WEIGHT_SLOTS * it)
                dst = raw[:, slot(u), 0:kn * 256].rearrange("p (k c) -> p k c", k=kn)
                sp.dma_start(dst, src).then_inc(landed[slot(u)], 16)

            def ffn(n):
                u0 = U_FFN[n]
                vin = ffn_in[n // 2, n % 2].rearrange("(k p) c -> p k c", p=P)
                vout = ffn_out[n // 2, n % 2].rearrange("(k p) c -> p k c", p=P)

                def pair(u, it, col):
                    load(u, it, KC, vin[:, :, bass.ds(col, 256)])
                    load(u + 1, it, KC, vin[:, :, bass.ds(col + FF, 256)])

                pair(u0, 0, 0)
                pair(u0 + 2, 0, 256)
                with sp.Fori(0, 4) as it:
                    pair(u0 + 4, it, 512 * it + 512)
                    pair(u0 + 6, it, 512 * it + 768)
                pair(u0 + 20, 0, 2560)
                with sp.Fori(0, 4) as it:
                    k0 = 0
                    for j, kn in enumerate(OUT_K):
                        load(u0 + FFN_IN_UNITS + j, it, kn, vout[:, k0:k0 + kn, bass.ds(256 * it, 256)])
                        k0 += kn

            ffn(0)
            v = w_qkv.rearrange("(k p) c -> p k c", p=P)
            for j, c0 in enumerate((1024, 1280, 0, 256, 512, 768)):
                load(U_QKV + j, 0, KC, v[:, :, c0:c0 + 256])
            v = w_o.rearrange("(k p) c -> p k c", p=P)
            for j in range(4):
                load(U_WO + j, 0, KC, v[:, :, 256 * j:256 * j + 256])
            ffn(1)
            ffn(2)
            v = rec_in.rearrange("(k p) c -> p k c", p=P)
            for j, what in enumerate(REC_ORDER):
                n, u = int(what[1]), U_REC + j
                if what[0] == "g":
                    sp.wait_ge(w_ready, u - WEIGHT_SLOTS + 1)
                    dst = raw[:, slot(u), :].rearrange("p (g k c) -> p g k c", g=4, k=2)
                    for g in range(4):
                        sp.dma_start(dst[:, g], gate_w[g // 2, g % 2, n].rearrange("(k p) c -> p k c", p=P)).then_inc(landed[slot(u)], 16)
                else:
                    c0 = (D if what[0] == "x" else 0) + 256 * n
                    load(u, 0, KC, v[:, :, c0:c0 + 256])
            v = rec_out.rearrange("(k p) c -> p k c", p=P)
            for j in range(4):
                load(U_ROUT + j, 0, KC, v[:, :, 256 * j:256 * j + 256])
            ffn(3)
            for t in range(2):
                sp.wait_ge(out_copied[t], 2)
                sp.dma_start(out[t * P:(t + 1) * P, :], tok_out[:, t, :]).then_inc(s_out, 16)
            sp.wait_ge(s_out, 32)

        @block.tensor
        def _(pe):
            def product(dst, u, tile, mh, ml, first, last):
                a = wh[:, slot(u), tile * P:(tile + 1) * P]
                b = wl[:, slot(u), tile * P:(tile + 1) * P]
                pe.matmul(dst, b, mh, start=first, stop=False)
                pe.matmul(dst, a, ml, start=False, stop=False)
                return pe.matmul(dst, a, mh, start=False, stop=last)

            def mean_of_h(n):
                pe.wait_ge(hacc_step, 8 * n + 8)
                pe.matmul(SUM_PRE[:, 0:L], ones, hacc[:, :], start=True, stop=True).then_inc(pre_sum, 1)

            def ffn(n):
                u0, f0, x0, t0, pj = U_FFN[n], n * FC, X_OF_FFN[n] * KC, FFN_T0[n], X_OF_FFN[n]

                pe.wait_ge(w_ready, u0 + 2)
                for k in range(KC):
                    pe.wait_ge(x_ready, x0 + k + 1)
                    for part in range(2):
                        for m in range(2):
                            last = product(bank[ffn_banks(m)[part]][:, t0:L], u0 + part, 2 * k + m,
                                           xh[:, k, t0:L], xl[:, k, t0:L], k == 0, k == KC - 1)
                            if k == KC - 1 and part == 1:
                                last.then_inc(gu_done, 1)
                mean_of_h(X_OF_FFN[n])

                def mtile(u, it, m, banks, f, before):
                    if m == 0:
                        pe.wait_ge(w_ready, u + 2 + WEIGHT_SLOTS * it)
                    if before is not None:
                        pe.wait_ge(up_scaled, before + 1 + WEIGHT_SLOTS * it)
                    for part in range(2):
                        for k in range(KC):
                            last = product(bank[banks[part]][:, t0:L], u + part, 2 * k + m,
                                           xh[:, k, t0:L], xl[:, k, t0:L], k == 0, k == KC - 1)
                    last.then_inc(gu_done, 1)

                def pair(p, it):
                    for j in range(2):
                        m = 2 * p + j
                        before = {2: None, 3: f0, 4: f0 + 1}.get(m, f0 + m - 2)
                        mtile(u0 + 2 * p, it, j, ffn_banks(m), f0 + m, before)

                pair(1, 0)
                pair(2, 0)
                pair(3, 0)
                with pe.Fori(0, 3) as it:
                    pair(4, it)
                    pair(5, it)
                pair(10, 0)

                v0 = u0 + FFN_IN_UNITS

                def group(g, it, banks, check):
                    k0 = 0
                    for j, kn in enumerate(OUT_K):
                        pe.wait_ge(w_ready, v0 + 4 * g + j + 1 + WEIGHT_SLOTS * it)
                        for m in range(2):
                            if check and j == 0:
                                pe.wait_ge(mg_ready, 8 * pj + 2 * g + m - 1 + 2 * it)
                            for k in range(kn):
                                if g == 0 and m == 0:
                                    pe.wait_ge(a_ready, f0 + k0 + k + 1)
                                last = product(bank[banks[m]][:, t0:L], v0 + 4 * g + j, 2 * k + m,
                                               ah[:, k0 + k, t0:L], al[:, k0 + k, t0:L],
                                               k0 + k == 0, k0 + k == FC - 1)
                            if j == len(OUT_K) - 1:
                                last.then_inc(proj_done, 1)
                            elif m == 1:
                                last.then_inc(out_unit_used, 1)
                        k0 += kn

                group(0, 0, PROJ_BANKS[pj][0], False)
                with pe.Fori(0, 2) as it:
                    group(1, it, PROJ_BANKS[pj][1], True)
                group(3, 0, PROJ_BANKS[pj][3], False)
                mean_of_projection(pj)

            def mean_of_projection(pj):
                t0 = PROJ_T0[pj]
                pe.wait_ge(acc_step, ACC * pj + ACC)
                pe.matmul(SUM_POST[:, t0:L], ones, acc[:, t0:L], start=True, stop=False)
                pe.wait_ge(sq_ready, 8 * pj + 8)
                pe.matmul(SUM_POST[:, t0:L], ones, sqb[:, 1, t0:L], start=False, stop=True).then_inc(post_sum, 1)

            def projection(pj, u0, ready, step):
                t0 = PROJ_T0[pj]
                for g in range(4):
                    pe.wait_ge(w_ready, u0 + g + 1)
                    for m in range(2):
                        if g == 3:
                            pe.wait_ge(mg_ready, 8 * pj + m + 1)
                        for k in range(KC):
                            if g == 0 and m == 0:
                                pe.wait_ge(ready, k // step + 1)
                            last = product(bank[PROJ_BANKS[pj][g][m]][:, t0:L], u0 + g, 2 * k + m,
                                           xh[:, k, t0:L], xl[:, k, t0:L], k == 0, k == KC - 1)
                        last.then_inc(proj_done, 1)
                mean_of_projection(pj)

            def attention():
                pe.wait_ge(w_ready, U_QKV + 2)
                for k in range(KC):
                    pe.wait_ge(x_ready, KC + k + 1)
                    for m in range(KT_N):
                        last = product(bank[m][:, 0:L], U_QKV, 2 * k + m, xh[:, k, :], xl[:, k, :], k == 0, k == KC - 1)
                        if k == KC - 1:
                            last.then_inc(qk_done, 1)
                    for c, (a, n) in enumerate(KTOK):
                        dst = bank[2 + c][0:n, 0:NKV * HD]
                        wv_h = wh[:, slot(U_QKV + 1), k * 256:(k + 1) * 256]
                        wv_l = wl[:, slot(U_QKV + 1), k * 256:(k + 1) * 256]
                        pe.matmul(dst, xl[:, k, a:a + n], wv_h, start=k == 0, stop=False)
                        pe.matmul(dst, xh[:, k, a:a + n], wv_l, start=False, stop=False)
                        last = pe.matmul(dst, xh[:, k, a:a + n], wv_h, start=False, stop=k == KC - 1)
                last.then_inc(v_done, 1)
                mean_of_h(1)

                def head_mean(t):
                    pe.wait_ge(q_squared, t + 1)
                    if t:
                        pe.wait_ge(q_root, t)
                    pe.matmul(QSUM[:, 0:L], bones, qs[:, t % 2, :], start=True, stop=True).then_inc(q_sum, 1)

                def rotate(t):
                    pe.wait_ge(q_normed, t + 1)
                    if t:
                        pe.wait_ge(q_sin, t)
                    else:
                        pe.wait_ge(rcol_ready, 2)
                    pe.matmul(ROTB[:, 0:L], rotm, qn[:, t % 2, :], start=True, stop=True).then_inc(q_rot, 1)

                q_bank = {2: (5, None, 0), 3: (0, q_scaled, 1), 4: (1, q_scaled, 2), 5: (2, v_ready, 1),
                          6: (3, v_ready, 2), 7: (4, v_ready, 3), 8: (5, q_scaled, 3), 9: (0, q_scaled, 4)}
                for t in range(KT_N, QKT):
                    b, freed, value = q_bank[t]
                    if t % 2 == 0:
                        pe.wait_ge(w_ready, U_QKV + 2 + (t - KT_N) // 2 + 1)
                    if freed is not None:
                        pe.wait_ge(freed, value)
                    for k in range(KC):
                        last = product(bank[b][:, 0:L], U_QKV + 2 + (t - KT_N) // 2, 2 * k + t % 2,
                                       xh[:, k, :], xl[:, k, :], k == 0, k == KC - 1)
                    last.then_inc(qk_done, 1)
                    if t == KT_N:
                        pe.wait_ge(r_ready, 2)
                        for c, (a, n) in enumerate(KTOK):
                            last = pe.matmul(ROTB[0:n, c:c + 1], r[0:1, a:a + n], cst[0:1, 0:1], start=True, stop=True)
                        last.then_inc(rcol_done, 1)
                    head_mean(t - 2)
                    if t >= 3:
                        rotate(t - 3)
                head_mean(QKT - 2)
                rotate(QKT - 3)
                head_mean(QKT - 1)
                rotate(QKT - 2)
                rotate(QKT - 1)

                def scores(a):
                    j, t = divmod(a, TILES_S)
                    if a >= 2:
                        pe.wait_ge(p_exp, a - 1)
                    if t == 0:
                        pe.wait_ge(q_final, KT_N + 2 * j + 2)
                        for g in range(GROUP):
                            o = HD * (g % 2)
                            last = pe.matmul(bank[a % 2][32 * g:32 * g + 32, 0:L], qt[o:o + HD, 2 * j + g // 2, L - 32:L],
                                             kd[o:o + HD, j, :], start=True, stop=True)
                    else:
                        g, half = divmod(t - 1, 2)
                        o = HD * (g % 2)
                        last = pe.matmul(bank[a % 2][:, 0:L], qt[o:o + HD, 2 * j + g // 2, P * half:P * half + P],
                                         kd[o:o + HD, j, :], start=True, stop=True)
                    last.then_inc(s_done, 1)

                def turn(a):
                    pe.wait_ge(p_norm, a + 1)
                    if a >= 2:
                        pe.wait_ge(pt_main, a - 1)
                        pe.wait_ge(pt_last, a - 1)
                    for c, (k0, n) in enumerate(KTOK):
                        dst = bank[2 + a % 2][0:n, c * P:(c + 1) * P] if c < 2 else bank[6 + a % 2][0:n, 0:P]
                        last = pe.transpose(dst, prow[:, a % 3, k0:k0 + n], ident)
                    last.then_inc(t_done, 1)

                def weigh(j, g):
                    a, pair = j * TILES_S + 2 * g + 2, 2 * j + g // 2
                    pe.wait_ge(pt_main, a + 1)
                    pe.wait_ge(pt_last, a + 1)
                    if pair >= 2 and g % 2 == 0:
                        pe.wait_ge(o_ready, pair - 1)
                    o = HD * (g % 2)
                    for c, (_, n) in enumerate(KTOK):
                        last = pe.matmul(bank[4 + pair % 2][o:o + HD, 0:L], vt[0:n, c, HD * j:HD * j + HD],
                                         pt[0:n, j % 2, c, g, :], start=c == 0, stop=c == 2)
                    if g % 2:
                        last.then_inc(pv_done, 1)

                pe.wait_ge(k_dup, 32)
                pe.wait_ge(q_sin, QKT)
                tiles = NKV * TILES_S
                scores(0)
                scores(1)
                for a in range(tiles):
                    turn(a)
                    if a + 2 < tiles:
                        scores(a + 2)
                    j, t = divmod(a - 1, TILES_S)
                    if a >= 1 and t >= 2 and t % 2 == 0:
                        weigh(j, (t - 2) // 2)
                weigh(NKV - 1, GROUP - 1)

            def recurrent():
                t0 = PROJ_T0[4]
                for j, what in enumerate(REC_ORDER):
                    n, u = int(what[1]), U_REC + j
                    pe.wait_ge(w_ready, u + 1)
                    if what[0] == "g":
                        pe.wait_ge(xcl_ready, 2 * n + 2)
                        for g in range(4):
                            for m in range(2):
                                o = 8 * n + 2 * g + m
                                if o >= 4:
                                    pe.wait_ge(sig_done, o - 3)
                                for k in range(2):
                                    last = product(bank[4 + o % 4][:, 0:L], u, (g * 2 + k) * 2 + m,
                                                   xch[:, n % 2, k, :], xcl[:, n % 2, k, :], k == 0, k == 1)
                                last.then_inc(g_done, 1)
                    elif what == "x0":
                        for k in range(KC):
                            pe.wait_ge(x_ready, 4 * KC + k + 1)
                            for m in range(2):
                                last = product(bank[m][:, 0:L], u, 2 * k + m, xh[:, k, :], xl[:, k, :], k == 0, k == KC - 1)
                                if k == KC - 1:
                                    last.then_inc(xr_done, 1)
                        mean_of_h(4)
                    else:
                        x_part = what[0] == "x"
                        a = 0 if x_part else t0
                        for m in range(2):
                            if n:
                                pe.wait_ge(xr_scaled if x_part else e_scaled, 2 * n + m - 1)
                            for k in range(KC):
                                last = product(bank[(0 if x_part else 2) + m][:, a:L], u, 2 * k + m,
                                               xh[:, k, a:L], xl[:, k, a:L], k == 0, k == KC - 1)
                            last.then_inc(xr_done if x_part else e_done, 1)

            pe.wait_ge(s_in, 16 * 8)
            pe.transpose(bank[4][:, 0:96], vrow[:, 0, :], ident[0:96, 0:96])
            pe.transpose(bank[4][:, 96:96 + VB], vrow[0:VB, 1, :], ident[0:VB, 0:VB]).then_inc(vecs_t, 1)
            pe.wait_ge(s_xin, 64)
            for c in range(KC):
                if c >= 4:
                    pe.wait_ge(h_ready, c - 3)
                elif c == 0:
                    pe.wait_ge(vec_ready, 3)
                for t, (a, n) in enumerate(TOK):
                    last = pe.transpose(bank[4 + c % 4][:, a:a + n], tok_in[0:n, t, c * P:(c + 1) * P], ident[0:n, 0:n])
                last.then_inc(x_trans, 1)
            ffn(0)
            attention()
            projection(1, U_WO, o_ready, 1)
            ffn(1)
            ffn(2)
            recurrent()
            projection(4, U_ROUT, y_ready, 2)
            ffn(3)
            for c in range(KC):
                pe.wait_ge(h_ready, 6 * KC + c + 1)
                for t in range(2):
                    last = pe.transpose(bank[2 * t + c // 4][:, (c % 4) * P:(c % 4 + 1) * P],
                                        h[:, c, META + t * P:META + (t + 1) * P], ident)
                    if c % 4 == 3:
                        last.then_inc(out_t, 1)

        @block.scalar
        def _(act):
            def high(u, it, kn=KC, freed=None):
                act.wait_ge(landed[slot(u)], landed_at[u] + 16 * it)
                if freed is not None:
                    act.wait_ge(*freed)
                act.activation(wh[:, slot(u), 0:kn * 256], raw[:, slot(u), 0:kn * 256], ACT.Copy).then_inc(wh_ready, 1)

            def make_x(n):
                t0 = PROJ_T0[n - 1] if n else 0
                for c in range(KC):
                    act.wait_ge(h_ready, 8 * n + c + 1)
                    g = GAIN(*PRE_GAIN[n], c)
                    act.activation(xh[:, c, t0:L], h[:, c, t0:L], ACT.Copy, scale=vec_a[:, g:g + 1]).then_inc(xh_ready, 1)
                    if 8 * n + c >= 2:
                        act.wait_ge(hacc_step, 8 * n + c - 1)
                    act.activation(sqh[:, c % 2, t0:L], h[:, c, t0:L], ACT.Square).then_inc(hsq_ready, 1)

            def root_of_h(n):
                act.wait_ge(pre_sum, n + 1)
                act.activation(r[:, :], SUM_PRE[:, 0:L], ACT.Sqrt, bias=EPS).then_inc(pre_root, 1)

            def square_tile(pj, m, b, it=0):
                t0 = PROJ_T0[pj]
                act.wait_ge(proj_done, 8 * pj + m + 1 + 2 * it)
                act.wait_ge(acc_step, ACC * pj + m + 1 + 2 * it)
                act.activation(sqb[:, m % 2, t0:L], bank[b][:, t0:L], ACT.Square).then_inc(sq_ready, 1)

            def root_of_projection(pj):
                t0 = PROJ_T0[pj]
                act.wait_ge(post_sum, pj + 1)
                act.activation(rt[:, t0:L], SUM_POST[:, t0:L], ACT.Sqrt, bias=EPS).then_inc(post_root, 1)

            def ffn(n, after):
                u0, f0, t0, pj = U_FFN[n], n * FC, FFN_T0[n], X_OF_FFN[n]
                root_of_h(X_OF_FFN[n])

                def tile(m, it=0):
                    b = m % 2
                    act.wait_ge(gate_scaled, f0 + m + 1 + 4 * it)
                    if f0 + m >= 2:
                        act.wait_ge(a_full, f0 + m - 1 + 4 * it)
                    act.activation(sl[:, b, t0:L], gp[:, b, t0:L], ACT.Silu).then_inc(silu_done, 1)
                    act.wait_ge(a_full, f0 + m + 1 + 4 * it)
                    act.activation(ah[:, m, t0:L] if isinstance(it, int) else
                                   ah[:, bass.ds(4 * it + m, 1), t0:L].rearrange("p a l -> p (a l)"),
                                   aa[:, b, t0:L], ACT.Copy).then_inc(ah_ready, 1)

                def pair(p, it=0):
                    tile(2 * p, it)
                    tile(2 * p + 1, it)
                    for j in range(2):
                        out_unit = 2 * p + j + 4 - FFN_IN_UNITS
                        high(u0 + 2 * p + j + 4, it, OUT_K[out_unit] if out_unit >= 0 else KC)

                pair(0)
                pair(1)
                with act.Fori(0, 3) as it:
                    pair(2, it)
                    pair(3, it)
                pair(8)
                pair(9)
                pair(10)

                def group(g, it=0):
                    for j in range(3):
                        used = 12 * n + 3 * g + j + 1 + 3 * it
                        next_unit(g, j, it, (out_unit_used, used))
                    square_tile(pj, 2 * g, PROJ_BANKS[pj][g][0], it)
                    square_tile(pj, 2 * g + 1, PROJ_BANKS[pj][g][1], it)
                    next_unit(g, 3, it, None)

                def next_unit(g, j, it, freed):
                    if g < 3:
                        high(u0 + FFN_IN_UNITS + 4 * g + j + 4, it, OUT_K[j], freed)
                    elif after is not None:
                        high(u0 + FFN_UNITS + j, 0, KC, freed)

                group(0)
                with act.Fori(0, 2) as it:
                    group(1, it)
                group(3)
                root_of_projection(pj)

            def projection(pj, u0):
                for g in range(4):
                    square_tile(pj, 2 * g, PROJ_BANKS[pj][g][0])
                    square_tile(pj, 2 * g + 1, PROJ_BANKS[pj][g][1])
                    high(u0 + g + 4, 0)
                root_of_projection(pj)

            def attention():
                root_of_h(1)

                def squared(t):
                    act.wait_ge(q_scaled, t + 1)
                    if t >= 2:
                        act.wait_ge(q_sum, t - 1)
                    act.activation(qs[:, t % 2, :], qp[:, t % 2, :], ACT.Square).then_inc(q_squared, 1)

                def root(t):
                    act.wait_ge(q_sum, t + 1)
                    if t >= 2:
                        act.wait_ge(q_normed, t - 1)
                    act.activation(sqb[:, t % 2, :], QSUM[:, 0:L], ACT.Sqrt, bias=EPS).then_inc(q_root, 1)

                squared(0)
                squared(1)
                act.wait_ge(v_done, 1)
                high(U_QKV + 4, 0)
                high(U_QKV + 5, 0)
                for t in range(KT_N, QKT):
                    root(t - 2)
                    squared(t)
                    if t % 2:
                        high(U_QKV + 2 + (t - KT_N) // 2 + 4, 0)
                root(QKT - 2)
                root(QKT - 1)

                def exponent(a):
                    act.wait_ge(nmax_ready, a + 1)
                    if a >= 3:
                        act.wait_ge(t_done, a - 2)
                    act.activation(prow[:, a % 3, :], bank[a % 2][:, 0:L], ACT.Exp, bias=nmax[:, a:a + 1],
                                   accum_out=rsum[:, a:a + 1]).then_inc(p_exp, 1)

                def place(a):
                    j, t = divmod(a, TILES_S)
                    act.wait_ge(t_done, a + 1)
                    if t == 0 and j >= 2:
                        act.wait_ge(pv_done, 2 * j - 2)
                    src = bank[2 + a % 2][0:96, 0:2 * P].rearrange("p (c q) -> p c q", c=2)
                    if t == 0:
                        src = bank[2 + a % 2][0:96, 0:2 * P].rearrange("p (c g q) -> p c g q", c=2, g=GROUP)[:, :, :, 16:32]
                        act.activation(pt[0:96, j % 2, 0:2, :, 2 * P:L], src, ACT.Copy).then_inc(pt_main, 1)
                    else:
                        g, half = divmod(t - 1, 2)
                        act.activation(pt[0:96, j % 2, 0:2, g, P * half:P * half + P], src, ACT.Copy).then_inc(pt_main, 1)

                def out_high(pair):
                    act.wait_ge(pv_done, pair + 1)
                    act.activation(xh[:, pair, :], bank[4 + pair % 2][:, 0:L], ACT.Copy).then_inc(oh_ready, 1)

                tiles = NKV * TILES_S
                exponent(0)
                for a in range(tiles):
                    if a + 1 < tiles:
                        exponent(a + 1)
                    place(a)
                    j, t = divmod(a - 2, TILES_S)
                    if a >= 2 and t in (4, 8):
                        out_high(2 * j + (t == 8))
                out_high(2 * NKV - 1)

            def recurrent():
                root_of_h(4)
                for j, what in enumerate(REC_ORDER):
                    n, u = int(what[1]), U_REC + j
                    b = n % 2
                    if what[0] == "x":
                        for i in range(2):
                            m = 2 * n + i
                            act.wait_ge(xr_scaled, m + 1)
                            if n >= 2:
                                act.wait_ge(ix_done, 2 * n - 2)
                            act.activation(xc[:, b, i, :], pad[:, i, 0:L], ACT.Identity, scale=vec_b[:, V_CONVW + m:V_CONVW + m + 1],
                                           bias=vec_b[:, V_CONVB + m:V_CONVB + m + 1]).then_inc(conv0, 1)
                            act.wait_ge(conv_step, 3 * m + 3)
                            if n >= 2:
                                act.wait_ge(g_done, 8 * n - 8)
                            act.activation(xch[:, b, i, :], xc[:, b, i, :], ACT.Copy).then_inc(xch_ready, 1)
                        high(u + 4, 0)
                    elif what[0] == "g":
                        for g in range(4):
                            for i in range(2):
                                o = 8 * n + 2 * g + i
                                act.wait_ge(g_done, o + 1)
                                if n >= 2 and o % 8 == 0:
                                    act.wait_ge(scan_done, 4 * n - 4)
                                dst = (gr, gi)[g % 2][:, b, g // 2, i, :]
                                v = V_GATEB + g * KC + 2 * n + i
                                act.activation(dst, bank[4 + o % 4][:, 0:L], ACT.Sigmoid, bias=vec_b[:, v:v + 1]).then_inc(sig_done, 1)
                        act.wait_ge(sig_done, 8 * n + 8)
                        for d in range(2):
                            for i in range(2):
                                act.activation(gr[:, b, d, i, :], gr[:, b, d, i, :], ACT.Tanh,
                                               scale=c4[:, d, 2 * n + i:2 * n + i + 1]).then_inc(tanh_done, 1)
                        high(u + 4, 0)
                        act.wait_ge(rec_step, 5 * n + 5)
                        act.activation(gw[:, b], gw[:, b], ACT.Sqrt, scale=-1.0).then_inc(root_done, 1)
                    else:
                        act.wait_ge(e_scaled, 2 * n + 2)
                        v = mg[:, 2 * n:2 * n + 2, PROJ_T0[4]:L]
                        act.activation(v, v, ACT.Gelu_apprx_tanh).then_inc(gelu_done, 1)
                        high(u + 4, 0)
                act.wait_ge(e_done, KC)
                for n in range(NB):
                    act.wait_ge(y_full, n + 1)
                    act.activation(xh[:, 2 * n:2 * n + 2, PROJ_T0[4]:L], ys[:, 2 * n:2 * n + 2, PROJ_T0[4]:L], ACT.Copy).then_inc(yh_ready, 1)

            act.dma_start(cst[:, :], consts).then_inc(s_in, 16)
            act.dma_start(vrow[:, 0, :], gains.rearrange("l i (c p) -> (l i c) p", p=P)).then_inc(s_in, 16)
            act.dma_start(tok_in[0:META, 0, :], meta).then_inc(s_xin, 16)
            act.dma_start(tok_in[META:P, 0, :], x[0:P - META, :]).then_inc(s_xin, 16)
            act.dma_start(tok_in[:, 1, :], x[P - META:2 * P - META, :]).then_inc(s_xin, 16)
            act.dma_start(tok_in[0:L - 2 * P, 2, :], x[2 * P - META:SEQ, :]).then_inc(s_xin, 16)
            act.dma_start(vrow[V_CONVW:V_CONVB, 1, :], conv_w.rearrange("j (c p) -> (j c) p", p=P)).then_inc(s_in, 16)
            act.dma_start(vrow[V_CONVB:V_GATEB, 1, :], conv_b.rearrange("(c p) -> c p", p=P)).then_inc(s_in, 16)
            act.dma_start(vrow[V_GATEB:V_LAM, 1, :], gate_b.rearrange("d g (c p) -> (d g c) p", p=P)).then_inc(s_in, 16)
            act.dma_start(vrow[V_LAM:V_QG, 1, :], lam.rearrange("d (c p) -> (d c) p", p=P)).then_inc(s_in, 16)
            act.dma_start(vrow[V_QG:V_QG + 1, 1, :].rearrange("a (n p) -> a n p", n=2), q_gain.rearrange("(a b p) -> a b p", a=1, b=1).broadcast_to([1, 2, HD])).then_inc(s_in, 16)
            act.dma_start(vrow[V_KG:V_KG + 1, 1, :].rearrange("a (n p) -> a n p", n=2), k_gain.rearrange("(a b p) -> a b p", a=1, b=1).broadcast_to([1, 2, HD])).then_inc(s_in, 16)
            act.wait_ge(vec_ready, 3)
            act.activation(small[:, 0, :], vec_b[:, V_LAM:V_QG], ACT.Abs).then_inc(lam_a, 1)
            act.wait_ge(lam_a, 1)
            act.activation(small[:, 1, :], small[:, 0, :], ACT.Exp, scale=-1.0).then_inc(lam_a, 1)
            high(0, 0)
            high(1, 0)
            make_x(0)
            high(2, 0)
            high(3, 0)
            ffn(0, True)
            make_x(1)
            attention()
            projection(1, U_WO)
            make_x(2)
            ffn(1, True)
            make_x(3)
            ffn(2, True)
            make_x(4)
            recurrent()
            projection(4, U_ROUT)
            make_x(5)
            ffn(3, None)
            for i in range(2):
                act.wait_ge(out_t, 2 * i + 2)
                act.activation(tok_out[:, 1, 512 * i:512 * i + 512], bank[2 + i][:, :], ACT.Copy).then_inc(out_copied[1], 1)

        @block.vector
        def _(dve):
            def low(u, it, kn=KC):
                dve.wait_ge(wh_ready, u + 1 + WEIGHT_SLOTS * it)
                w = raw[:, slot(u), 0:kn * 256]
                dve.tensor_tensor(wl[:, slot(u), 0:kn * 256], w, wh[:, slot(u), 0:kn * 256].bitcast(F32), ALU.subtract).then_inc(w_ready, 1)

            def low_x(n, c):
                t0 = PROJ_T0[n - 1] if n else 0
                g = GAIN(*PRE_GAIN[n], c)
                dve.wait_ge(xh_ready, 8 * n + c + 1)
                dve.scalar_tensor_tensor(xl[:, c, t0:L], h[:, c, t0:L], vec_a[:, g:g + 1], xh[:, c, t0:L].bitcast(F32),
                                         ALU.mult, ALU.subtract).then_inc(x_ready, 1)

            def r_of_h(n):
                dve.wait_ge(pre_root, n + 1)
                dve.reciprocal(r[:, :], r[:, :]).then_inc(r_ready, 1)
                dve.wait_ge(r_ready, n + 1)

            def gain_tile(pj, m, b, it=0):
                t0 = PROJ_T0[pj]
                gains_of = vec_h if pj in FFN_OF_PROJ else vec_a
                g = GAIN(*POST_GAIN[pj], 0) + m
                dve.wait_ge(sq_ready, 8 * pj + m + 1 + 2 * it)
                if isinstance(it, int):
                    dve.tensor_scalar(mg[:, m, t0:L], bank[b][:, t0:L], gains_of[:, g:g + 1], None, ALU.mult).then_inc(mg_ready, 1)
                else:
                    dve.tensor_scalar(mg[:, bass.ds(2 * it + m, 1), t0:L].rearrange("p a l -> p (a l)"), bank[b][:, t0:L],
                                      gains_of[:, bass.ds(2 * it + g, 1)], None, ALU.mult).then_inc(mg_ready, 1)
                if m < KC - 1:
                    dve.wait_ge(acc_step, ACC * pj + m + 2 + 2 * it)
                    dve.tensor_tensor(acc[:, t0:L], acc[:, t0:L], sqb[:, m % 2, t0:L], ALU.add).then_inc(acc_step, 1)

            def residual(pj):
                n, t0 = pj + 1, PROJ_T0[pj]
                dve.wait_ge(post_root, pj + 1)
                dve.reciprocal(rt[:, t0:L], rt[:, t0:L]).then_inc(rt_ready, 1)
                dve.wait_ge(rt_ready, pj + 1)
                dve.wait_ge(mg_ready, 8 * pj + 8)
                for c in range(KC):
                    dve.tensor_tensor(mg[:, c, t0:L], mg[:, c, t0:L], rt[:, t0:L], ALU.mult).then_inc(mg_scaled, 1)
                    if c >= 1 and n < NPROJ:
                        low_x(n, c - 1)
                    dve.wait_ge(mg_scaled, 8 * pj + c + 1)
                    dve.tensor_tensor(h[:, c, t0:L], h[:, c, t0:L], mg[:, c, t0:L], ALU.add).then_inc(h_ready, 1)
                if n < NPROJ:
                    low_x(n, KC - 1)
                    dve.memset(acc[:, :], 0.0).then_inc(acc_step, 2)

            def ffn(n, after):
                u0, f0, t0, pj = U_FFN[n], n * FC, FFN_T0[n], X_OF_FFN[n]
                r_of_h(X_OF_FFN[n])

                def tile(m, it=0, banks=None):
                    b = m % 2
                    dve.wait_ge(gu_done, f0 + m + 1 + 4 * it)
                    if f0 + m >= 2:
                        dve.wait_ge(silu_done, f0 + m - 1 + 4 * it)
                    dve.tensor_tensor(gp[:, b, t0:L], bank[banks[0]][:, t0:L], r[:, t0:L], ALU.mult).then_inc(gate_scaled, 1)
                    dve.tensor_tensor(up[:, b, t0:L], bank[banks[1]][:, t0:L], r[:, t0:L], ALU.mult).then_inc(up_scaled, 1)
                    dve.wait_ge(silu_done, f0 + m + 1 + 4 * it)
                    dve.wait_ge(up_scaled, f0 + m + 1 + 4 * it)
                    if f0 + m >= 2:
                        dve.wait_ge(ah_ready, f0 + m - 1 + 4 * it)
                    dve.tensor_tensor(aa[:, b, t0:L], sl[:, b, t0:L], up[:, b, t0:L], ALU.mult).then_inc(a_full, 1)

                def tile_low(m, it=0):
                    b = m % 2
                    dve.wait_ge(ah_ready, f0 + m + 1 + 4 * it)
                    if isinstance(it, int):
                        d, s = al[:, m, t0:L], ah[:, m, t0:L].bitcast(F32)
                    else:
                        d = al[:, bass.ds(4 * it + m, 1), t0:L].rearrange("p a l -> p (a l)")
                        s = ah[:, bass.ds(4 * it + m, 1), t0:L].bitcast(F32).rearrange("p a l -> p (a l)")
                    dve.tensor_tensor(d, aa[:, b, t0:L], s, ALU.subtract).then_inc(a_ready, 1)

                def pair(p, it=0):
                    for j in range(2):
                        tile(2 * p + j, it, ffn_banks(2 * p + j))
                        tile_low(2 * p + j, it)
                    for j in range(2):
                        out_unit = 2 * p + j + 4 - FFN_IN_UNITS
                        low(u0 + 2 * p + j + 4, it, OUT_K[out_unit] if out_unit >= 0 else KC)

                pair(0)
                pair(1)
                with dve.Fori(0, 3) as it:
                    pair(2, it)
                    pair(3, it)
                pair(8)
                pair(9)
                pair(10)

                def next_unit(g, j, it):
                    if g < 3:
                        low(u0 + FFN_IN_UNITS + 4 * g + j + 4, it, OUT_K[j])
                    elif after is not None:
                        low(u0 + FFN_UNITS + j, 0)

                def group(g, it=0):
                    for j in range(3):
                        next_unit(g, j, it)
                    gain_tile(pj, 2 * g, PROJ_BANKS[pj][g][0], it)
                    gain_tile(pj, 2 * g + 1, PROJ_BANKS[pj][g][1], it)
                    next_unit(g, 3, it)

                group(0)
                with dve.Fori(0, 2) as it:
                    group(1, it)
                group(3)
                residual(pj)

            def projection(pj, u0):
                for g in range(4):
                    gain_tile(pj, 2 * g, PROJ_BANKS[pj][g][0])
                    gain_tile(pj, 2 * g + 1, PROJ_BANKS[pj][g][1])
                    low(u0 + g + 4, 0)
                residual(pj)

            def attention():
                r_of_h(1)
                q_bank = (0, 1, 5, 0, 1, 2, 3, 4, 5, 0)

                def scaled(t):
                    dve.wait_ge(qk_done, t + 1)
                    if t >= 2:
                        dve.wait_ge(q_normed, t - 1)
                    dve.tensor_tensor(qp[:, t % 2, :], bank[q_bank[t]][:, 0:L], r[:, :], ALU.mult).then_inc(q_scaled, 1)

                def normed(t):
                    g = 1 if t < KT_N else 0
                    dve.wait_ge(q_root, t + 1)
                    dve.reciprocal(sqb[:, t % 2, :], sqb[:, t % 2, :]).then_inc(q_rinv, 1)
                    dve.wait_ge(q_rinv, t + 1)
                    if t >= 2:
                        dve.wait_ge(q_rot, t - 1)
                        dve.wait_ge(q_cos, t - 1)
                    dve.scalar_tensor_tensor(qn[:, t % 2, :], qp[:, t % 2, :], qg[:, g:g + 1], sqb[:, t % 2, :],
                                             ALU.mult, ALU.mult).then_inc(q_normed, 1)

                def times_sin(t):
                    dve.wait_ge(q_rot, t + 1)
                    if t >= 2:
                        dve.wait_ge(q_final, t - 1)
                    dve.tensor_tensor(pad[:, t % 2, 0:L], ROTB[:, 0:L], sin, ALU.mult).then_inc(q_sin, 1)

                scaled(0)
                scaled(1)
                dve.wait_ge(v_done, 1)
                dve.wait_ge(rcol_done, 1)
                dve.tensor_copy(rcol[0:96, 0:2], ROTB[0:96, 0:2]).then_inc(rcol_ready, 1)
                dve.tensor_copy(rcol[0:80, 2:3], ROTB[0:80, 2:3]).then_inc(rcol_ready, 1)
                dve.wait_ge(rcol_ready, 2)
                for c, (_, n) in enumerate(KTOK):
                    dve.tensor_scalar(vt[0:n, c, :], bank[2 + c][0:n, 0:NKV * HD], rcol[0:n, c:c + 1], None, ALU.mult).then_inc(v_ready, 1)
                low(U_QKV + 4, 0)
                low(U_QKV + 5, 0)
                for t in range(KT_N, QKT):
                    normed(t - 2)
                    scaled(t)
                    if t >= 3:
                        times_sin(t - 3)
                    if t % 2:
                        low(U_QKV + 2 + (t - KT_N) // 2 + 4, 0)
                normed(QKT - 2)
                times_sin(QKT - 3)
                normed(QKT - 1)
                times_sin(QKT - 2)
                times_sin(QKT - 1)

                def maximum(a):
                    dve.wait_ge(s_done, a + 1)
                    dve.tensor_reduce(nmax[:, a:a + 1], bank[a % 2][:, 0:L], AX_X, ALU.max, negate=True).then_inc(nmax_ready, 1)

                def normalise(a):
                    dve.wait_ge(p_exp, a + 1)
                    dve.reciprocal(rinv[:, a:a + 1], rsum[:, a:a + 1]).then_inc(p_inv, 1)
                    dve.wait_ge(p_inv, a + 1)
                    dve.tensor_scalar(prow[:, a % 3, :], prow[:, a % 3, :], rinv[:, a:a + 1], None, ALU.mult).then_inc(p_norm, 1)

                def place(a):
                    j, t = divmod(a, TILES_S)
                    dve.wait_ge(t_done, a + 1)
                    if t == 0 and j >= 2:
                        dve.wait_ge(pv_done, 2 * j - 2)
                    n = KTOK[2][1]
                    src = bank[6 + a % 2][0:n, 0:P]
                    if t == 0:
                        dve.tensor_copy(pt[0:n, j % 2, 2, :, 2 * P:L], src.rearrange("p (g q) -> p g q", g=GROUP)[:, :, 16:32]).then_inc(pt_last, 1)
                    else:
                        g, half = divmod(t - 1, 2)
                        dve.tensor_copy(pt[0:n, j % 2, 2, g, P * half:P * half + P], src).then_inc(pt_last, 1)

                def out_low(pair):
                    dve.wait_ge(oh_ready, pair + 1)
                    dve.tensor_tensor(xl[:, pair, :], bank[4 + pair % 2][:, 0:L], xh[:, pair, :].bitcast(F32), ALU.subtract).then_inc(o_ready, 1)

                tiles = NKV * TILES_S
                maximum(0)
                for a in range(tiles):
                    if a + 1 < tiles:
                        maximum(a + 1)
                    normalise(a)
                    if a >= 1:
                        place(a - 1)
                    j, t = divmod(a - 3, TILES_S)
                    if a >= 3 and t in (4, 8):
                        out_low(2 * j + (t == 8))
                place(tiles - 1)
                out_low(2 * NKV - 1)

            def recurrent():
                r_of_h(4)
                for j, what in enumerate(REC_ORDER):
                    n, u = int(what[1]), U_REC + j
                    b = n % 2
                    if what[0] == "x":
                        for i in range(2):
                            m = 2 * n + i
                            dve.wait_ge(xr_done, m + 1)
                            if n:
                                dve.wait_ge(conv_step, 3 * m - 3)
                                dve.wait_ge(conv0, m - 1)
                            dve.tensor_tensor(pad[:, i, CONVL:CONVL + L], bank[i][:, 0:L], r[:, :], ALU.mult).then_inc(xr_scaled, 1)
                        for i in range(2):
                            m = 2 * n + i
                            dve.wait_ge(conv0, m + 1)
                            for tap in range(1, CONVW):
                                if tap > 1:
                                    dve.wait_ge(conv_step, 3 * m + tap - 1)
                                v = V_CONVW + tap * KC + m
                                dve.scalar_tensor_tensor(xc[:, b, i, :], pad[:, i, tap:tap + L], vec_b[:, v:v + 1], xc[:, b, i, :],
                                                         ALU.mult, ALU.add).then_inc(conv_step, 1)
                        low(u + 4, 0)
                    elif what[0] == "g":
                        dve.wait_ge(tanh_done, 4 * n + 4)
                        if n >= 2:
                            dve.wait_ge(ysum_done, n - 1)
                        dve.tensor_scalar(gw[:, b], gr[:, b], 1.0, None, ALU.add).then_inc(rec_step, 1)
                        dve.wait_ge(rec_step, 5 * n + 1)
                        dve.reciprocal(gw[:, b], gw[:, b]).then_inc(rec_step, 1)
                        dve.wait_ge(rec_step, 5 * n + 2)
                        flat = "p d m l -> p (d m l)"
                        fr, fw, fm, fi = (v[:, b].rearrange(flat) for v in (gr, gw, gm, gi))
                        dve.scalar_tensor_tensor(fm, fr, 2.0, fw, ALU.mult, ALU.mult).then_inc(rec_step, 1)
                        dve.wait_ge(rec_step, 5 * n + 3)
                        dve.tensor_scalar(fr, fm, -1.0, 1.0, ALU.mult, ALU.add).then_inc(rec_step, 1)
                        dve.scalar_tensor_tensor(fw, fm, 2.0, fm, ALU.subtract, ALU.mult).then_inc(rec_step, 1)
                        low(u + 4, 0)
                        dve.wait_ge(root_done, n + 1)
                        dve.wait_ge(ix_done, 2 * n + 2)
                        dve.tensor_tensor(fi, fi, fw, ALU.mult).then_inc(b_done, 1)
                        dve.wait_ge(b_done, n + 1)
                        for d in range(2):
                            for i in range(2):
                                a_, b_, o_ = gr[:, b, d, i, :], gi[:, b, d, i, :], gm[:, b, d, i, :]
                                if d:
                                    a_, b_, o_ = a_[:, ::-1], b_[:, ::-1], o_[:, ::-1]
                                dve.tensor_tensor_scan(o_, a_, b_, 0.0, ALU.mult, ALU.add).then_inc(scan_done, 1)
                    else:
                        for i in range(2):
                            m = 2 * n + i
                            dve.wait_ge(e_done, m + 1)
                            dve.tensor_tensor(mg[:, m, PROJ_T0[4]:L], bank[2 + i][:, PROJ_T0[4]:L], r[:, PROJ_T0[4]:L], ALU.mult).then_inc(e_scaled, 1)
                        low(u + 4, 0)
                for n in range(NB):
                    dve.wait_ge(yh_ready, n + 1)
                    s = slice(2 * n, 2 * n + 2)
                    t = slice(PROJ_T0[4], L)
                    dve.tensor_tensor(xl[:, s, t], ys[:, s, t], xh[:, s, t].bitcast(F32), ALU.subtract).then_inc(y_ready, 1)

            dve.memset(acc[:, :], 0.0).then_inc(acc_step, 2)
            dve.memset(pad[:, :, :], 0.0).then_inc(pad_zero, 1)
            dve.wait_ge(vecs_t, 1)
            dve.tensor_copy(vec_a[:, :], bank[4][:, 0:96]).then_inc(vec_ready, 1)
            dve.tensor_scalar(vec_h[:, :], bank[4][:, 0:96], 0.5, None, ALU.mult).then_inc(vec_ready, 1)
            dve.tensor_copy(vec_b[:, :], bank[4][:, 96:96 + VB]).then_inc(vec_ready, 1)
            dve.wait_ge(vec_ready, 3)
            low(0, 0)
            low(1, 0)
            for c in range(KC):
                dve.wait_ge(x_trans, c + 1)
                dve.tensor_copy(h[:, c, :], bank[4 + c % 4][:, 0:L]).then_inc(h_ready, 1)
                if c >= 1:
                    low_x(0, c - 1)
            low_x(0, KC - 1)
            low(2, 0)
            low(3, 0)

            steps = [0]

            def link(ins):
                steps[0] += 1
                ins.then_inc(lam_v, 1)
                dve.wait_ge(lam_v, steps[0])

            e, w, z, zz, p, m0 = (small[:, i, :] for i in (1, 2, 3, 4, 5, 6))
            dve.wait_ge(lam_a, 2)
            link(dve.tensor_scalar(w, e, 2.0, None, ALU.add))
            link(dve.reciprocal(w, w))
            link(dve.tensor_tensor(z, e, w, ALU.mult))
            link(dve.tensor_tensor(zz, z, z, ALU.mult))
            link(dve.tensor_scalar(p, zz, 1.0 / 15, None, ALU.mult))
            for k in (13, 11, 9, 7, 5, 3):
                link(dve.scalar_tensor_tensor(p, p, 1.0 / k, zz, ALU.add, ALU.mult))
            link(dve.scalar_tensor_tensor(p, p, 1.0, z, ALU.add, ALU.mult))
            link(dve.tensor_scalar(m0, vec_b[:, V_LAM:V_QG], -1.0, 0.0, ALU.mult, ALU.max))
            link(dve.scalar_tensor_tensor(m0, p, 2.0, m0, ALU.mult, ALU.add))
            link(dve.tensor_scalar(c4[:, :, :].rearrange("p d c -> p (d c)"), m0, 4.0, None, ALU.mult))
            link(dve.tensor_scalar(qg[:, 0:1], vec_b[:, V_QG:V_QG + 1], HD ** -0.5, None, ALU.mult))
            link(dve.tensor_copy(qg[:, 1:2], vec_b[:, V_KG:V_KG + 1]))

            ffn(0, True)
            attention()
            projection(1, U_WO)
            ffn(1, True)
            ffn(2, True)
            dve.memset(pad[:, :, 0:CONVL], 0.0).then_inc(pad_zero, 1)
            dve.memset(pad[:, :, CONVL + L:], 0.0).then_inc(pad_zero, 1)
            recurrent()
            projection(4, U_ROUT)
            ffn(3, None)
            for i in range(2):
                dve.wait_ge(out_t, 2 * i + 1)
                dve.tensor_copy(tok_out[:, 0, 512 * i:512 * i + 512], bank[i][:, :]).then_inc(out_copied[0], 1)

        @block.gpsimd
        def _(pool):
            def sum_squares(n):
                t0 = PROJ_T0[n - 1] if n else 0
                if n:
                    pool.wait_ge(pre_sum, n)
                for c in range(KC):
                    pool.wait_ge(hsq_ready, 8 * n + c + 1)
                    if c == 0:
                        pool.tensor_copy(hacc[:, t0:L], sqh[:, 0, t0:L]).then_inc(hacc_step, 1)
                    else:
                        pool.wait_ge(hacc_step, 8 * n + c)
                        pool.tensor_tensor(hacc[:, t0:L], hacc[:, t0:L], sqh[:, c % 2, t0:L], ALU.add).then_inc(hacc_step, 1)

            def rotary():
                def times_cos(t):
                    pool.wait_ge(q_normed, t + 1)
                    if t >= 2:
                        pool.wait_ge(q_final, t - 1)
                    pool.tensor_tensor(qc[:, t % 2, :], qn[:, t % 2, :], cos, ALU.mult).then_inc(q_cos, 1)

                def final(t):
                    pool.wait_ge(q_sin, t + 1)
                    pool.wait_ge(q_cos, t + 1)
                    if t < KT_N:
                        for half in range(2):
                            ins = pool.tensor_tensor(kd[:, 2 * t + half, :], qc[:, t % 2, :], pad[:, t % 2, 0:L], ALU.add)
                        ins.then_inc(q_final, 1)
                    else:
                        pool.tensor_tensor(qt[:, t - KT_N, :], qc[:, t % 2, :], pad[:, t % 2, 0:L], ALU.add).then_inc(q_final, 1)

                times_cos(0)
                for t in range(1, QKT):
                    times_cos(t)
                    final(t - 1)
                    if t == KT_N:
                        pool.wait_ge(q_final, KT_N)
                        pool.dma_start(kd[HD:P, 0:NKV:2, :], kd[0:HD, 0:NKV:2, :]).then_inc(k_dup, 16)
                        pool.dma_start(kd[0:HD, 1:NKV:2, :], kd[HD:P, 1:NKV:2, :]).then_inc(k_dup, 16)
                final(QKT - 1)

            def recurrent():
                for j, what in enumerate(REC_ORDER):
                    n = int(what[1])
                    b = n % 2
                    if what[0] == "x":
                        for i in range(2):
                            pool.wait_ge(xch_ready, 2 * n + i + 1)
                            pool.tensor_tensor(xcl[:, b, i, :], xc[:, b, i, :], xch[:, b, i, :].bitcast(F32), ALU.subtract).then_inc(xcl_ready, 1)
                    elif what[0] == "g":
                        pool.wait_ge(sig_done, 8 * n + 8)
                        for d in range(2):
                            pool.tensor_tensor(gi[:, b, d], gi[:, b, d], xc[:, b], ALU.mult).then_inc(ix_done, 1)
                        if n:
                            y_sum(n - 1)
                    elif n == 0:
                        y_sum(NB - 1)
                for n in range(NB):
                    pool.wait_ge(gelu_done, n + 1)
                    pool.wait_ge(ysum_done, n + 1)
                    s = slice(2 * n, 2 * n + 2)
                    t = slice(PROJ_T0[4], L)
                    pool.tensor_tensor(ys[:, s, t], ys[:, s, t], mg[:, s, t], ALU.mult).then_inc(y_full, 1)

            def y_sum(n):
                pool.wait_ge(scan_done, 4 * n + 4)
                pool.tensor_tensor(ys[:, 2 * n:2 * n + 2, :], gm[:, n % 2, 0], gm[:, n % 2, 1], ALU.add).then_inc(ysum_done, 1)

            sum_squares(0)
            sum_squares(1)
            rotary()
            sum_squares(2)
            sum_squares(3)
            sum_squares(4)
            recurrent()
            sum_squares(5)


_INS = ["x", "meta_tokens", "norm_gains", "ffn_w_in", "ffn_w_out", "attn_w_qkv", "attn_q_gain", "attn_k_gain",
        "attn_w_o", "rec_w_in", "rec_conv_w", "rec_conv_b", "rec_gate_w", "rec_gate_b", "rec_lambda", "rec_w_out"]
_LAYERED = _INS[5:]
_OUT = (1, SEQ, D)


def kernel(**inputs):
    import concourse.bacc as _bacc
    from concourse.bass_utils import run_bass_kernel_spmd as _run

    nc = _bacc.Bacc("TRN2", target_bir_lowering=False, num_devices=1)
    arrays, args = {}, []
    for name in _INS:
        a = np.ascontiguousarray(inputs[name])
        arrays[f"in_{name}"] = a
        ap = nc.dram_tensor(f"in_{name}", a.shape, mybir.dt.from_np(a.dtype), kind="ExternalInput").ap()
        args.append(ap[0] if name == "x" or name in _LAYERED else ap)
    arrays["in_consts"] = shape_constants()
    args.append(nc.dram_tensor("in_consts", (P, C_N), F32, kind="ExternalInput").ap())
    out = nc.dram_tensor("out_0", _OUT, F32, kind="ExternalOutput").ap()
    build(nc, *args, out[0])
    r = _run(nc, [arrays], core_ids=[0])
    return r.results[0]["out_0"]
```

```python
from contextlib import ExitStack

import numpy as np

import concourse.bass as bass
from concourse import mybir

ALU = mybir.AluOpType
ACT = mybir.ActivationFunctionType
F32 = mybir.dt.float32
F32R = mybir.dt.float32r
AX_X = mybir.AxisListType.X

P = 128
D = 1024
KC = D // P
SEQ = 256
META = 16
L = SEQ + META
FF = 2816
FC = FF // P
HD = 64
NKV = 4
GROUP = 4
QT_N = D // P
KT_N = NKV * HD // P
QKT = KT_N + QT_N
CONVW = 4
CONVL = 2
NB = 4
GRID_W = 64
THETA = 10000.0
EPS = 1e-6
WEIGHT_SLOTS = 4
UNIT_TILES = 16
OUT_K = (6, 6, 5, 5)
TOK = [(0, P), (P, P), (2 * P, L - 2 * P)]
KT = 96
KTOK = [0, KT, L - KT]
OVERLAP = 2 * KT - KTOK[2]

FFN_IN_UNITS = FC
FFN_OUT_UNITS = 4 * len(OUT_K)
FFN_UNITS = FFN_IN_UNITS + FFN_OUT_UNITS
U_QKV = FFN_UNITS
U_WO = U_QKV + 6
U_FFN = [0, U_WO + 4, U_WO + 4 + FFN_UNITS, 0]
U_REC = U_FFN[2] + FFN_UNITS
REC_ORDER = ["x0", "x1", "g0", "x2", "g1", "x3", "g2", "g3", "e0", "e1", "e2", "e3"]
U_ROUT = U_REC + len(REC_ORDER)
U_FFN[3] = U_ROUT + 4
UNITS = U_FFN[3] + FFN_UNITS

GAIN = lambda layer, i, c: (layer * 6 + i) * KC + c
V_CONVW, V_CONVB, V_GATEB, V_LAM, V_QG, V_KG = 0, 32, 40, 72, 88, 89
VB = 90
C_ID, C_ONES, C_BONES, C_ROT, C_COS, C_SIN = 0, P, P + 1, P + 3, 2 * P + 3, 2 * P + 3 + L
C_N = 2 * P + 3 + 2 * L

NPROJ = 6
TILES_S = 9


def shape_constants():
    c = np.zeros((P, C_N), np.float32)
    c[:, C_ID:C_ID + P] = np.eye(P)
    half = HD // 2
    for m in range(P):
        if m % HD < half:
            c[m + half, C_ROT + m] = -1.0
        else:
            c[m - half, C_ROT + m] = 1.0
    for half_tile in range(2):
        c[half_tile * HD:(half_tile + 1) * HD, C_BONES + half_tile] = 1.0 / HD
    c[:, C_ONES] = 1.0 / D
    inv = (np.float32(1.0) / (np.float32(THETA) ** (np.arange(0, half, 2, dtype=np.float32) / np.float32(half)))).astype(np.float32)
    pos = np.arange(SEQ)
    zeros = np.zeros(META, np.float32)
    row = np.concatenate([zeros, (pos // GRID_W).astype(np.float32)])
    col = np.concatenate([zeros, (pos % GRID_W).astype(np.float32)])
    theta = np.concatenate([row[:, None] * inv, col[:, None] * inv], axis=-1).astype(np.float32)
    cos, sin = np.cos(theta).T, np.sin(theta).T
    for b in range(P // half):
        c[b * half:(b + 1) * half, C_COS:C_COS + L] = cos
        c[b * half:(b + 1) * half, C_SIN:C_SIN + L] = sin
    return c


def build(nc, x, meta, gains, ffn_in, ffn_out, w_qkv, q_gain, k_gain, w_o, rec_in, conv_w, conv_b,
          gate_w, gate_b, lam, rec_out, consts, out):
    ctx = ExitStack()
    with ctx:
        def sb(name, shape, dt=F32):
            return ctx.enter_context(nc.sbuf_tensor(name, shape, dt))

        def sem(name):
            return ctx.enter_context(nc.semaphore(name))

        h = sb("h", [P, KC, L])
        xh, xl = sb("xh", [P, KC, L], F32R), sb("xl", [P, KC, L], F32R)
        raw = sb("raw", [P, WEIGHT_SLOTS, UNIT_TILES * P])
        wh = sb("wh", [P, WEIGHT_SLOTS, UNIT_TILES * P], F32R)
        wl = sb("wl", [P, WEIGHT_SLOTS, UNIT_TILES * P], F32R)
        mg = sb("mg", [P, KC, L])
        cst = sb("cst", [P, C_N])
        vec_a = sb("vec_a", [P, 96])
        vec_h = sb("vec_h", [P, 96])
        vec_b = sb("vec_b", [P, VB])
        tmp = sb("tmp", [P, 8, L])
        pad = sb("pad", [P, 2, L + 4])
        sqb = sb("sqb", [P, 2, L])
        sqh = sb("sqh", [P, 2, L])
        acc = sb("acc", [P, L])
        hacc = sb("hacc", [P, L])
        r = sb("r", [P, L])
        rc_pre = sb("rc_pre", [KT, 3])
        rc_post = sb("rc_post", [KT, 3])
        rsq = sb("rsq", [KT, 3])
        hs = sb("hs", [KT, QKT, 3, 2])
        warm = sb("warm", [1, 2])
        small = sb("small", [P, 8, 16])
        c4 = sb("c4", [P, 2, KC])
        c8 = sb("c8", [P, 2, KC])
        qg = sb("qg", [P, 2])
        nmax = sb("nmax", [P, NKV * TILES_S])
        rsum = sb("rsum", [P, NKV * TILES_S])
        rinv = sb("rinv", [P, NKV * TILES_S])
        prow = sb("prow", [P, 4, L])

        with nc.sbuf_tensor("ah", [P, FC, L], F32R) as ah, nc.sbuf_tensor("al", [P, FC, L], F32R) as al:
            pass
        with nc.sbuf_tensor("tok_in", [P, 3, D], F32) as tok_in, nc.sbuf_tensor("vrow", [96, 2, P], F32) as vrow, \
                nc.sbuf_tensor("tok_out", [P, 2, D], F32) as tok_out:
            pass
        with nc.sbuf_tensor("qt", [P, QT_N, L], F32) as qt, nc.sbuf_tensor("kd", [P, NKV, L], F32) as kd, \
                nc.sbuf_tensor("vt", [KT, 3, NKV * HD], F32) as vt, nc.sbuf_tensor("pt", [KT, 2, 3, GROUP, L], F32) as pt:
            pass
        with nc.sbuf_tensor("xch", [P, 2, 2, L], F32R) as xch, nc.sbuf_tensor("xcl", [P, 2, 2, L], F32R) as xcl, \
                nc.sbuf_tensor("xc", [P, 2, 2, L], F32) as xc, nc.sbuf_tensor("gr", [P, 2, 2, 2, L], F32) as gr, \
                nc.sbuf_tensor("gi", [P, 2, 2, 2, L], F32) as gi, nc.sbuf_tensor("gw", [P, 2, 2, 2, L], F32) as gw, \
                nc.sbuf_tensor("gm", [P, 2, 2, 2, L], F32) as gm:
            pass
        ctx.enter_context(nc.sbuf_tensor("region", [P, 2 * FC * L], F32))

        bank = [ctx.enter_context(nc.psum_tensor(f"bank{i}", [P, 512], F32)) for i in range(8)]
        SUM_POST, SUM_PRE = bank[6], bank[7]
        SC = 384
        QSUM, ROTB, QSCALE = bank[5], bank[6], bank[7]
        S_BANK = (bank[0], bank[1], bank[6], bank[7])

        ident = cst[:, C_ID:C_ID + P]
        rotm = cst[:, C_ROT:C_ROT + P]
        head_mean_w = cst[:, C_BONES:C_BONES + 2]
        mean_w = cst[:, C_ONES:C_ONES + 1]
        cos = cst[:, C_COS:C_COS + L]
        sin = cst[:, C_SIN:C_SIN + L]
        qp, qs, qn, qc = tmp[:, 0:2, :], tmp[:, 2:4, :], tmp[:, 4:6, :], tmp[:, 6:8, :]
        gp, sl, up, aa = qp, qs, qn, qc
        ys = tmp

        s_in = sem("inputs_landed")
        table_loaded, warm_set = sem("table_loaded"), sem("warm_set")
        s_rope = sem("rotary_tables_landed")
        s_xin = sem("tokens_landed")
        landed = [sem(f"landed{i}") for i in range(WEIGHT_SLOTS)]
        wh_ready, w_ready, out_unit_used = sem("wh_ready"), sem("w_ready"), sem("out_unit_used")
        vecs_t, x_trans = sem("vecs_transposed"), sem("x_transposed")
        lam_a, lam_v = sem("lambda_act"), sem("lambda_dve")
        h_ready, xh_ready, x_ready = sem("h_ready"), sem("xh_ready"), sem("x_ready")
        hsq_ready, hacc_step, pre_sum, pre_root, rc_ready, r_spread, r_ready = (sem(n) for n in (
            "hsq_ready", "hacc_step", "pre_sum", "pre_root", "rc_ready", "r_spread", "r_ready"))
        gu_done, gate_scaled, silu_done, up_scaled, a_full, ah_ready, a_ready = (sem(n) for n in (
            "gu_done", "gate_scaled", "silu_done", "up_scaled", "a_full", "ah_ready", "a_ready"))
        proj_done, sq_ready, mg_ready, acc_step, post_sum, post_root, rt_ready, rt_spread, mg_scaled = (sem(n) for n in (
            "proj_done", "sq_ready", "mg_ready", "acc_step", "post_sum", "post_root", "rt_ready", "rt_spread", "mg_scaled"))
        qk_done, q_squared, q_gained, q_sum, q_step, q_root, q_rot, q_cos, q_sin, q_roped, q_spread, q_final = (sem(n) for n in (
            "qk_done", "q_squared", "q_gained", "q_sum", "q_step", "q_root", "q_rot", "q_cos", "q_sin", "q_roped", "q_spread", "q_final"))
        v_done, rsq_ready, v_ready, k_dup = (sem(n) for n in ("v_done", "rsq_ready", "v_ready", "k_dup"))
        s_done, nmax_ready, p_exp, p_inv, p_norm, t_done, pt_even, pt_odd, pv_done, oh_ready, o_ready = (sem(n) for n in (
            "s_done", "nmax_ready", "p_exp", "p_inv", "p_norm", "t_done", "pt_even", "pt_odd", "pv_done", "oh_ready", "o_ready"))
        xr_done, pad_zero, xr_scaled, conv0, conv_step, xch_ready, xcl_ready = (sem(n) for n in (
            "xr_done", "pad_zero", "xr_scaled", "conv0", "conv_step", "xch_ready", "xcl_ready"))
        g_done, sig_done, exp_done, tanh_done, rec_step, root_done, ix_done, b_done, scan_done, ysum_done = (sem(n) for n in (
            "g_done", "sig_done", "exp_done", "tanh_done", "rec_step", "root_done", "ix_done", "b_done", "scan_done", "ysum_done"))
        e_done, e_scaled, gelu_done, y_full, yh_ready, y_ready = (sem(n) for n in (
            "e_done", "e_scaled", "gelu_done", "y_full", "yh_ready", "y_ready"))
        out_t, s_out = sem("out_transposed"), sem("out_stored")
        out_copied = [sem("out_copied0"), sem("out_copied1")]
        vec_ready = sem("vec_ready")

        landed_at, count = [], [0] * WEIGHT_SLOTS
        for u in range(UNITS):
            gates = U_REC <= u < U_ROUT and REC_ORDER[u - U_REC][0] == "g"
            count[u % WEIGHT_SLOTS] += 64 if gates else 16
            landed_at.append(count[u % WEIGHT_SLOTS])

        def slot(u):
            return u % WEIGHT_SLOTS

        FFN_OF_PROJ = {0: 0, 2: 1, 3: 2, 5: 3}
        X_OF_FFN = (0, 2, 3, 5)
        PRE_GAIN = [(0, 0), (0, 2), (0, 4), (1, 0), (1, 2), (1, 4)]
        POST_GAIN = [(0, 1), (0, 3), (0, 5), (1, 1), (1, 3), (1, 5)]
        PROJ_BANKS = {n: ((4, 5), (0, 1), (0, 1), (2, 3)) if n in FFN_OF_PROJ else ((0, 1), (2, 3), (4, 5), (0, 1)) for n in range(NPROJ)}
        PROJ_T0 = [META if n >= 4 else 0 for n in range(NPROJ)]
        FFN_T0 = [0, 0, 0, META]
        ACC = 8

        def turned_tile(a):
            j, t = divmod(a, TILES_S)
            src = bank[2 + a % 2][0:KT, 0:3 * P]
            if t == 0:
                return pt[:, j % 2, :, :, 2 * P:L], src.rearrange("p (c g q) -> p c g q", c=3, g=GROUP)[:, :, :, 16:32]
            g, half = divmod(t - 1, 2)
            return pt[:, j % 2, :, g, P * half:P * half + P], src.rearrange("p (c q) -> p c q", c=3)

        def ffn_banks(m):
            return {0: (0, 1), 1: (2, 3), 2: (4, 5)}.get(m, (2, 3) if m % 2 == 0 else (0, 1))

        block = ctx.enter_context(nc.Block())

        @block.sync
        def _(sp):
            def load(u, it, kn, src):
                if u >= WEIGHT_SLOTS:
                    sp.wait_ge(w_ready, u - WEIGHT_SLOTS + 1 + WEIGHT_SLOTS * it)
                dst = raw[:, slot(u), 0:kn * 256].rearrange("p (k c) -> p k c", k=kn)
                sp.dma_start(dst, src).then_inc(landed[slot(u)], 16)

            def ffn(n):
                u0 = U_FFN[n]
                vin = ffn_in[n // 2, n % 2].rearrange("(k p) c -> p k c", p=P)
                vout = ffn_out[n // 2, n % 2].rearrange("(k p) c -> p k c", p=P)

                def pair(u, it, col):
                    load(u, it, KC, vin[:, :, bass.ds(col, 256)])
                    load(u + 1, it, KC, vin[:, :, bass.ds(col + FF, 256)])

                pair(u0, 0, 0)
                pair(u0 + 2, 0, 256)
                with sp.Fori(0, 4) as it:
                    pair(u0 + 4, it, 512 * it + 512)
                    pair(u0 + 6, it, 512 * it + 768)
                pair(u0 + 20, 0, 2560)
                with sp.Fori(0, 4) as it:
                    k0 = 0
                    for j, kn in enumerate(OUT_K):
                        load(u0 + FFN_IN_UNITS + j, it, kn, vout[:, k0:k0 + kn, bass.ds(256 * it, 256)])
                        k0 += kn

            sp.dma_start(tok_in[META:P, 0, :], x[0:P - META, :]).then_inc(s_xin, 16)
            sp.dma_start(tok_in[:, 1, :], x[P - META:2 * P - META, :]).then_inc(s_xin, 16)
            ffn(0)
            v = w_qkv.rearrange("(k p) c -> p k c", p=P)
            for j, c0 in enumerate((1024, 1280, 0, 256, 512, 768)):
                load(U_QKV + j, 0, KC, v[:, :, c0:c0 + 256])
            v = w_o.rearrange("(k p) c -> p k c", p=P)
            for j in range(4):
                load(U_WO + j, 0, KC, v[:, :, 256 * j:256 * j + 256])
            ffn(1)
            ffn(2)
            v = rec_in.rearrange("(k p) c -> p k c", p=P)
            for j, what in enumerate(REC_ORDER):
                n, u = int(what[1]), U_REC + j
                if what[0] == "g":
                    sp.wait_ge(w_ready, u - WEIGHT_SLOTS + 1)
                    dst = raw[:, slot(u), :].rearrange("p (g k c) -> p g k c", g=4, k=2)
                    for g in range(4):
                        sp.dma_start(dst[:, g], gate_w[g // 2, g % 2, n].rearrange("(k p) c -> p k c", p=P)).then_inc(landed[slot(u)], 16)
                else:
                    c0 = (D if what[0] == "x" else 0) + 256 * n
                    load(u, 0, KC, v[:, :, c0:c0 + 256])
            v = rec_out.rearrange("(k p) c -> p k c", p=P)
            for j in range(4):
                load(U_ROUT + j, 0, KC, v[:, :, 256 * j:256 * j + 256])
            ffn(3)
            for t in range(2):
                sp.wait_ge(out_copied[t], 2)
                sp.dma_start(out[t * P:(t + 1) * P, :], tok_out[:, t, :]).then_inc(s_out, 16)
            sp.wait_ge(s_out, 32)

        @block.tensor
        def _(pe):
            def product(dst, u, tile, mh, ml, first, last):
                a = wh[:, slot(u), tile * P:(tile + 1) * P]
                b = wl[:, slot(u), tile * P:(tile + 1) * P]
                pe.matmul(dst, b, mh, start=first, stop=False)
                pe.matmul(dst, a, ml, start=False, stop=False)
                return pe.matmul(dst, a, mh, start=False, stop=last)

            def spread(dst, cols, heads=1):
                size = P // heads
                for c, a in enumerate(KTOK):
                    for g in range(heads):
                        w = cols[:, heads * c + g:heads * c + g + 1].broadcast_to([KT, size])
                        last = pe.matmul(dst[g * size:(g + 1) * size, a:a + KT], w, ident[0:KT, 0:KT], start=True, stop=True)
                return last

            def mean_of_h(n):
                pe.wait_ge(hacc_step, 8 * n + 8)
                for c, a in enumerate(KTOK):
                    last = pe.matmul(SUM_PRE[0:KT, SC + c:SC + c + 1], hacc[:, a:a + KT], mean_w, start=True, stop=True)
                last.then_inc(pre_sum, 1)

            def spread_r(n):
                pe.wait_ge(rc_ready, n + 1)
                spread(SUM_PRE, rc_pre).then_inc(r_spread, 1)

            def ffn(n):
                u0, f0, x0, t0, pj = U_FFN[n], n * FC, X_OF_FFN[n] * KC, FFN_T0[n], X_OF_FFN[n]

                pe.wait_ge(w_ready, u0 + 2)
                for k in range(KC):
                    pe.wait_ge(x_ready, x0 + k + 1)
                    for part in range(2):
                        for m in range(2):
                            last = product(bank[ffn_banks(m)[part]][:, t0:L], u0 + part, 2 * k + m,
                                           xh[:, k, t0:L], xl[:, k, t0:L], k == 0, k == KC - 1)
                            if k == KC - 1 and part == 1:
                                last.then_inc(gu_done, 1)
                mean_of_h(X_OF_FFN[n])

                def mtile(u, it, m, banks, f, before):
                    if m == 0:
                        pe.wait_ge(w_ready, u + 2 + WEIGHT_SLOTS * it)
                    if before is not None:
                        pe.wait_ge(up_scaled, before + 1 + WEIGHT_SLOTS * it)
                    for part in range(2):
                        for k in range(KC):
                            last = product(bank[banks[part]][:, t0:L], u + part, 2 * k + m,
                                           xh[:, k, t0:L], xl[:, k, t0:L], k == 0, k == KC - 1)
                            if f == f0 + 2 and part == 0 and k == 3:
                                spread_r(X_OF_FFN[n])
                    last.then_inc(gu_done, 1)

                def pair(p, it):
                    for j in range(2):
                        m = 2 * p + j
                        before = {2: None, 3: f0, 4: f0 + 1}.get(m, f0 + m - 2)
                        mtile(u0 + 2 * p, it, j, ffn_banks(m), f0 + m, before)

                pair(1, 0)
                pair(2, 0)
                pair(3, 0)
                with pe.Fori(0, 3) as it:
                    pair(4, it)
                    pair(5, it)
                pair(10, 0)

                v0 = u0 + FFN_IN_UNITS

                def group(g, it, banks, check):
                    k0 = 0
                    for j, kn in enumerate(OUT_K):
                        pe.wait_ge(w_ready, v0 + 4 * g + j + 1 + WEIGHT_SLOTS * it)
                        for m in range(2):
                            if check and j == 0:
                                pe.wait_ge(mg_ready, 8 * pj + 2 * g + m - 1 + 2 * it)
                            for k in range(kn):
                                if g == 0 and m == 0:
                                    pe.wait_ge(a_ready, f0 + k0 + k + 1)
                                last = product(bank[banks[m]][:, t0:L], v0 + 4 * g + j, 2 * k + m,
                                               ah[:, k0 + k, t0:L], al[:, k0 + k, t0:L],
                                               k0 + k == 0, k0 + k == FC - 1)
                            if j == len(OUT_K) - 1:
                                last.then_inc(proj_done, 1)
                            elif m == 1:
                                last.then_inc(out_unit_used, 1)
                        k0 += kn

                group(0, 0, PROJ_BANKS[pj][0], False)
                with pe.Fori(0, 2) as it:
                    group(1, it, PROJ_BANKS[pj][1], True)
                group(3, 0, PROJ_BANKS[pj][3], False)
                mean_of_projection(pj)

            def mean_of_projection(pj):
                first = True
                for ready, value, squares in ((acc_step, ACC * pj + ACC, acc[:, :]),
                                              (sq_ready, 8 * pj + 7, sqb[:, 0, :]), (sq_ready, 8 * pj + 8, sqb[:, 1, :])):
                    pe.wait_ge(ready, value)
                    for c, a in enumerate(KTOK):
                        last = pe.matmul(SUM_POST[0:KT, SC + c:SC + c + 1], squares[:, a:a + KT], mean_w,
                                         start=first, stop=value == 8 * pj + 8, skip_group_check=True)
                        first = False
                last.then_inc(post_sum, 1)
                pe.wait_ge(rt_ready, pj + 1)
                spread(SUM_POST, rc_post).then_inc(rt_spread, 1)

            def projection(pj, u0, ready, step):
                t0 = PROJ_T0[pj]
                for g in range(4):
                    pe.wait_ge(w_ready, u0 + g + 1)
                    for m in range(2):
                        if g == 3:
                            pe.wait_ge(mg_ready, 8 * pj + m + 1)
                        for k in range(KC):
                            if g == 0 and m == 0:
                                pe.wait_ge(ready, k // step + 1)
                            last = product(bank[PROJ_BANKS[pj][g][m]][:, t0:L], u0 + g, 2 * k + m,
                                           xh[:, k, t0:L], xl[:, k, t0:L], k == 0, k == KC - 1)
                        last.then_inc(proj_done, 1)
                mean_of_projection(pj)

            def attention():
                pe.wait_ge(w_ready, U_QKV + 2)
                for k in range(KC):
                    pe.wait_ge(x_ready, KC + k + 1)
                    for m in range(KT_N):
                        last = product(bank[m][:, 0:L], U_QKV, 2 * k + m, xh[:, k, :], xl[:, k, :], k == 0, k == KC - 1)
                        if k == KC - 1:
                            last.then_inc(qk_done, 1)
                    for c, a in enumerate(KTOK):
                        dst = bank[2 + c][0:KT, 0:NKV * HD]
                        wv_h = wh[:, slot(U_QKV + 1), k * 256:(k + 1) * 256]
                        wv_l = wl[:, slot(U_QKV + 1), k * 256:(k + 1) * 256]
                        pe.matmul(dst, xl[:, k, a:a + KT], wv_h, start=k == 0, stop=False)
                        pe.matmul(dst, xh[:, k, a:a + KT], wv_l, start=False, stop=False)
                        last = pe.matmul(dst, xh[:, k, a:a + KT], wv_h, start=False, stop=k == KC - 1)
                last.then_inc(v_done, 1)
                mean_of_h(1)

                def head_means(t):
                    pe.wait_ge(q_squared, t + 1)
                    if t:
                        pe.wait_ge(q_step, 3 * t - 2)
                    for c, a in enumerate(KTOK):
                        last = pe.matmul(QSUM[0:KT, 2 * c:2 * c + 2], qs[:, t % 2, a:a + KT], head_mean_w, start=True, stop=True)
                    last.then_inc(q_sum, 1)

                def rotate(t):
                    pe.wait_ge(q_gained, t + 1)
                    if t:
                        pe.wait_ge(q_sin, t)
                    pe.matmul(ROTB[:, 0:L], rotm, qp[:, t % 2, :], start=True, stop=True).then_inc(q_rot, 1)

                def spread_scale(t):
                    pe.wait_ge(q_step, 3 * t + 3)
                    if t:
                        pe.wait_ge(q_final, t)
                    spread(QSCALE, hs[:, t].rearrange("p c g -> p (c g)"), 2).then_inc(q_spread, 1)

                pe.wait_ge(s_rope, 16)
                for t in range(KT_N, QKT):
                    if t % 2 == 0:
                        pe.wait_ge(w_ready, U_QKV + 2 + (t - KT_N) // 2 + 1)
                    pe.wait_ge(q_gained, t - 1)
                    for k in range(KC):
                        last = product(bank[t % 2][:, 0:L], U_QKV + 2 + (t - KT_N) // 2, 2 * k + t % 2,
                                       xh[:, k, :], xl[:, k, :], k == 0, k == KC - 1)
                        if t == KT_N and k == 3:
                            spread_r(1)
                    last.then_inc(qk_done, 1)
                    if t == KT_N:
                        head_means(0)
                        rotate(0)
                    head_means(t - 1)
                    rotate(t - 1)
                    spread_scale(t - 2)
                head_means(QKT - 1)
                rotate(QKT - 1)
                spread_scale(QKT - 2)
                spread_scale(QKT - 1)

                def scores(a):
                    j, t = divmod(a, TILES_S)
                    dst = S_BANK[a % 4]
                    if a >= 4:
                        pe.wait_ge(p_exp, a - 3)
                    if t == 0:
                        pe.wait_ge(q_final, KT_N + 2 * j + 2)
                        for g in range(GROUP):
                            o = HD * (g % 2)
                            last = pe.matmul(dst[32 * g:32 * g + 32, 0:L], qt[o:o + HD, 2 * j + g // 2, L - 32:L],
                                             kd[o:o + HD, j, :], start=True, stop=True)
                    else:
                        g, half = divmod(t - 1, 2)
                        o = HD * (g % 2)
                        last = pe.matmul(dst[:, 0:L], qt[o:o + HD, 2 * j + g // 2, P * half:P * half + P],
                                         kd[o:o + HD, j, :], start=True, stop=True)
                    last.then_inc(s_done, 1)

                def turned(a):
                    pe.wait_ge(pt_odd if a % 2 else pt_even, a // 2 + 1)

                def turn(a):
                    pe.wait_ge(p_norm, a + 1)
                    if a >= 2:
                        turned(a - 2)
                    for c, k0 in enumerate(KTOK):
                        last = pe.transpose(bank[2 + a % 2][0:KT, c * P:(c + 1) * P], prow[:, a % 4, k0:k0 + KT], ident)
                    last.then_inc(t_done, 1)

                def weigh(j, g):
                    a, pair = j * TILES_S + 2 * g + 2, 2 * j + g // 2
                    turned(a)
                    turned(a - 1)
                    if g == 0:
                        turned(j * TILES_S)
                    if pair >= 2 and g % 2 == 0:
                        pe.wait_ge(o_ready, pair - 1)
                    o = HD * (g % 2)
                    for c in range(3):
                        last = pe.matmul(bank[4 + pair % 2][o:o + HD, 0:L], vt[:, c, HD * j:HD * j + HD],
                                         pt[:, j % 2, c, g, :], start=c == 0, stop=c == 2)
                    if g % 2:
                        last.then_inc(pv_done, 1)

                pe.wait_ge(k_dup, 32)
                pe.wait_ge(v_ready, 4)
                pe.wait_ge(q_final, QKT)
                tiles = NKV * TILES_S
                for a in range(3):
                    scores(a)
                for a in range(tiles):
                    if a + 3 < tiles:
                        scores(a + 3)
                    turn(a)
                    j, t = divmod(a - 1, TILES_S)
                    if a >= 1 and t >= 2 and t % 2 == 0:
                        weigh(j, (t - 2) // 2)
                weigh(NKV - 1, GROUP - 1)

            def recurrent():
                t0 = PROJ_T0[4]
                for j, what in enumerate(REC_ORDER):
                    n, u = int(what[1]), U_REC + j
                    pe.wait_ge(w_ready, u + 1)
                    if what[0] == "g":
                        pe.wait_ge(xcl_ready, 2 * n + 2)
                        for g in range(4):
                            for m in range(2):
                                o = 8 * n + 2 * g + m
                                if o >= 4:
                                    pe.wait_ge(sig_done, o - 3)
                                for k in range(2):
                                    last = product(bank[4 + o % 4][:, 0:L], u, (g * 2 + k) * 2 + m,
                                                   xch[:, n % 2, k, :], xcl[:, n % 2, k, :], k == 0, k == 1)
                                last.then_inc(g_done, 1)
                    elif what == "x0":
                        for k in range(KC):
                            pe.wait_ge(x_ready, 4 * KC + k + 1)
                            for m in range(2):
                                last = product(bank[m][:, 0:L], u, 2 * k + m, xh[:, k, :], xl[:, k, :], k == 0, k == KC - 1)
                                if k == KC - 1:
                                    last.then_inc(xr_done, 1)
                        mean_of_h(4)
                        spread_r(4)
                    else:
                        x_part = what[0] == "x"
                        a = 0 if x_part else t0
                        for m in range(2):
                            if n:
                                pe.wait_ge(xr_scaled if x_part else e_scaled, 2 * n + m - 1)
                            for k in range(KC):
                                last = product(bank[(0 if x_part else 2) + m][:, a:L], u, 2 * k + m,
                                               xh[:, k, a:L], xl[:, k, a:L], k == 0, k == KC - 1)
                            last.then_inc(xr_done if x_part else e_done, 1)

            pe.wait_ge(s_in, 16 * 8)
            pe.transpose(bank[4][:, 0:96], vrow[:, 0, :], ident[0:96, 0:96])
            pe.transpose(bank[4][:, 96:96 + VB], vrow[0:VB, 1, :], ident[0:VB, 0:VB]).then_inc(vecs_t, 1)
            pe.wait_ge(s_xin, 64)
            for c in range(KC):
                if c >= 4:
                    pe.wait_ge(h_ready, c - 3)
                elif c == 0:
                    pe.wait_ge(vec_ready, 3)
                for t, (a, n) in enumerate(TOK):
                    last = pe.transpose(bank[4 + c % 4][:, a:a + n], tok_in[0:n, t, c * P:(c + 1) * P], ident[0:n, 0:n])
                last.then_inc(x_trans, 1)
            ffn(0)
            attention()
            projection(1, U_WO, o_ready, 1)
            ffn(1)
            ffn(2)
            recurrent()
            projection(4, U_ROUT, y_ready, 2)
            ffn(3)
            for c in range(KC):
                pe.wait_ge(h_ready, 6 * KC + c + 1)
                for t in range(2):
                    last = pe.transpose(bank[2 * t + c // 4][:, (c % 4) * P:(c % 4 + 1) * P],
                                        h[:, c, META + t * P:META + (t + 1) * P], ident)
                    if c % 4 == 3:
                        last.then_inc(out_t, 1)

        @block.scalar
        def _(act):
            def high(u, it, kn=KC, freed=None):
                act.wait_ge(landed[slot(u)], landed_at[u] + 16 * it)
                if freed is not None:
                    act.wait_ge(*freed)
                act.activation(wh[:, slot(u), 0:kn * 256], raw[:, slot(u), 0:kn * 256], ACT.Copy).then_inc(wh_ready, 1)

            def make_x(n):
                t0 = PROJ_T0[n - 1] if n else 0
                for c in range(KC):
                    act.wait_ge(h_ready, 8 * n + c + 1)
                    g = GAIN(*PRE_GAIN[n], c)
                    act.activation(xh[:, c, t0:L], h[:, c, t0:L], ACT.Copy, scale=vec_a[:, g:g + 1]).then_inc(xh_ready, 1)
                    if 8 * n + c >= 2:
                        act.wait_ge(hacc_step, 8 * n + c - 1)
                    act.activation(sqh[:, c % 2, t0:L], h[:, c, t0:L], ACT.Square).then_inc(hsq_ready, 1)

            def root_of_h(n):
                act.wait_ge(pre_sum, n + 1)
                act.activation(rc_pre[:, :], SUM_PRE[0:KT, SC:SC + 3], ACT.Sqrt, bias=EPS).then_inc(pre_root, 1)

            def square_tile(pj, m, b, it=0):
                t0 = PROJ_T0[pj]
                gains_of = vec_h if pj in FFN_OF_PROJ else vec_a
                g = GAIN(*POST_GAIN[pj], 0) + m
                act.wait_ge(proj_done, 8 * pj + m + 1 + 2 * it)
                act.wait_ge(acc_step, ACC * pj + m + 1 + 2 * it)
                act.activation(sqb[:, m % 2, t0:L], bank[b][:, t0:L], ACT.Square).then_inc(sq_ready, 1)
                if isinstance(it, int):
                    act.activation(mg[:, m, t0:L], bank[b][:, t0:L], ACT.Copy, scale=gains_of[:, g:g + 1]).then_inc(mg_ready, 1)
                else:
                    act.activation(mg[:, bass.ds(2 * it + m, 1), t0:L].rearrange("p a l -> p (a l)"), bank[b][:, t0:L],
                                   ACT.Copy, scale=gains_of[:, bass.ds(2 * it + g, 1)]).then_inc(mg_ready, 1)

            def root_of_projection(pj):
                act.wait_ge(post_sum, pj + 1)
                act.activation(rc_post[:, :], SUM_POST[0:KT, SC:SC + 3], ACT.Sqrt, bias=EPS).then_inc(post_root, 1)

            def load_table(func):
                act.activation(warm[:, 1:2], warm[:, 0:1], func).then_inc(table_loaded, 1)

            def ffn(n, after):
                u0, f0, t0, pj = U_FFN[n], n * FC, FFN_T0[n], X_OF_FFN[n]
                root_of_h(X_OF_FFN[n])
                load_table(ACT.Silu)

                def tile(m, it=0):
                    b = m % 2
                    act.wait_ge(gate_scaled, f0 + m + 1 + 4 * it)
                    if f0 + m >= 2:
                        act.wait_ge(a_full, f0 + m - 1 + 4 * it)
                    act.activation(sl[:, b, t0:L], gp[:, b, t0:L], ACT.Silu).then_inc(silu_done, 1)
                    act.wait_ge(a_full, f0 + m + 1 + 4 * it)
                    act.activation(ah[:, m, t0:L] if isinstance(it, int) else
                                   ah[:, bass.ds(4 * it + m, 1), t0:L].rearrange("p a l -> p (a l)"),
                                   aa[:, b, t0:L], ACT.Copy).then_inc(ah_ready, 1)

                def pair(p, it=0):
                    tile(2 * p, it)
                    tile(2 * p + 1, it)
                    for j in range(2):
                        out_unit = 2 * p + j + 4 - FFN_IN_UNITS
                        high(u0 + 2 * p + j + 4, it, OUT_K[out_unit] if out_unit >= 0 else KC)

                pair(0)
                pair(1)
                with act.Fori(0, 3) as it:
                    pair(2, it)
                    pair(3, it)
                pair(8)
                pair(9)
                pair(10)

                def group(g, it=0):
                    for j in range(3):
                        used = 12 * n + 3 * g + j + 1 + 3 * it
                        next_unit(g, j, it, (out_unit_used, used))
                    square_tile(pj, 2 * g, PROJ_BANKS[pj][g][0], it)
                    square_tile(pj, 2 * g + 1, PROJ_BANKS[pj][g][1], it)
                    if g < 3:
                        next_unit(g, 3, it, None)

                def next_unit(g, j, it, freed):
                    if g < 3:
                        high(u0 + FFN_IN_UNITS + 4 * g + j + 4, it, OUT_K[j], freed)
                    elif after is not None:
                        high(u0 + FFN_UNITS + j, 0, KC, freed)

                load_table(ACT.Sqrt)
                group(0)
                with act.Fori(0, 2) as it:
                    group(1, it)
                group(3)
                root_of_projection(pj)

            def projection(pj, u0):
                for g in range(4):
                    square_tile(pj, 2 * g, PROJ_BANKS[pj][g][0])
                    square_tile(pj, 2 * g + 1, PROJ_BANKS[pj][g][1])
                    if g < 3:
                        high(u0 + g + 4, 0)
                root_of_projection(pj)

            def attention():
                def squared(t):
                    act.wait_ge(qk_done, t + 1)
                    if t >= 2:
                        act.wait_ge(q_sum, t - 1)
                    act.activation(qs[:, t % 2, :], bank[t % 2][:, 0:L], ACT.Square).then_inc(q_squared, 1)
                    if t >= 2:
                        act.wait_ge(q_rot, t - 1)
                        act.wait_ge(q_cos, t - 1)
                    g = 1 if t < KT_N else 0
                    act.activation(qp[:, t % 2, :], bank[t % 2][:, 0:L], ACT.Copy, scale=qg[:, g:g + 1]).then_inc(q_gained, 1)

                def root(t):
                    act.wait_ge(q_step, 3 * t + 1)
                    v = hs[:, t].rearrange("p c g -> p (c g)")
                    act.activation(v, v, ACT.Sqrt, bias=EPS).then_inc(q_root, 1)

                squared(0)
                squared(1)
                root_of_h(1)
                act.wait_ge(v_done, 1)
                high(U_QKV + 4, 0)
                high(U_QKV + 5, 0)
                for t in range(KT_N, QKT):
                    squared(t)
                    root(t - 2)
                    if t % 2:
                        high(U_QKV + 2 + (t - KT_N) // 2 + 4, 0)
                root(QKT - 2)
                root(QKT - 1)
                load_table(ACT.Exp)

                def exponent(a):
                    act.wait_ge(nmax_ready, a + 1)
                    if a >= 4:
                        act.wait_ge(t_done, a - 3)
                    act.activation(prow[:, a % 4, :], S_BANK[a % 4][:, 0:L], ACT.Exp, bias=nmax[:, a:a + 1],
                                   accum_out=rsum[:, a:a + 1]).then_inc(p_exp, 1)

                def place(a):
                    act.wait_ge(t_done, a + 1)
                    if a % TILES_S < 2 and a >= 2 * TILES_S:
                        act.wait_ge(pv_done, 2 * (a // TILES_S) - 2)
                    dst, src = turned_tile(a)
                    act.activation(dst, src, ACT.Copy).then_inc(pt_even, 1)

                def out_high(pair):
                    act.wait_ge(pv_done, pair + 1)
                    act.activation(xh[:, pair, :], bank[4 + pair % 2][:, 0:L], ACT.Copy).then_inc(oh_ready, 1)

                tiles = NKV * TILES_S
                exponent(0)
                exponent(1)
                for a in range(tiles):
                    if a + 2 < tiles:
                        exponent(a + 2)
                    if a % 2 == 0:
                        place(a)
                    j, t = divmod(a - 2, TILES_S)
                    if a >= 2 and t in (4, 8):
                        out_high(2 * j + (t == 8))
                out_high(2 * NKV - 1)
                load_table(ACT.Sqrt)

            def recurrent():
                root_of_h(4)
                for j, what in enumerate(REC_ORDER):
                    n, u = int(what[1]), U_REC + j
                    b = n % 2
                    if what[0] == "x":
                        for i in range(2):
                            m = 2 * n + i
                            act.wait_ge(xr_scaled, m + 1)
                            if n >= 2:
                                act.wait_ge(ix_done, 2 * n - 2)
                            act.activation(xc[:, b, i, :], pad[:, i, 0:L], ACT.Identity, scale=vec_b[:, V_CONVW + m:V_CONVW + m + 1],
                                           bias=vec_b[:, V_CONVB + m:V_CONVB + m + 1]).then_inc(conv0, 1)
                            act.wait_ge(conv_step, 3 * m + 3)
                            if n >= 2:
                                act.wait_ge(g_done, 8 * n - 8)
                            act.activation(xch[:, b, i, :], xc[:, b, i, :], ACT.Copy).then_inc(xch_ready, 1)
                        high(u + 4, 0)
                    elif what[0] == "g":
                        for g in range(4):
                            for i in range(2):
                                o = 8 * n + 2 * g + i
                                act.wait_ge(g_done, o + 1)
                                if n >= 2 and o % 8 == 0:
                                    act.wait_ge(scan_done, 4 * n - 4)
                                dst = (gr, gi)[g % 2][:, b, g // 2, i, :]
                                v = V_GATEB + g * KC + 2 * n + i
                                act.activation(dst, bank[4 + o % 4][:, 0:L], ACT.Sigmoid, bias=vec_b[:, v:v + 1]).then_inc(sig_done, 1)
                        act.wait_ge(sig_done, 8 * n + 8)
                        for d in range(2):
                            for i in range(2):
                                act.activation(gw[:, b, d, i, :], gr[:, b, d, i, :], ACT.Exp,
                                               scale=c8[:, d, 2 * n + i:2 * n + i + 1]).then_inc(exp_done, 1)
                        act.wait_ge(exp_done, 4 * n + 4)
                        for d in range(2):
                            for i in range(2):
                                act.activation(gr[:, b, d, i, :], gr[:, b, d, i, :], ACT.Tanh,
                                               scale=c4[:, d, 2 * n + i:2 * n + i + 1]).then_inc(tanh_done, 1)
                        high(u + 4, 0)
                        act.wait_ge(rec_step, 3 * n + 3)
                        act.activation(gw[:, b], gw[:, b], ACT.Sqrt, scale=-1.0).then_inc(root_done, 1)
                    else:
                        act.wait_ge(e_scaled, 2 * n + 2)
                        v = mg[:, 2 * n:2 * n + 2, PROJ_T0[4]:L]
                        act.activation(v, v, ACT.Gelu_apprx_tanh).then_inc(gelu_done, 1)
                        high(u + 4, 0)
                act.wait_ge(e_done, KC)
                for n in range(NB):
                    act.wait_ge(y_full, n + 1)
                    act.activation(xh[:, 2 * n:2 * n + 2, PROJ_T0[4]:L], ys[:, 2 * n:2 * n + 2, PROJ_T0[4]:L], ACT.Copy).then_inc(yh_ready, 1)

            act.dma_start(cst[:, 0:C_ROT], consts[:, 0:C_ROT]).then_inc(s_in, 16)
            act.dma_start(tok_in[0:META, 0, :], meta).then_inc(s_xin, 16)
            act.dma_start(tok_in[0:L - 2 * P, 2, :], x[2 * P - META:SEQ, :]).then_inc(s_xin, 16)
            act.dma_start(vrow[:, 0, :], gains.rearrange("l i (c p) -> (l i c) p", p=P)).then_inc(s_in, 16)
            act.dma_start(vrow[V_CONVW:V_CONVB, 1, :], conv_w.rearrange("j (c p) -> (j c) p", p=P)).then_inc(s_in, 16)
            act.dma_start(vrow[V_CONVB:V_GATEB, 1, :], conv_b.rearrange("(c p) -> c p", p=P)).then_inc(s_in, 16)
            act.dma_start(vrow[V_GATEB:V_LAM, 1, :], gate_b.rearrange("d g (c p) -> (d g c) p", p=P)).then_inc(s_in, 16)
            act.dma_start(vrow[V_LAM:V_QG, 1, :], lam.rearrange("d (c p) -> (d c) p", p=P)).then_inc(s_in, 16)
            for row, gain in ((V_QG, q_gain), (V_KG, k_gain)):
                act.dma_start(vrow[row:row + 1, 1, :].rearrange("a (n p) -> a n p", n=2),
                              gain.rearrange("(a b p) -> a b p", a=1, b=1).broadcast_to([1, 2, HD])).then_inc(s_in, 16)
            act.dma_start(cst[:, C_ROT:C_N], consts[:, C_ROT:C_N]).then_inc(s_rope, 16)
            act.wait_ge(vec_ready, 3)
            act.activation(small[:, 0, :], vec_b[:, V_LAM:V_QG], ACT.Abs).then_inc(lam_a, 1)
            act.wait_ge(lam_a, 1)
            act.activation(small[:, 1, :], small[:, 0, :], ACT.Exp, scale=-1.0).then_inc(lam_a, 1)
            act.wait_ge(warm_set, 1)
            make_x(0)
            high(0, 0)
            high(1, 0)
            high(2, 0)
            high(3, 0)
            ffn(0, True)
            make_x(1)
            high(U_FFN[0] + FFN_UNITS + 3, 0)
            attention()
            projection(1, U_WO)
            make_x(2)
            high(U_WO + 3 + 4, 0)
            ffn(1, True)
            make_x(3)
            high(U_FFN[1] + FFN_UNITS + 3, 0)
            ffn(2, True)
            make_x(4)
            high(U_FFN[2] + FFN_UNITS + 3, 0)
            recurrent()
            projection(4, U_ROUT)
            make_x(5)
            high(U_ROUT + 3 + 4, 0)
            ffn(3, None)
            for i in range(2):
                act.wait_ge(out_t, 2 * i + 2)
                act.activation(tok_out[:, 1, 512 * i:512 * i + 512], bank[2 + i][:, :], ACT.Copy).then_inc(out_copied[1], 1)

        @block.vector
        def _(dve):
            def low(u, it, kn=KC):
                dve.wait_ge(wh_ready, u + 1 + WEIGHT_SLOTS * it)
                w = raw[:, slot(u), 0:kn * 256]
                dve.tensor_tensor(wl[:, slot(u), 0:kn * 256], w, wh[:, slot(u), 0:kn * 256].bitcast(F32), ALU.subtract).then_inc(w_ready, 1)

            def low_x(n, c):
                t0 = PROJ_T0[n - 1] if n else 0
                g = GAIN(*PRE_GAIN[n], c)
                dve.wait_ge(xh_ready, 8 * n + c + 1)
                dve.scalar_tensor_tensor(xl[:, c, t0:L], h[:, c, t0:L], vec_a[:, g:g + 1], xh[:, c, t0:L].bitcast(F32),
                                         ALU.mult, ALU.subtract).then_inc(x_ready, 1)

            def rc_of_h(n):
                dve.wait_ge(pre_root, n + 1)
                dve.reciprocal(rc_pre[:, :], rc_pre[:, :]).then_inc(rc_ready, 1)

            def r_of_h(n):
                rc_of_h(n)
                dve.wait_ge(r_spread, n + 1)
                dve.tensor_copy(r[:, :], SUM_PRE[:, 0:L]).then_inc(r_ready, 1)
                dve.wait_ge(r_ready, n + 1 if n == 0 else n)

            def add_squares(pj, m, it=0):
                t0 = PROJ_T0[pj]
                dve.wait_ge(sq_ready, 8 * pj + m + 1 + 2 * it)
                dve.wait_ge(acc_step, ACC * pj + m + 2 + 2 * it)
                dve.tensor_tensor(acc[:, t0:L], acc[:, t0:L], sqb[:, m % 2, t0:L], ALU.add).then_inc(acc_step, 1)

            def residual(pj):
                n, t0 = pj + 1, PROJ_T0[pj]
                dve.wait_ge(post_root, pj + 1)
                dve.reciprocal(rc_post[:, :], rc_post[:, :]).then_inc(rt_ready, 1)
                dve.wait_ge(mg_ready, 8 * pj + 8)
                dve.wait_ge(rt_spread, pj + 1)
                for c in range(KC):
                    dve.tensor_tensor(mg[:, c, t0:L], mg[:, c, t0:L], SUM_POST[:, t0:L], ALU.mult).then_inc(mg_scaled, 1)
                    if c >= 1 and n < NPROJ:
                        low_x(n, c - 1)
                    dve.wait_ge(mg_scaled, 8 * pj + c + 1)
                    dve.tensor_tensor(h[:, c, t0:L], h[:, c, t0:L], mg[:, c, t0:L], ALU.add).then_inc(h_ready, 1)
                if n < NPROJ:
                    low_x(n, KC - 1)
                    dve.memset(acc[:, :], 0.0).then_inc(acc_step, 2)

            def ffn(n, after):
                u0, f0, t0, pj = U_FFN[n], n * FC, FFN_T0[n], X_OF_FFN[n]
                r_of_h(X_OF_FFN[n])

                def tile(m, it=0, banks=None):
                    b = m % 2
                    dve.wait_ge(gu_done, f0 + m + 1 + 4 * it)
                    if f0 + m >= 2:
                        dve.wait_ge(silu_done, f0 + m - 1 + 4 * it)
                    dve.tensor_tensor(gp[:, b, t0:L], bank[banks[0]][:, t0:L], r[:, t0:L], ALU.mult).then_inc(gate_scaled, 1)
                    dve.tensor_tensor(up[:, b, t0:L], bank[banks[1]][:, t0:L], r[:, t0:L], ALU.mult).then_inc(up_scaled, 1)
                    dve.wait_ge(silu_done, f0 + m + 1 + 4 * it)
                    dve.wait_ge(up_scaled, f0 + m + 1 + 4 * it)
                    if f0 + m >= 2:
                        dve.wait_ge(ah_ready, f0 + m - 1 + 4 * it)
                    dve.tensor_tensor(aa[:, b, t0:L], sl[:, b, t0:L], up[:, b, t0:L], ALU.mult).then_inc(a_full, 1)

                def tile_low(m, it=0):
                    b = m % 2
                    dve.wait_ge(ah_ready, f0 + m + 1 + 4 * it)
                    if isinstance(it, int):
                        d, s = al[:, m, t0:L], ah[:, m, t0:L].bitcast(F32)
                    else:
                        d = al[:, bass.ds(4 * it + m, 1), t0:L].rearrange("p a l -> p (a l)")
                        s = ah[:, bass.ds(4 * it + m, 1), t0:L].bitcast(F32).rearrange("p a l -> p (a l)")
                    dve.tensor_tensor(d, aa[:, b, t0:L], s, ALU.subtract).then_inc(a_ready, 1)

                def pair(p, it=0):
                    for j in range(2):
                        tile(2 * p + j, it, ffn_banks(2 * p + j))
                        tile_low(2 * p + j, it)
                    for j in range(2):
                        out_unit = 2 * p + j + 4 - FFN_IN_UNITS
                        low(u0 + 2 * p + j + 4, it, OUT_K[out_unit] if out_unit >= 0 else KC)

                pair(0)
                pair(1)
                with dve.Fori(0, 3) as it:
                    pair(2, it)
                    pair(3, it)
                pair(8)
                pair(9)
                pair(10)

                def next_unit(g, j, it):
                    if g < 3:
                        low(u0 + FFN_IN_UNITS + 4 * g + j + 4, it, OUT_K[j])
                    elif after is not None:
                        low(u0 + FFN_UNITS + j, 0)

                def group(g, it=0):
                    for j in range(3):
                        next_unit(g, j, it)
                    if g < 3:
                        add_squares(pj, 2 * g, it)
                        add_squares(pj, 2 * g + 1, it)
                        next_unit(g, 3, it)

                group(0)
                with dve.Fori(0, 2) as it:
                    group(1, it)
                group(3)
                residual(pj)

            def projection(pj, u0):
                for g in range(4):
                    if g < 3:
                        add_squares(pj, 2 * g)
                        add_squares(pj, 2 * g + 1)
                        low(u0 + g + 4, 0)
                residual(pj)

            def attention():
                def head_root_in(t):
                    dve.wait_ge(q_sum, t + 1)
                    dve.tensor_tensor(hs[:, t], QSUM[0:KT, 0:6].rearrange("p (c g) -> p c g", g=2),
                                      rsq[:, :].rearrange("p (c o) -> p c o", o=1).broadcast_to([KT, 3, 2]), ALU.mult).then_inc(q_step, 1)

                def head_factor(t):
                    dve.wait_ge(q_root, t + 1)
                    dve.reciprocal(hs[:, t], hs[:, t]).then_inc(q_step, 1)
                    dve.wait_ge(q_step, 3 * t + 2)
                    dve.tensor_tensor(hs[:, t], hs[:, t], rc_pre[:, :].rearrange("p (c o) -> p c o", o=1).broadcast_to([KT, 3, 2]),
                                      ALU.mult).then_inc(q_step, 1)

                def times_sin(t):
                    dve.wait_ge(q_rot, t + 1)
                    if t >= 2:
                        dve.wait_ge(q_roped, t - 1)
                    dve.tensor_tensor(pad[:, t % 2, 0:L], ROTB[:, 0:L], sin, ALU.mult).then_inc(q_sin, 1)

                def final(t):
                    dve.wait_ge(q_roped, t + 1)
                    dve.wait_ge(q_spread, t + 1)
                    if t < KT_N:
                        dve.tensor_tensor(kd[:, 2 * t, :], qn[:, t % 2, :], QSCALE[:, 0:L], ALU.mult)
                        dve.tensor_tensor(kd[:, 2 * t + 1, :], qn[:, t % 2, :], QSCALE[:, 0:L], ALU.mult).then_inc(q_final, 1)
                    else:
                        dve.tensor_tensor(qt[:, t - KT_N, :], qn[:, t % 2, :], QSCALE[:, 0:L], ALU.mult).then_inc(q_final, 1)

                rc_of_h(1)
                dve.wait_ge(rc_ready, 2)
                dve.tensor_tensor(rsq[:, :], rc_pre[:, :], rc_pre[:, :], ALU.mult).then_inc(rsq_ready, 1)
                dve.wait_ge(v_done, 1)
                for c in range(3):
                    dve.tensor_scalar(vt[:, c, :], bank[2 + c][0:KT, 0:NKV * HD], rc_pre[:, c:c + 1], None, ALU.mult).then_inc(v_ready, 1)
                dve.wait_ge(v_ready, 3)
                dve.memset(vt[0:OVERLAP, 2, :], 0.0).then_inc(v_ready, 1)
                dve.wait_ge(rsq_ready, 1)
                low(U_QKV + 4, 0)
                low(U_QKV + 5, 0)
                head_root_in(0)
                times_sin(0)
                for t in range(KT_N, QKT):
                    head_factor(t - 2)
                    head_root_in(t - 1)
                    times_sin(t - 1)
                    final(t - 2)
                    if t % 2:
                        low(U_QKV + 2 + (t - KT_N) // 2 + 4, 0)
                head_factor(QKT - 2)
                head_root_in(QKT - 1)
                times_sin(QKT - 1)
                final(QKT - 2)
                head_factor(QKT - 1)
                final(QKT - 1)

                def maximum(a):
                    dve.wait_ge(s_done, a + 1)
                    dve.tensor_reduce(nmax[:, a:a + 1], S_BANK[a % 4][:, 0:L], AX_X, ALU.max, negate=True).then_inc(nmax_ready, 1)

                def normalise(a):
                    dve.wait_ge(p_exp, a + 1)
                    dve.reciprocal(rinv[:, a:a + 1], rsum[:, a:a + 1]).then_inc(p_inv, 1)
                    dve.wait_ge(p_inv, a + 1)
                    dve.tensor_scalar(prow[:, a % 4, :], prow[:, a % 4, :], rinv[:, a:a + 1], None, ALU.mult).then_inc(p_norm, 1)

                def place(a):
                    dve.wait_ge(t_done, a + 1)
                    if a % TILES_S < 2 and a >= 2 * TILES_S:
                        dve.wait_ge(pv_done, 2 * (a // TILES_S) - 2)
                    dst, src = turned_tile(a)
                    dve.tensor_copy(dst, src).then_inc(pt_odd, 1)

                def out_low(pair):
                    dve.wait_ge(oh_ready, pair + 1)
                    dve.tensor_tensor(xl[:, pair, :], bank[4 + pair % 2][:, 0:L], xh[:, pair, :].bitcast(F32), ALU.subtract).then_inc(o_ready, 1)

                tiles = NKV * TILES_S
                maximum(0)
                maximum(1)
                for a in range(tiles):
                    if a + 2 < tiles:
                        maximum(a + 2)
                    normalise(a)
                    if a >= 1 and a % 2 == 0:
                        place(a - 1)
                    j, t = divmod(a - 3, TILES_S)
                    if a >= 3 and t in (4, 8):
                        out_low(2 * j + (t == 8))
                place(tiles - 1)
                out_low(2 * NKV - 1)

            def recurrent():
                r_of_h(4)
                for j, what in enumerate(REC_ORDER):
                    n, u = int(what[1]), U_REC + j
                    b = n % 2
                    if what[0] == "x":
                        for i in range(2):
                            m = 2 * n + i
                            dve.wait_ge(xr_done, m + 1)
                            if n:
                                dve.wait_ge(conv_step, 3 * m - 3)
                                dve.wait_ge(conv0, m - 1)
                            dve.tensor_tensor(pad[:, i, CONVL:CONVL + L], bank[i][:, 0:L], r[:, :], ALU.mult).then_inc(xr_scaled, 1)
                        for i in range(2):
                            m = 2 * n + i
                            dve.wait_ge(conv0, m + 1)
                            for tap in range(1, CONVW):
                                if tap > 1:
                                    dve.wait_ge(conv_step, 3 * m + tap - 1)
                                v = V_CONVW + tap * KC + m
                                dve.scalar_tensor_tensor(xc[:, b, i, :], pad[:, i, tap:tap + L], vec_b[:, v:v + 1], xc[:, b, i, :],
                                                         ALU.mult, ALU.add).then_inc(conv_step, 1)
                        low(u + 4, 0)
                    elif what[0] == "g":
                        dve.wait_ge(tanh_done, 4 * n + 4)
                        if n >= 2:
                            dve.wait_ge(ysum_done, n - 1)
                        flat = "p d m l -> p (d m l)"
                        fr, fw, fm, fi = (v[:, b].rearrange(flat) for v in (gr, gw, gm, gi))
                        dve.scalar_tensor_tensor(fm, fw, 1.0, fr, ALU.add, ALU.mult).then_inc(rec_step, 1)
                        dve.wait_ge(rec_step, 3 * n + 1)
                        dve.tensor_scalar(fr, fm, -1.0, 1.0, ALU.mult, ALU.add).then_inc(rec_step, 1)
                        dve.scalar_tensor_tensor(fw, fm, 2.0, fm, ALU.subtract, ALU.mult).then_inc(rec_step, 1)
                        low(u + 4, 0)
                        dve.wait_ge(root_done, n + 1)
                        dve.wait_ge(ix_done, 2 * n + 2)
                        dve.tensor_tensor(fi, fi, fw, ALU.mult).then_inc(b_done, 1)
                        dve.wait_ge(b_done, n + 1)
                        for d in range(2):
                            for i in range(2):
                                a_, b_, o_ = gr[:, b, d, i, :], gi[:, b, d, i, :], gm[:, b, d, i, :]
                                if d:
                                    a_, b_, o_ = a_[:, ::-1], b_[:, ::-1], o_[:, ::-1]
                                dve.tensor_tensor_scan(o_, a_, b_, 0.0, ALU.mult, ALU.add).then_inc(scan_done, 1)
                    else:
                        for i in range(2):
                            m = 2 * n + i
                            dve.wait_ge(e_done, m + 1)
                            dve.tensor_tensor(mg[:, m, PROJ_T0[4]:L], bank[2 + i][:, PROJ_T0[4]:L], r[:, PROJ_T0[4]:L], ALU.mult).then_inc(e_scaled, 1)
                        low(u + 4, 0)
                for n in range(NB):
                    dve.wait_ge(yh_ready, n + 1)
                    s = slice(2 * n, 2 * n + 2)
                    t = slice(PROJ_T0[4], L)
                    dve.tensor_tensor(xl[:, s, t], ys[:, s, t], xh[:, s, t].bitcast(F32), ALU.subtract).then_inc(y_ready, 1)

            dve.memset(warm[:, :], 1.0).then_inc(warm_set, 1)
            dve.memset(acc[:, :], 0.0).then_inc(acc_step, 2)
            dve.memset(pad[:, :, :], 0.0).then_inc(pad_zero, 1)
            dve.wait_ge(vecs_t, 1)
            dve.tensor_copy(vec_a[:, :], bank[4][:, 0:96]).then_inc(vec_ready, 1)
            dve.tensor_scalar(vec_h[:, :], bank[4][:, 0:96], 0.5, None, ALU.mult).then_inc(vec_ready, 1)
            dve.tensor_copy(vec_b[:, :], bank[4][:, 96:96 + VB]).then_inc(vec_ready, 1)
            dve.wait_ge(vec_ready, 3)
            for c in range(KC):
                dve.wait_ge(x_trans, c + 1)
                dve.tensor_copy(h[:, c, :], bank[4 + c % 4][:, 0:L]).then_inc(h_ready, 1)
                if c >= 1:
                    low_x(0, c - 1)
            low_x(0, KC - 1)
            for u in range(WEIGHT_SLOTS):
                low(u, 0)

            steps = [0]

            def link(ins):
                steps[0] += 1
                ins.then_inc(lam_v, 1)
                dve.wait_ge(lam_v, steps[0])

            e, w, z, zz, p, m0 = (small[:, i, :] for i in (1, 2, 3, 4, 5, 6))
            dve.wait_ge(lam_a, 2)
            link(dve.tensor_scalar(w, e, 2.0, None, ALU.add))
            link(dve.reciprocal(w, w))
            link(dve.tensor_tensor(z, e, w, ALU.mult))
            link(dve.tensor_tensor(zz, z, z, ALU.mult))
            link(dve.tensor_scalar(p, zz, 1.0 / 15, None, ALU.mult))
            for k in (13, 11, 9, 7, 5, 3):
                link(dve.scalar_tensor_tensor(p, p, 1.0 / k, zz, ALU.add, ALU.mult))
            link(dve.scalar_tensor_tensor(p, p, 1.0, z, ALU.add, ALU.mult))
            link(dve.tensor_scalar(m0, vec_b[:, V_LAM:V_QG], -1.0, 0.0, ALU.mult, ALU.max))
            link(dve.scalar_tensor_tensor(m0, p, 2.0, m0, ALU.mult, ALU.add))
            link(dve.tensor_scalar(c4[:, :, :].rearrange("p d c -> p (d c)"), m0, 4.0, None, ALU.mult))
            link(dve.tensor_scalar(c8[:, :, :].rearrange("p d c -> p (d c)"), m0, -8.0, None, ALU.mult))
            link(dve.tensor_scalar(qg[:, 0:1], vec_b[:, V_QG:V_QG + 1], HD ** -0.5, None, ALU.mult))
            link(dve.tensor_copy(qg[:, 1:2], vec_b[:, V_KG:V_KG + 1]))

            ffn(0, True)
            low(U_FFN[0] + FFN_UNITS + 3, 0)
            attention()
            projection(1, U_WO)
            low(U_WO + 3 + 4, 0)
            ffn(1, True)
            low(U_FFN[1] + FFN_UNITS + 3, 0)
            ffn(2, True)
            low(U_FFN[2] + FFN_UNITS + 3, 0)
            dve.memset(pad[:, :, 0:CONVL], 0.0).then_inc(pad_zero, 1)
            dve.memset(pad[:, :, CONVL + L:], 0.0).then_inc(pad_zero, 1)
            recurrent()
            projection(4, U_ROUT)
            low(U_ROUT + 3 + 4, 0)
            ffn(3, None)
            for i in range(2):
                dve.wait_ge(out_t, 2 * i + 1)
                dve.tensor_copy(tok_out[:, 0, 512 * i:512 * i + 512], bank[i][:, :]).then_inc(out_copied[0], 1)

        @block.gpsimd
        def _(pool):
            def sum_squares(n):
                t0 = PROJ_T0[n - 1] if n else 0
                if n:
                    pool.wait_ge(pre_sum, n)
                for c in range(KC):
                    pool.wait_ge(hsq_ready, 8 * n + c + 1)
                    if c == 0:
                        pool.tensor_copy(hacc[:, t0:L], sqh[:, 0, t0:L]).then_inc(hacc_step, 1)
                    else:
                        pool.wait_ge(hacc_step, 8 * n + c)
                        pool.tensor_tensor(hacc[:, t0:L], hacc[:, t0:L], sqh[:, c % 2, t0:L], ALU.add).then_inc(hacc_step, 1)

            def rotary():
                def times_cos(t):
                    pool.wait_ge(q_gained, t + 1)
                    if t >= 2:
                        pool.wait_ge(q_roped, t - 1)
                    pool.tensor_tensor(qc[:, t % 2, :], qp[:, t % 2, :], cos, ALU.mult).then_inc(q_cos, 1)

                def roped(t):
                    pool.wait_ge(q_sin, t + 1)
                    pool.wait_ge(q_cos, t + 1)
                    if t >= 2:
                        pool.wait_ge(q_final, t - 1)
                    pool.tensor_tensor(qn[:, t % 2, :], qc[:, t % 2, :], pad[:, t % 2, 0:L], ALU.add).then_inc(q_roped, 1)

                pool.wait_ge(s_rope, 16)
                times_cos(0)
                for t in range(1, QKT):
                    times_cos(t)
                    roped(t - 1)
                    if t == KT_N + 1:
                        pool.wait_ge(q_final, KT_N)
                        pool.dma_start(kd[HD:P, 0:NKV:2, :], kd[0:HD, 0:NKV:2, :]).then_inc(k_dup, 16)
                        pool.dma_start(kd[0:HD, 1:NKV:2, :], kd[HD:P, 1:NKV:2, :]).then_inc(k_dup, 16)
                roped(QKT - 1)

            def recurrent():
                for j, what in enumerate(REC_ORDER):
                    n = int(what[1])
                    b = n % 2
                    if what[0] == "x":
                        for i in range(2):
                            pool.wait_ge(xch_ready, 2 * n + i + 1)
                            pool.tensor_tensor(xcl[:, b, i, :], xc[:, b, i, :], xch[:, b, i, :].bitcast(F32), ALU.subtract).then_inc(xcl_ready, 1)
                    elif what[0] == "g":
                        pool.wait_ge(sig_done, 8 * n + 8)
                        for d in range(2):
                            pool.tensor_tensor(gi[:, b, d], gi[:, b, d], xc[:, b], ALU.mult).then_inc(ix_done, 1)
                        if n:
                            y_sum(n - 1)
                    elif n == 0:
                        y_sum(NB - 1)
                for n in range(NB):
                    pool.wait_ge(gelu_done, n + 1)
                    pool.wait_ge(ysum_done, n + 1)
                    s = slice(2 * n, 2 * n + 2)
                    t = slice(PROJ_T0[4], L)
                    pool.tensor_tensor(ys[:, s, t], ys[:, s, t], mg[:, s, t], ALU.mult).then_inc(y_full, 1)

            def y_sum(n):
                pool.wait_ge(scan_done, 4 * n + 4)
                pool.tensor_tensor(ys[:, 2 * n:2 * n + 2, :], gm[:, n % 2, 0], gm[:, n % 2, 1], ALU.add).then_inc(ysum_done, 1)

            sum_squares(0)
            sum_squares(1)
            rotary()
            sum_squares(2)
            sum_squares(3)
            sum_squares(4)
            recurrent()
            sum_squares(5)


_INS = ["x", "meta_tokens", "norm_gains", "ffn_w_in", "ffn_w_out", "attn_w_qkv", "attn_q_gain", "attn_k_gain",
        "attn_w_o", "rec_w_in", "rec_conv_w", "rec_conv_b", "rec_gate_w", "rec_gate_b", "rec_lambda", "rec_w_out"]
_LAYERED = _INS[5:]
_OUT = (1, SEQ, D)


def kernel(**inputs):
    import concourse.bacc as _bacc
    from concourse.bass_utils import run_bass_kernel_spmd as _run

    nc = _bacc.Bacc("TRN2", target_bir_lowering=False, num_devices=1)
    arrays, args = {}, []
    for name in _INS:
        a = np.ascontiguousarray(inputs[name])
        arrays[f"in_{name}"] = a
        ap = nc.dram_tensor(f"in_{name}", a.shape, mybir.dt.from_np(a.dtype), kind="ExternalInput").ap()
        args.append(ap[0] if name == "x" or name in _LAYERED else ap)
    arrays["in_consts"] = shape_constants()
    args.append(nc.dram_tensor("in_consts", (P, C_N), F32, kind="ExternalInput").ap())
    out = nc.dram_tensor("out_0", _OUT, F32, kind="ExternalOutput").ap()
    build(nc, *args, out[0])
    r = _run(nc, [arrays], core_ids=[0])
    return r.results[0]["out_0"]
```

```python
from contextlib import ExitStack

import numpy as np

import concourse.bass as bass
from concourse import mybir

ALU = mybir.AluOpType
ACT = mybir.ActivationFunctionType
F32 = mybir.dt.float32
F32R = mybir.dt.float32r
AX_X = mybir.AxisListType.X

P = 128
D = 1024
KC = D // P
SEQ = 256
META = 16
L = SEQ + META
FF = 2816
FC = FF // P
HD = 64
NKV = 4
GROUP = 4
QT_N = D // P
KT_N = NKV * HD // P
QKT = KT_N + QT_N
CONVW = 4
CONVL = 2
NB = 4
GRID_W = 64
THETA = 10000.0
EPS = 1e-6
WEIGHT_SLOTS = 4
UNIT_TILES = 16
OUT_K = (6, 6, 5, 5)
TOK = [(0, P), (P, P), (2 * P, L - 2 * P)]
KT = 96
KTOK = [0, KT, L - KT]
OVERLAP = 2 * KT - KTOK[2]

FFN_IN_UNITS = FC
FFN_OUT_UNITS = 4 * len(OUT_K)
FFN_UNITS = FFN_IN_UNITS + FFN_OUT_UNITS
U_QKV = FFN_UNITS
U_WO = U_QKV + 6
U_FFN = [0, U_WO + 4, U_WO + 4 + FFN_UNITS, 0]
U_REC = U_FFN[2] + FFN_UNITS
REC_ORDER = ["x0", "x1", "e0", "g0", "g1", "x2", "x3", "e1", "g2", "g3", "e2", "e3"]
U_ROUT = U_REC + len(REC_ORDER)
U_FFN[3] = U_ROUT + 4
UNITS = U_FFN[3] + FFN_UNITS

GAIN = lambda layer, i, c: (layer * 6 + i) * KC + c
V_CONVW, V_CONVB, V_GATEB, V_LAM, V_QG, V_KG = 0, 32, 40, 72, 88, 89
VB = 90
C_ID, C_ONES, C_BONES, C_ROT, C_COS, C_SIN = 0, P, P + 1, P + 3, 2 * P + 3, 2 * P + 3 + L
C_N = 2 * P + 3 + 2 * L

NPROJ = 6
TILES_S = 9


def shape_constants():
    c = np.zeros((P, C_N), np.float32)
    c[:, C_ID:C_ID + P] = np.eye(P)
    half = HD // 2
    for m in range(P):
        if m % HD < half:
            c[m + half, C_ROT + m] = -1.0
        else:
            c[m - half, C_ROT + m] = 1.0
    for half_tile in range(2):
        c[half_tile * HD:(half_tile + 1) * HD, C_BONES + half_tile] = 1.0 / HD
    c[:, C_ONES] = 1.0 / D
    inv = (np.float32(1.0) / (np.float32(THETA) ** (np.arange(0, half, 2, dtype=np.float32) / np.float32(half)))).astype(np.float32)
    pos = np.arange(SEQ)
    zeros = np.zeros(META, np.float32)
    row = np.concatenate([zeros, (pos // GRID_W).astype(np.float32)])
    col = np.concatenate([zeros, (pos % GRID_W).astype(np.float32)])
    theta = np.concatenate([row[:, None] * inv, col[:, None] * inv], axis=-1).astype(np.float32)
    cos, sin = np.cos(theta).T, np.sin(theta).T
    for b in range(P // half):
        c[b * half:(b + 1) * half, C_COS:C_COS + L] = cos
        c[b * half:(b + 1) * half, C_SIN:C_SIN + L] = sin
    return c


def build(nc, x, meta, gains, ffn_in, ffn_out, w_qkv, q_gain, k_gain, w_o, rec_in, conv_w, conv_b,
          gate_w, gate_b, lam, rec_out, consts, out):
    ctx = ExitStack()
    with ctx:
        def sb(name, shape, dt=F32):
            return ctx.enter_context(nc.sbuf_tensor(name, shape, dt))

        def sem(name):
            return ctx.enter_context(nc.semaphore(name))

        h = sb("h", [P, KC, L])
        xh, xl = sb("xh", [P, KC, L], F32R), sb("xl", [P, KC, L], F32R)
        raw = sb("raw", [P, WEIGHT_SLOTS, UNIT_TILES * P])
        wh = sb("wh", [P, WEIGHT_SLOTS, UNIT_TILES * P], F32R)
        wl = sb("wl", [P, WEIGHT_SLOTS, UNIT_TILES * P], F32R)
        mg = sb("mg", [P, KC, L])
        cst = sb("cst", [P, C_N])
        vec_a = sb("vec_a", [P, 96])
        vec_h = sb("vec_h", [P, 96])
        vec_b = sb("vec_b", [P, VB])
        tmp = sb("tmp", [P, 8, L])
        pad = sb("pad", [P, 2, L + 4])
        sqb = sb("sqb", [P, 2, L])
        sqh = sb("sqh", [P, 2, L])
        acc = sb("acc", [P, L])
        hacc = sb("hacc", [P, L])
        r = sb("r", [P, L])
        rc_pre = sb("rc_pre", [KT, 3])
        rc_post = sb("rc_post", [KT, 3])
        rsq = sb("rsq", [KT, 3])
        hs = sb("hs", [KT, QKT, 3, 2])
        warm = sb("warm", [1, 2])
        small = sb("small", [P, 8, 16])
        c4 = sb("c4", [P, 2, KC])
        c8 = sb("c8", [P, 2, KC])
        qg = sb("qg", [P, 2])
        nmax = sb("nmax", [P, NKV * TILES_S])
        rsum = sb("rsum", [P, NKV * TILES_S])
        rinv = sb("rinv", [P, NKV * TILES_S])
        prow = sb("prow", [P, 4, L])

        with nc.sbuf_tensor("ah", [P, FC, L], F32R) as ah, nc.sbuf_tensor("al", [P, FC, L], F32R) as al:
            pass
        with nc.sbuf_tensor("tok_in", [P, 3, D], F32) as tok_in, nc.sbuf_tensor("vrow", [96, 2, P], F32) as vrow, \
                nc.sbuf_tensor("tok_out", [P, 2, D], F32) as tok_out:
            pass
        with nc.sbuf_tensor("qt", [P, QT_N, L], F32) as qt, nc.sbuf_tensor("kd", [P, NKV, L], F32) as kd, \
                nc.sbuf_tensor("vt", [KT, 3, NKV * HD], F32) as vt, nc.sbuf_tensor("pt", [KT, 2, 3, GROUP, L], F32) as pt:
            pass
        with nc.sbuf_tensor("xch", [P, 2, 2, L], F32R) as xch, nc.sbuf_tensor("xcl", [P, 2, 2, L], F32R) as xcl, \
                nc.sbuf_tensor("xc", [P, 2, 2, L], F32) as xc, nc.sbuf_tensor("gr", [P, 2, 2, 2, L], F32) as gr, \
                nc.sbuf_tensor("gi", [P, 2, 2, 2, L], F32) as gi, nc.sbuf_tensor("gw", [P, 2, 2, 2, L], F32) as gw, \
                nc.sbuf_tensor("gm", [P, 2, 2, 2, L], F32) as gm:
            pass
        ctx.enter_context(nc.sbuf_tensor("region", [P, 2 * FC * L], F32))

        bank = [ctx.enter_context(nc.psum_tensor(f"bank{i}", [P, 512], F32)) for i in range(8)]
        SUM_POST, SUM_PRE = bank[6], bank[7]
        SC = 384
        QSUM, ROTB, QSCALE = bank[5], bank[6], bank[7]
        S_BANK = (bank[0], bank[1], bank[6], bank[7])

        ident = cst[:, C_ID:C_ID + P]
        rotm = cst[:, C_ROT:C_ROT + P]
        head_mean_w = cst[:, C_BONES:C_BONES + 2]
        mean_w = cst[:, C_ONES:C_ONES + 1]
        cos = cst[:, C_COS:C_COS + L]
        sin = cst[:, C_SIN:C_SIN + L]
        qp, qs, qn, qc = tmp[:, 0:2, :], tmp[:, 2:4, :], tmp[:, 4:6, :], tmp[:, 6:8, :]
        gp, sl, up, aa = qp, qs, qn, qc
        ys = tmp

        s_in, s_vec = sem("gains_landed"), sem("vectors_landed")
        table_loaded, warm_set = sem("table_loaded"), sem("warm_set")
        s_rope = sem("rotary_tables_landed")
        s_xin = sem("tokens_landed")
        landed = [sem(f"landed{i}") for i in range(WEIGHT_SLOTS)]
        wh_ready, w_ready, out_unit_used = sem("wh_ready"), sem("w_ready"), sem("out_unit_used")
        vecs_t, x_trans = sem("vecs_transposed"), sem("x_transposed")
        lam_a, lam_v = sem("lambda_act"), sem("lambda_dve")
        h_ready, xh_ready, x_ready = sem("h_ready"), sem("xh_ready"), sem("x_ready")
        hsq_ready, hacc_step, pre_sum, pre_root, rc_ready, r_spread, r_ready = (sem(n) for n in (
            "hsq_ready", "hacc_step", "pre_sum", "pre_root", "rc_ready", "r_spread", "r_ready"))
        gu_done, gate_scaled, silu_done, up_scaled, a_full, ah_ready, a_ready = (sem(n) for n in (
            "gu_done", "gate_scaled", "silu_done", "up_scaled", "a_full", "ah_ready", "a_ready"))
        proj_done, sq_ready, mg_ready, acc_step, post_sum, post_root, rt_ready, rt_spread, mg_scaled = (sem(n) for n in (
            "proj_done", "sq_ready", "mg_ready", "acc_step", "post_sum", "post_root", "rt_ready", "rt_spread", "mg_scaled"))
        qk_done, q_squared, q_gained, q_sum, q_step, q_root, q_rot, q_cos, q_sin, q_roped, q_spread, q_final = (sem(n) for n in (
            "qk_done", "q_squared", "q_gained", "q_sum", "q_step", "q_root", "q_rot", "q_cos", "q_sin", "q_roped", "q_spread", "q_final"))
        v_done, rsq_ready, v_ready, k_dup = (sem(n) for n in ("v_done", "rsq_ready", "v_ready", "k_dup"))
        s_done, nmax_ready, p_exp, p_inv, p_norm, t_done, pt_ready, pv_done, oh_ready, o_ready = (sem(n) for n in (
            "s_done", "nmax_ready", "p_exp", "p_inv", "p_norm", "t_done", "pt_ready", "pv_done", "oh_ready", "o_ready"))
        xr_done, pad_zero, xr_scaled, conv_step, xch_ready, xcl_ready = (sem(n) for n in (
            "xr_done", "pad_zero", "xr_scaled", "conv_step", "xch_ready", "xcl_ready"))
        g_done, sig_done, exp_done, tanh_done, rec_step, root_done, ix_done, b_done, scan_done, ysum_done = (sem(n) for n in (
            "g_done", "sig_done", "exp_done", "tanh_done", "rec_step", "root_done", "ix_done", "b_done", "scan_done", "ysum_done"))
        e_done, e_scaled, gelu_done, y_full, yh_ready, y_ready = (sem(n) for n in (
            "e_done", "e_scaled", "gelu_done", "y_full", "yh_ready", "y_ready"))
        out_t, s_out = sem("out_transposed"), sem("out_stored")
        out_copied = [sem("out_copied0"), sem("out_copied1")]
        vec_ready = sem("vec_ready")
        last_b_done = sem("last_b_done")

        landed_at, count = [], [0] * WEIGHT_SLOTS
        for u in range(UNITS):
            gates = U_REC <= u < U_ROUT and REC_ORDER[u - U_REC][0] == "g"
            count[u % WEIGHT_SLOTS] += 64 if gates else 16
            landed_at.append(count[u % WEIGHT_SLOTS])

        def slot(u):
            return u % WEIGHT_SLOTS

        def y_part(high, c):
            if c < 4:
                return (xch if high else xcl)[:, c // 2, c % 2, :]
            return (xh if high else xl)[:, c, :]

        FFN_OF_PROJ = {0: 0, 2: 1, 3: 2, 5: 3}
        X_OF_FFN = (0, 2, 3, 5)
        PRE_GAIN = [(0, 0), (0, 2), (0, 4), (1, 0), (1, 2), (1, 4)]
        POST_GAIN = [(0, 1), (0, 3), (0, 5), (1, 1), (1, 3), (1, 5)]
        PROJ_BANKS = {n: ((4, 5), (0, 1), (0, 1), (2, 3)) if n in FFN_OF_PROJ else ((0, 1), (2, 3), (4, 5), (0, 1)) for n in range(NPROJ)}
        PROJ_T0 = [META if n >= 4 else 0 for n in range(NPROJ)]
        FFN_T0 = [0, 0, 0, META]
        ACC = 8

        def turned_tile(a):
            j, t = divmod(a, TILES_S)
            src = bank[2 + a % 2][0:KT, 0:3 * P]
            if t == 0:
                return pt[:, j % 2, :, :, 2 * P:L], src.rearrange("p (c g q) -> p c g q", c=3, g=GROUP)[:, :, :, 16:32]
            g, half = divmod(t - 1, 2)
            return pt[:, j % 2, :, g, P * half:P * half + P], src.rearrange("p (c q) -> p c q", c=3)

        def ffn_banks(m):
            return {0: (0, 1), 1: (2, 3), 2: (4, 5)}.get(m, (2, 3) if m % 2 == 0 else (0, 1))

        REC_BANKS = {"x0": bank[0:2], "x1": bank[2:4], "e0": bank[4:6], "x2": bank[2:4], "x3": bank[4:6],
                     "e1": bank[2:4], "e2": bank[4:6], "e3": bank[2:4]}
        GATE_BANKS = (bank[0], bank[1], bank[6], bank[7])

        block = ctx.enter_context(nc.Block())

        @block.sync
        def _(sp):
            def load(u, it, kn, src):
                if u >= WEIGHT_SLOTS:
                    sp.wait_ge(w_ready, u - WEIGHT_SLOTS + 1 + WEIGHT_SLOTS * it)
                dst = raw[:, slot(u), 0:kn * 256].rearrange("p (k c) -> p k c", k=kn)
                sp.dma_start(dst, src).then_inc(landed[slot(u)], 16)

            def ffn(n):
                u0 = U_FFN[n]
                vin = ffn_in[n // 2, n % 2].rearrange("(k p) c -> p k c", p=P)
                vout = ffn_out[n // 2, n % 2].rearrange("(k p) c -> p k c", p=P)

                def pair(u, it, col):
                    load(u, it, KC, vin[:, :, bass.ds(col, 256)])
                    load(u + 1, it, KC, vin[:, :, bass.ds(col + FF, 256)])

                pair(u0, 0, 0)
                pair(u0 + 2, 0, 256)
                if n == 0:
                    vectors()
                with sp.Fori(0, 4) as it:
                    pair(u0 + 4, it, 512 * it + 512)
                    pair(u0 + 6, it, 512 * it + 768)
                pair(u0 + 20, 0, 2560)
                with sp.Fori(0, 4) as it:
                    k0 = 0
                    for j, kn in enumerate(OUT_K):
                        load(u0 + FFN_IN_UNITS + j, it, kn, vout[:, k0:k0 + kn, bass.ds(256 * it, 256)])
                        k0 += kn

            def vectors():
                sp.dma_start(vrow[V_CONVW:V_CONVB, 1, :], conv_w.rearrange("j (c p) -> (j c) p", p=P)).then_inc(s_vec, 16)
                sp.dma_start(vrow[V_CONVB:V_GATEB, 1, :], conv_b.rearrange("(c p) -> c p", p=P)).then_inc(s_vec, 16)
                sp.dma_start(vrow[V_GATEB:V_LAM, 1, :], gate_b.rearrange("d g (c p) -> (d g c) p", p=P)).then_inc(s_vec, 16)
                sp.dma_start(vrow[V_LAM:V_QG, 1, :], lam.rearrange("d (c p) -> (d c) p", p=P)).then_inc(s_vec, 16)
                for row, gain in ((V_QG, q_gain), (V_KG, k_gain)):
                    sp.dma_start(vrow[row:row + 1, 1, :].rearrange("a (n p) -> a n p", n=2),
                                 gain.rearrange("(a b p) -> a b p", a=1, b=1).broadcast_to([1, 2, HD])).then_inc(s_vec, 16)
                sp.dma_start(cst[:, C_ROT:C_N], consts[:, C_ROT:C_N]).then_inc(s_rope, 16)

            sp.dma_start(tok_in[META:P, 0, :], x[0:P - META, :]).then_inc(s_xin, 16)
            sp.dma_start(tok_in[:, 1, :], x[P - META:2 * P - META, :]).then_inc(s_xin, 16)
            sp.dma_start(vrow[:, 0, :], gains.rearrange("l i (c p) -> (l i c) p", p=P)).then_inc(s_in, 16)
            ffn(0)
            v = w_qkv.rearrange("(k p) c -> p k c", p=P)
            for j, c0 in enumerate((1024, 1280, 0, 256, 512, 768)):
                load(U_QKV + j, 0, KC, v[:, :, c0:c0 + 256])
            v = w_o.rearrange("(k p) c -> p k c", p=P)
            for j in range(4):
                load(U_WO + j, 0, KC, v[:, :, 256 * j:256 * j + 256])
            ffn(1)
            ffn(2)
            v = rec_in.rearrange("(k p) c -> p k c", p=P)
            for j, what in enumerate(REC_ORDER):
                n, u = int(what[1]), U_REC + j
                if what[0] == "g":
                    sp.wait_ge(w_ready, u - WEIGHT_SLOTS + 1)
                    dst = raw[:, slot(u), :].rearrange("p (g k c) -> p g k c", g=4, k=2)
                    for g in range(4):
                        sp.dma_start(dst[:, g], gate_w[g // 2, g % 2, n].rearrange("(k p) c -> p k c", p=P)).then_inc(landed[slot(u)], 16)
                else:
                    c0 = (D if what[0] == "x" else 0) + 256 * n
                    load(u, 0, KC, v[:, :, c0:c0 + 256])
            v = rec_out.rearrange("(k p) c -> p k c", p=P)
            for j in range(4):
                load(U_ROUT + j, 0, KC, v[:, :, 256 * j:256 * j + 256])
            ffn(3)
            for half in range(2):
                cols = slice(D // 2 * half, D // 2 * (half + 1))
                for t in range(2):
                    sp.wait_ge(out_copied[t], half + 1)
                    sp.dma_start(out[t * P:(t + 1) * P, cols], tok_out[:, t, cols]).then_inc(s_out, 16)
            sp.wait_ge(s_out, 16 * 4)

        @block.tensor
        def _(pe):
            def product(dst, u, tile, mh, ml, first, last):
                a = wh[:, slot(u), tile * P:(tile + 1) * P]
                b = wl[:, slot(u), tile * P:(tile + 1) * P]
                pe.matmul(dst, b, mh, start=first, stop=False)
                pe.matmul(dst, a, ml, start=False, stop=False)
                return pe.matmul(dst, a, mh, start=False, stop=last)

            def keep_warm(products, dst):
                for _ in range(products):
                    pe.matmul(dst[:, 0:P], ident, ident, start=True, stop=True)

            def chunk(tiles, k, norm, t0):
                pe.wait_ge(xh_ready, KC * norm + k + 1)
                for dst, u, tile in tiles:
                    a, b = (v[:, slot(u), tile * P:(tile + 1) * P] for v in (wh, wl))
                    pe.matmul(dst, b, xh[:, k, t0:L], start=k == 0, stop=False)
                    pe.matmul(dst, a, xh[:, k, t0:L], start=False, stop=False)
                pe.wait_ge(x_ready, KC * norm + k + 1)
                return [pe.matmul(dst, wh[:, slot(u), tile * P:(tile + 1) * P], xl[:, k, t0:L], start=False, stop=k == KC - 1)
                        for dst, u, tile in tiles]

            def spread(dst, cols, heads=1):
                size = P // heads
                for c, a in enumerate(KTOK):
                    for g in range(heads):
                        w = cols[:, heads * c + g:heads * c + g + 1].broadcast_to([KT, size])
                        last = pe.matmul(dst[g * size:(g + 1) * size, a:a + KT], w, ident[0:KT, 0:KT], start=True, stop=True)
                return last

            def mean_of_h(n):
                pe.wait_ge(hacc_step, 8 * n + 8)
                for c, a in enumerate(KTOK):
                    last = pe.matmul(SUM_PRE[0:KT, SC + c:SC + c + 1], hacc[:, a:a + KT], mean_w, start=True, stop=True)
                last.then_inc(pre_sum, 1)

            def spread_r(n):
                pe.wait_ge(rc_ready, n + 1)
                spread(SUM_PRE, rc_pre).then_inc(r_spread, 1)

            def ffn(n):
                u0, f0, x0, t0, pj = U_FFN[n], n * FC, X_OF_FFN[n] * KC, FFN_T0[n], X_OF_FFN[n]

                tiles = [[(bank[ffn_banks(m)[part]][:, t0:L], u0 + part, m) for m in range(2)] for part in range(2)]
                for step in ([tiles[0] + tiles[1]] if n else tiles):
                    pe.wait_ge(w_ready, step[-1][1] + 1)
                    for k in range(KC):
                        last = chunk([(dst, u, 2 * k + m) for dst, u, m in step], k, X_OF_FFN[n], t0)
                for m in range(2):
                    last[-2 + m].then_inc(gu_done, 1)
                mean_of_h(X_OF_FFN[n])
                if n == 0:
                    pe.wait_ge(s_vec, 16 * 6)
                    pe.transpose(bank[6][:, 0:VB], vrow[0:VB, 1, :], ident[0:VB, 0:VB]).then_inc(vecs_t, 1)

                def mtile(u, it, m, banks, f, before):
                    if before is not None:
                        pe.wait_ge(up_scaled, before + 1 + WEIGHT_SLOTS * it)
                    for part in range(2):
                        if m == 0:
                            pe.wait_ge(w_ready, u + 1 + part + WEIGHT_SLOTS * it)
                        for k in range(KC):
                            last = product(bank[banks[part]][:, t0:L], u + part, 2 * k + m,
                                           xh[:, k, t0:L], xl[:, k, t0:L], k == 0, k == KC - 1)
                            if f == f0 + 2 and part == 0 and k == 3:
                                spread_r(X_OF_FFN[n])
                    last.then_inc(gu_done, 1)

                def pair(p, it):
                    for j in range(2):
                        m = 2 * p + j
                        before = {2: None, 3: f0, 4: f0 + 1}.get(m, f0 + m - 2)
                        mtile(u0 + 2 * p, it, j, ffn_banks(m), f0 + m, before)

                pair(1, 0)
                pair(2, 0)
                pair(3, 0)
                with pe.Fori(0, 3) as it:
                    pair(4, it)
                    pair(5, it)
                pair(10, 0)

                v0 = u0 + FFN_IN_UNITS

                def group(g, it, banks, check):
                    k0 = 0
                    for j, kn in enumerate(OUT_K):
                        pe.wait_ge(w_ready, v0 + 4 * g + j + 1 + WEIGHT_SLOTS * it)
                        for m in range(2):
                            if check and j == 0:
                                pe.wait_ge(mg_ready, 8 * pj + 2 * g + m - 1 + 2 * it)
                            for k in range(kn):
                                if g == 0 and m == 0:
                                    pe.wait_ge(a_ready, f0 + k0 + k + 1)
                                last = product(bank[banks[m]][:, t0:L], v0 + 4 * g + j, 2 * k + m,
                                               ah[:, k0 + k, t0:L], al[:, k0 + k, t0:L],
                                               k0 + k == 0, k0 + k == FC - 1)
                            if j == len(OUT_K) - 1:
                                last.then_inc(proj_done, 1)
                            elif m == 1:
                                last.then_inc(out_unit_used, 1)
                        k0 += kn

                group(0, 0, PROJ_BANKS[pj][0], False)
                with pe.Fori(0, 2) as it:
                    group(1, it, PROJ_BANKS[pj][1], True)
                group(3, 0, PROJ_BANKS[pj][3], False)
                mean_of_projection(pj)

            def mean_of_projection(pj):
                first = True
                for ready, value, squares in ((acc_step, ACC * pj + ACC, acc[:, :]),
                                              (sq_ready, 8 * pj + 7, sqb[:, 0, :]), (sq_ready, 8 * pj + 8, sqb[:, 1, :])):
                    pe.wait_ge(ready, value)
                    for c, a in enumerate(KTOK):
                        last = pe.matmul(SUM_POST[0:KT, SC + c:SC + c + 1], squares[:, a:a + KT], mean_w,
                                         start=first, stop=value == 8 * pj + 8, skip_group_check=True)
                        first = False
                last.then_inc(post_sum, 1)
                keep_warm(3, bank[5])
                pe.wait_ge(rt_ready, pj + 1)
                spread(SUM_POST, rc_post).then_inc(rt_spread, 1)
                keep_warm(6, bank[5])

            def projection(pj, u0, ready, step, part):
                t0 = PROJ_T0[pj]
                for g in range(4):
                    pe.wait_ge(w_ready, u0 + g + 1)
                    order = [(k, m) for k in range(KC) for m in range(2)] if g == 0 else [(k, m) for m in range(2) for k in range(KC)]
                    for k, m in order:
                        if g == 3 and k == 0:
                            pe.wait_ge(mg_ready, 8 * pj + m + 1)
                        if g == 0 and m == 0:
                            if k == 4 and pj == 4:
                                keep_warm(28, bank[6])
                            pe.wait_ge(ready, k // step + 1)
                        last = product(bank[PROJ_BANKS[pj][g][m]][:, t0:L], u0 + g, 2 * k + m,
                                       part(True, k)[:, t0:L], part(False, k)[:, t0:L], k == 0, k == KC - 1)
                        if k == KC - 1:
                            last.then_inc(proj_done, 1)
                mean_of_projection(pj)

            def attention():
                pe.wait_ge(w_ready, U_QKV + 2)
                for k in range(KC):
                    pe.wait_ge(x_ready, KC + k + 1)
                    for m in range(KT_N):
                        last = product(bank[m][:, 0:L], U_QKV, 2 * k + m, xh[:, k, :], xl[:, k, :], k == 0, k == KC - 1)
                        if k == KC - 1:
                            last.then_inc(qk_done, 1)
                    for c, a in enumerate(KTOK):
                        dst = bank[2 + c][0:KT, 0:NKV * HD]
                        wv_h = wh[:, slot(U_QKV + 1), k * 256:(k + 1) * 256]
                        wv_l = wl[:, slot(U_QKV + 1), k * 256:(k + 1) * 256]
                        pe.matmul(dst, xl[:, k, a:a + KT], wv_h, start=k == 0, stop=False)
                        pe.matmul(dst, xh[:, k, a:a + KT], wv_l, start=False, stop=False)
                        last = pe.matmul(dst, xh[:, k, a:a + KT], wv_h, start=False, stop=k == KC - 1)
                last.then_inc(v_done, 1)
                mean_of_h(1)

                def head_means(t):
                    pe.wait_ge(q_squared, t + 1)
                    if t:
                        pe.wait_ge(q_step, 3 * t - 2)
                    for c, a in enumerate(KTOK):
                        last = pe.matmul(QSUM[0:KT, 2 * c:2 * c + 2], qs[:, t % 2, a:a + KT], head_mean_w, start=True, stop=True)
                    last.then_inc(q_sum, 1)

                def rotate(t):
                    pe.wait_ge(q_gained, t + 1)
                    if t:
                        pe.wait_ge(q_sin, t)
                    pe.matmul(ROTB[:, 0:L], rotm, qp[:, t % 2, :], start=True, stop=True).then_inc(q_rot, 1)

                def spread_scale(t):
                    pe.wait_ge(q_step, 3 * t + 3)
                    if t:
                        pe.wait_ge(q_final, t)
                    spread(QSCALE, hs[:, t].rearrange("p c g -> p (c g)"), 2).then_inc(q_spread, 1)

                pe.wait_ge(s_rope, 16)
                for t in range(KT_N, QKT):
                    if t % 2 == 0:
                        pe.wait_ge(w_ready, U_QKV + 2 + (t - KT_N) // 2 + 1)
                    pe.wait_ge(q_gained, t - 1)
                    for k in range(KC):
                        last = product(bank[t % 2][:, 0:L], U_QKV + 2 + (t - KT_N) // 2, 2 * k + t % 2,
                                       xh[:, k, :], xl[:, k, :], k == 0, k == KC - 1)
                        if t == KT_N and k == 3:
                            spread_r(1)
                    last.then_inc(qk_done, 1)
                    if t == KT_N:
                        head_means(0)
                        rotate(0)
                    head_means(t - 1)
                    rotate(t - 1)
                    spread_scale(t - 2)

                def scores(a):
                    j, t = divmod(a, TILES_S)
                    dst = S_BANK[a % 4]
                    if a >= 4:
                        pe.wait_ge(p_exp, a - 3)
                    if t == 0:
                        pe.wait_ge(q_final, KT_N + 2 * j + 2)
                        for g in range(GROUP):
                            o = HD * (g % 2)
                            last = pe.matmul(dst[32 * g:32 * g + 32, 0:L], qt[o:o + HD, 2 * j + g // 2, L - 32:L],
                                             kd[o:o + HD, j, :], start=True, stop=True)
                    else:
                        g, half = divmod(t - 1, 2)
                        o = HD * (g % 2)
                        last = pe.matmul(dst[:, 0:L], qt[o:o + HD, 2 * j + g // 2, P * half:P * half + P],
                                         kd[o:o + HD, j, :], start=True, stop=True)
                    last.then_inc(s_done, 1)

                def turned(a):
                    pe.wait_ge(pt_ready, a + 1)

                def turn(a):
                    pe.wait_ge(p_norm, a + 1)
                    if a >= 2:
                        turned(a - 2)
                    for c, k0 in enumerate(KTOK):
                        last = pe.transpose(bank[2 + a % 2][0:KT, c * P:(c + 1) * P], prow[:, a % 4, k0:k0 + KT], ident)
                    last.then_inc(t_done, 1)

                def weigh(j, g):
                    a, pair = j * TILES_S + 2 * g + 2, 2 * j + g // 2
                    turned(a)
                    turned(a - 1)
                    if g == 0:
                        turned(j * TILES_S)
                    if pair >= 2 and g % 2 == 0:
                        pe.wait_ge(o_ready, pair - 1)
                    o = HD * (g % 2)
                    for c in range(3):
                        last = pe.matmul(bank[4 + pair % 2][o:o + HD, 0:L], vt[:, c, HD * j:HD * j + HD],
                                         pt[:, j % 2, c, g, :], start=c == 0, stop=c == 2)
                    if g % 2:
                        last.then_inc(pv_done, 1)

                head_means(QKT - 1)
                rotate(QKT - 1)
                pe.wait_ge(k_dup, 32)
                pe.wait_ge(q_gained, QKT)
                scores(0)
                scores(1)
                spread_scale(QKT - 2)
                pe.wait_ge(v_ready, 4)
                keep_warm(4, bank[4])
                spread_scale(QKT - 1)
                keep_warm(4, bank[4])
                pe.wait_ge(q_final, QKT)
                tiles = NKV * TILES_S
                scores(2)
                for a in range(tiles):
                    if a + 3 < tiles:
                        scores(a + 3)
                    turn(a)
                    j, t = divmod(a - 1, TILES_S)
                    if a >= 1 and t >= 2 and t % 2 == 0:
                        weigh(j, (t - 2) // 2)
                weigh(NKV - 1, GROUP - 1)

            def recurrent():
                t0 = PROJ_T0[4]
                banks_read = {"x2": (xr_scaled, 4), "x3": (e_scaled, 2), "e1": (xr_scaled, 6), "e2": (xr_scaled, 8), "e3": (e_scaled, 4)}

                pe.wait_ge(w_ready, U_REC + 2)
                for k in range(KC):
                    last = chunk([(REC_BANKS[REC_ORDER[j]][m][:, 0:L], U_REC + j, 2 * k + m) for j in range(2) for m in range(2)],
                                 k, 4, 0)
                for product_done in last:
                    product_done.then_inc(xr_done, 1)
                mean_of_h(4)

                for j, what in enumerate(REC_ORDER[2:], 2):
                    n, u = int(what[1]), U_REC + j
                    if what == "g0":
                        keep_warm(8, bank[6])
                    pe.wait_ge(w_ready, u + 1)
                    if what[0] == "g":
                        pe.wait_ge(xcl_ready, 2 * n + 2)
                        for o in range(8 * n, 8 * n + 8):
                            g, m = o % 8 // 2, o % 2
                            if o >= 4:
                                pe.wait_ge(sig_done, o - 3)
                            for k in range(2):
                                last = product(GATE_BANKS[o % 4][:, 0:L], u, (g * 2 + k) * 2 + m,
                                               xch[:, n % 2, k, :], xcl[:, n % 2, k, :], k == 0, k == 1)
                            last.then_inc(g_done, 1)
                    else:
                        x_part = what[0] == "x"
                        a = 0 if x_part else t0
                        if what in banks_read:
                            pe.wait_ge(*banks_read[what])
                        for m in range(2):
                            for k in range(KC):
                                last = product(REC_BANKS[what][m][:, a:L], u, 2 * k + m,
                                               xh[:, k, a:L], xl[:, k, a:L], k == 0, k == KC - 1)
                                if what == "e0" and m == 0 and k == 2:
                                    spread_r(4)
                            last.then_inc(xr_done if x_part else e_done, 1)

            pe.wait_ge(s_in, 16 * 2)
            pe.transpose(bank[4][:, 0:96], vrow[:, 0, :], ident[0:96, 0:96]).then_inc(vecs_t, 1)
            pe.wait_ge(s_xin, 64)
            for c in range(KC):
                if c >= 4:
                    pe.wait_ge(h_ready, c - 3)
                elif c == 0:
                    pe.wait_ge(vec_ready, 2)
                for t, (a, n) in enumerate(TOK):
                    last = pe.transpose(bank[4 + c % 4][:, a:a + n], tok_in[0:n, t, c * P:(c + 1) * P], ident[0:n, 0:n])
                last.then_inc(x_trans, 1)
            keep_warm(16, bank[0])
            ffn(0)
            attention()
            projection(1, U_WO, o_ready, 1, lambda high, c: (xh if high else xl)[:, c, :])
            ffn(1)
            ffn(2)
            recurrent()
            pe.wait_ge(sig_done, 8 * NB)
            keep_warm(14, bank[6])
            projection(4, U_ROUT, y_ready, 2, y_part)
            ffn(3)
            for c in range(KC):
                pe.wait_ge(h_ready, 6 * KC + c + 1)
                for t in range(2):
                    last = pe.transpose(bank[2 * t + c // 4][:, (c % 4) * P:(c % 4 + 1) * P],
                                        h[:, c, META + t * P:META + (t + 1) * P], ident)
                    if c % 4 == 3:
                        last.then_inc(out_t, 1)

        @block.scalar
        def _(act):
            def high(u, it, kn=KC, freed=None):
                act.wait_ge(landed[slot(u)], landed_at[u] + 16 * it)
                if freed is not None:
                    act.wait_ge(*freed)
                act.activation(wh[:, slot(u), 0:kn * 256], raw[:, slot(u), 0:kn * 256], ACT.Copy).then_inc(wh_ready, 1)

            def x_high(n, c):
                t0 = PROJ_T0[n - 1] if n else 0
                g = GAIN(*PRE_GAIN[n], c)
                act.wait_ge(h_ready, 8 * n + c + 1)
                act.activation(xh[:, c, t0:L], h[:, c, t0:L], ACT.Copy, scale=vec_a[:, g:g + 1]).then_inc(xh_ready, 1)

            def h_square(n, c):
                t0 = PROJ_T0[n - 1] if n else 0
                if 8 * n + c >= 2:
                    act.wait_ge(hacc_step, 8 * n + c - 1)
                act.activation(sqh[:, c % 2, t0:L], h[:, c, t0:L], ACT.Square).then_inc(hsq_ready, 1)

            def make_x(n):
                for c in range(KC):
                    x_high(n, c)
                    h_square(n, c)

            def root_of_h(n):
                act.wait_ge(pre_sum, n + 1)
                act.activation(rc_pre[:, :], SUM_PRE[0:KT, SC:SC + 3], ACT.Sqrt, bias=EPS).then_inc(pre_root, 1)

            def square_tile(pj, m, b, it=0):
                t0 = PROJ_T0[pj]
                gains_of = vec_h if pj in FFN_OF_PROJ else vec_a
                g = GAIN(*POST_GAIN[pj], 0) + m
                act.wait_ge(proj_done, 8 * pj + m + 1 + 2 * it)
                act.wait_ge(acc_step, ACC * pj + m + 1 + 2 * it)
                act.activation(sqb[:, m % 2, t0:L], bank[b][:, t0:L], ACT.Square).then_inc(sq_ready, 1)
                if isinstance(it, int):
                    act.activation(mg[:, m, t0:L], bank[b][:, t0:L], ACT.Copy, scale=gains_of[:, g:g + 1]).then_inc(mg_ready, 1)
                else:
                    act.activation(mg[:, bass.ds(2 * it + m, 1), t0:L].rearrange("p a l -> p (a l)"), bank[b][:, t0:L],
                                   ACT.Copy, scale=gains_of[:, bass.ds(2 * it + g, 1)]).then_inc(mg_ready, 1)

            def root_of_projection(pj):
                act.wait_ge(post_sum, pj + 1)
                act.activation(rc_post[:, :], SUM_POST[0:KT, SC:SC + 3], ACT.Sqrt, bias=EPS).then_inc(post_root, 1)

            loads = [0]

            def load_table(func):
                if loads[0]:
                    act.wait_ge(table_loaded, loads[0])
                loads[0] += 1
                act.activation(warm[:, 1:2], warm[:, 0:1], func).then_inc(table_loaded, 1)

            def lambda_exponents():
                act.wait_ge(vec_ready, 3)
                act.activation(small[:, 0, :], vec_b[:, V_LAM:V_QG], ACT.Abs).then_inc(lam_a, 1)
                act.wait_ge(lam_a, 1)
                act.activation(small[:, 1, :], small[:, 0, :], ACT.Exp, scale=-1.0).then_inc(lam_a, 1)

            def ffn(n, after):
                u0, f0, t0, pj = U_FFN[n], n * FC, FFN_T0[n], X_OF_FFN[n]

                def silu(m, it=0):
                    b = m % 2
                    act.wait_ge(gate_scaled, f0 + m + 1 + 4 * it)
                    if f0 + m >= 2:
                        act.wait_ge(a_full, f0 + m - 1 + 4 * it)
                    act.activation(sl[:, b, t0:L], gp[:, b, t0:L], ACT.Silu).then_inc(silu_done, 1)

                def hidden_high(m, it=0):
                    b = m % 2
                    act.wait_ge(a_full, f0 + m + 1 + 4 * it)
                    act.activation(ah[:, m, t0:L] if isinstance(it, int) else
                                   ah[:, bass.ds(4 * it + m, 1), t0:L].rearrange("p a l -> p (a l)"),
                                   aa[:, b, t0:L], ACT.Copy).then_inc(ah_ready, 1)

                def pair(p, it=0):
                    for m in (2 * p, 2 * p + 1):
                        silu(m, it)
                        hidden_high(m, it)
                    for j in range(2):
                        out_unit = 2 * p + j + 4 - FFN_IN_UNITS
                        high(u0 + 2 * p + j + 4, it, OUT_K[out_unit] if out_unit >= 0 else KC)

                root_of_h(X_OF_FFN[n])
                high(u0 + 4, 0, KC, (gu_done, f0 + 2))
                load_table(ACT.Silu)
                silu(0)
                silu(1)
                high(u0 + 5, 0)
                hidden_high(0)
                hidden_high(1)
                pair(1)
                with act.Fori(0, 3) as it:
                    pair(2, it)
                    pair(3, it)
                pair(8)
                pair(9)
                pair(10)

                def group(g, it=0):
                    for j in range(3):
                        used = 12 * n + 3 * g + j + 1 + 3 * it
                        next_unit(g, j, it, (out_unit_used, used))
                    square_tile(pj, 2 * g, PROJ_BANKS[pj][g][0], it)
                    square_tile(pj, 2 * g + 1, PROJ_BANKS[pj][g][1], it)
                    if g < 3:
                        next_unit(g, 3, it, None)

                def next_unit(g, j, it, freed):
                    if g < 3:
                        high(u0 + FFN_IN_UNITS + 4 * g + j + 4, it, OUT_K[j], freed)
                    elif after:
                        high(u0 + FFN_UNITS + j, 0, KC, freed)

                if n == 0:
                    lambda_exponents()
                load_table(ACT.Sqrt)
                group(0)
                with act.Fori(0, 2) as it:
                    group(1, it)
                group(3)
                root_of_projection(pj)

            def projection(pj, u0):
                for g in range(4):
                    square_tile(pj, 2 * g, PROJ_BANKS[pj][g][0])
                    square_tile(pj, 2 * g + 1, PROJ_BANKS[pj][g][1])
                    if g < 3:
                        high(u0 + g + 4, 0)
                root_of_projection(pj)

            def attention():
                def squared(t):
                    act.wait_ge(qk_done, t + 1)
                    if t >= 2:
                        act.wait_ge(q_sum, t - 1)
                    act.activation(qs[:, t % 2, :], bank[t % 2][:, 0:L], ACT.Square).then_inc(q_squared, 1)
                    if t >= 2:
                        act.wait_ge(q_rot, t - 1)
                        act.wait_ge(q_cos, t - 1)
                    g = 1 if t < KT_N else 0
                    act.activation(qp[:, t % 2, :], bank[t % 2][:, 0:L], ACT.Copy, scale=qg[:, g:g + 1]).then_inc(q_gained, 1)

                def root(t):
                    act.wait_ge(q_step, 3 * t + 1)
                    v = hs[:, t].rearrange("p c g -> p (c g)")
                    act.activation(v, v, ACT.Sqrt, bias=EPS).then_inc(q_root, 1)

                squared(0)
                squared(1)
                root_of_h(1)
                act.wait_ge(v_done, 1)
                high(U_QKV + 4, 0)
                high(U_QKV + 5, 0)
                for t in range(KT_N, QKT):
                    if t == KT_N:
                        squared(t)
                        root(t - 2)
                    else:
                        root(t - 2)
                        squared(t)
                    if t % 2 and t < QKT - 1:
                        high(U_QKV + 2 + (t - KT_N) // 2 + 4, 0)
                root(QKT - 2)
                root(QKT - 1)
                load_table(ACT.Exp)

                def exponent(a):
                    act.wait_ge(nmax_ready, a + 1)
                    if a >= 4:
                        act.wait_ge(t_done, a - 3)
                    act.activation(prow[:, a % 4, :], S_BANK[a % 4][:, 0:L], ACT.Exp, bias=nmax[:, a:a + 1],
                                   accum_out=rsum[:, a:a + 1]).then_inc(p_exp, 1)

                def place(a):
                    act.wait_ge(t_done, a + 1)
                    if a % TILES_S == 0 and a >= 2 * TILES_S:
                        act.wait_ge(pv_done, 2 * (a // TILES_S) - 2)
                    dst, src = turned_tile(a)
                    act.activation(dst, src, ACT.Copy).then_inc(pt_ready, 1)

                def out_high(pair):
                    act.wait_ge(pv_done, pair + 1)
                    act.activation(xh[:, pair, :], bank[4 + pair % 2][:, 0:L], ACT.Copy).then_inc(oh_ready, 1)

                tiles = NKV * TILES_S
                exponent(0)
                exponent(1)
                for a in range(tiles):
                    if a + 2 < tiles:
                        exponent(a + 2)
                    place(a)
                    j, t = divmod(a - 2, TILES_S)
                    if a >= 2 and t in (4, 8):
                        out_high(2 * j + (t == 8))
                out_high(2 * NKV - 1)
                high(U_WO + 3, 0)
                load_table(ACT.Sqrt)

            def recurrent():
                def split_next(what):
                    n = int(what[1])
                    used = {"x": (xr_done, 2 * n + 2), "g": (g_done, 8 * n + 8), "e": (e_done, 2 * n + 2)}[what[0]]
                    high(U_REC + REC_ORDER.index(what) + WEIGHT_SLOTS, 0, KC, used)

                def conv_high(n):
                    for i in range(2):
                        m = 2 * n + i
                        act.wait_ge(conv_step, 2 * CONVW * n + 2 * CONVW - 1 + i)
                        if n >= 2:
                            act.wait_ge(g_done, 8 * n - 8)
                        act.activation(xch[:, n % 2, i, :], xc[:, n % 2, i, :], ACT.Copy).then_inc(xch_ready, 1)

                def gates(n, d):
                    for o in range(8 * n + 4 * d, 8 * n + 4 * d + 4):
                        g, i = o % 8 // 2, o % 2
                        act.wait_ge(g_done, o + 1)
                        if n >= 2 and o % 8 == 0:
                            act.wait_ge(scan_done, 4 * n - 4)
                        dst = (gr, gi)[g % 2][:, n % 2, d, i, :]
                        v = V_GATEB + g * KC + 2 * n + i
                        act.activation(dst, GATE_BANKS[o % 4][:, 0:L], ACT.Sigmoid, bias=vec_b[:, v:v + 1]).then_inc(sig_done, 1)

                def exponents(n, d):
                    act.wait_ge(sig_done, 8 * n + 4 * d + 4)
                    for i in range(2):
                        act.activation(gw[:, n % 2, d, i, :], gr[:, n % 2, d, i, :], ACT.Exp,
                                       scale=c8[:, d, 2 * n + i:2 * n + i + 1]).then_inc(exp_done, 1)

                def tangents(n, d):
                    act.wait_ge(exp_done, 4 * n + 2 * d + 2)
                    for i in range(2):
                        act.activation(gr[:, n % 2, d, i, :], gr[:, n % 2, d, i, :], ACT.Tanh,
                                       scale=c4[:, d, 2 * n + i:2 * n + i + 1]).then_inc(tanh_done, 1)

                def input_scale(n, d):
                    act.wait_ge(rec_step, 6 * n + 3 * d + 2)
                    act.activation(gw[:, n % 2, d], gw[:, n % 2, d], ACT.Sqrt, scale=-1.0).then_inc(root_done, 1)

                def gelu(n):
                    act.wait_ge(e_scaled, 2 * n + 2)
                    v = mg[:, 2 * n:2 * n + 2, PROJ_T0[4]:L]
                    act.activation(v, v, ACT.Gelu_apprx_tanh).then_inc(gelu_done, 1)

                def y_high(n):
                    act.wait_ge(y_full, n + 1)
                    s, t = slice(2 * n, 2 * n + 2), slice(PROJ_T0[4], L)
                    act.activation((xch[:, n, :, t] if n < 2 else xh[:, s, t]), ys[:, s, t], ACT.Copy).then_inc(yh_ready, 1)

                root_of_h(4)
                load_table(ACT.Sigmoid)
                high(U_REC + 3, 0)
                conv_high(0)
                split_next("x0")
                gates(0, 0)
                conv_high(1)
                split_next("x1")
                gates(0, 1)
                split_next("e0")
                gates(1, 0)
                split_next("g0")
                gates(1, 1)
                split_next("g1")
                for n in range(2):
                    for d in range(2):
                        exponents(n, d)
                        tangents(n, d)
                conv_high(2)
                split_next("x2")
                load_table(ACT.Sqrt)
                input_scale(0, 0)
                input_scale(0, 1)
                input_scale(1, 0)
                input_scale(1, 1)
                load_table(ACT.Sigmoid)
                gates(2, 0)
                conv_high(3)
                gates(2, 1)
                split_next("x3")
                gates(3, 0)
                split_next("e1")
                gates(3, 1)
                for n in (2, 3):
                    for d in range(2):
                        exponents(n, d)
                gelu(0)
                gelu(1)
                for n in (2, 3):
                    for d in range(2):
                        tangents(n, d)
                gelu(2)
                gelu(3)
                y_high(0)
                y_high(1)
                load_table(ACT.Sqrt)
                for n in (2, 3):
                    for d in range(2):
                        input_scale(n, d)
                act.wait_ge(wh_ready, U_ROUT + 1)
                split_next("g3")
                act.wait_ge(e_done, KC)
                y_high(2)
                y_high(3)
                split_next("e2")
                split_next("e3")

            act.dma_start(cst[:, 0:C_ROT], consts[:, 0:C_ROT]).then_inc(s_in, 16)
            act.dma_start(tok_in[0:META, 0, :], meta).then_inc(s_xin, 16)
            act.dma_start(tok_in[0:L - 2 * P, 2, :], x[2 * P - META:SEQ, :]).then_inc(s_xin, 16)
            act.wait_ge(warm_set, 1)
            load_table(ACT.Sqrt)
            act.wait_ge(vec_ready, 2)
            for u in range(2):
                for c in range(KC // 2 * u, KC // 2 * (u + 1)):
                    x_high(0, c)
                high(u, 0)
            for c in range(KC):
                h_square(0, c)
            high(2, 0)
            high(3, 0)
            ffn(0, True)
            make_x(1)
            high(U_FFN[0] + FFN_UNITS + 3, 0)
            attention()
            projection(1, U_WO)
            make_x(2)
            high(U_WO + 3 + 4, 0)
            ffn(1, True)
            make_x(3)
            high(U_FFN[1] + FFN_UNITS + 3, 0)
            ffn(2, True)
            make_x(4)
            recurrent()
            projection(4, U_ROUT)
            make_x(5)
            high(U_ROUT + 3 + 4, 0)
            ffn(3, False)
            for i, t in ((0, 0), (0, 1), (1, 1)):
                act.wait_ge(out_t, 2 * i + t + 1)
                act.activation(tok_out[:, t, 512 * i:512 * i + 512], bank[2 * t + i][:, :], ACT.Copy).then_inc(out_copied[t], 1)

        @block.vector
        def _(dve):
            def low(u, it, kn=KC):
                dve.wait_ge(wh_ready, u + 1 + WEIGHT_SLOTS * it)
                w = raw[:, slot(u), 0:kn * 256]
                dve.tensor_tensor(wl[:, slot(u), 0:kn * 256], w, wh[:, slot(u), 0:kn * 256].bitcast(F32), ALU.subtract).then_inc(w_ready, 1)

            def low_x(n, c):
                t0 = PROJ_T0[n - 1] if n else 0
                g = GAIN(*PRE_GAIN[n], c)
                dve.wait_ge(xh_ready, 8 * n + c + 1)
                dve.scalar_tensor_tensor(xl[:, c, t0:L], h[:, c, t0:L], vec_a[:, g:g + 1], xh[:, c, t0:L].bitcast(F32),
                                         ALU.mult, ALU.subtract).then_inc(x_ready, 1)

            def rc_of_h(n):
                dve.wait_ge(pre_root, n + 1)
                dve.reciprocal(rc_pre[:, :], rc_pre[:, :]).then_inc(rc_ready, 1)

            def r_of_h(n):
                rc_of_h(n)
                dve.wait_ge(r_spread, n + 1)
                dve.tensor_copy(r[:, :], SUM_PRE[:, 0:L]).then_inc(r_ready, 1)
                dve.wait_ge(r_ready, n + 1 if n == 0 else n)

            def add_squares(pj, m, it=0):
                t0 = PROJ_T0[pj]
                dve.wait_ge(sq_ready, 8 * pj + m + 1 + 2 * it)
                dve.wait_ge(acc_step, ACC * pj + m + 2 + 2 * it)
                dve.tensor_tensor(acc[:, t0:L], acc[:, t0:L], sqb[:, m % 2, t0:L], ALU.add).then_inc(acc_step, 1)

            def clear_sum():
                dve.memset(acc[:, :], 0.0).then_inc(acc_step, 2)

            def residual(pj):
                n, t0 = pj + 1, PROJ_T0[pj]
                dve.wait_ge(post_root, pj + 1)
                dve.reciprocal(rc_post[:, :], rc_post[:, :]).then_inc(rt_ready, 1)
                dve.wait_ge(mg_ready, 8 * pj + 8)
                dve.wait_ge(rt_spread, pj + 1)

                def scale(c):
                    dve.tensor_tensor(mg[:, c, t0:L], mg[:, c, t0:L], SUM_POST[:, t0:L], ALU.mult).then_inc(mg_scaled, 1)

                def add(c):
                    dve.wait_ge(mg_scaled, 8 * pj + c + 1)
                    dve.tensor_tensor(h[:, c, t0:L], h[:, c, t0:L], mg[:, c, t0:L], ALU.add).then_inc(h_ready, 1)

                if n < NPROJ:
                    for c in range(KC):
                        scale(c)
                        add(c)
                        if c >= 1:
                            low_x(n, c - 1)
                    low_x(n, KC - 1)
                else:
                    scale(0)
                    for c in range(KC):
                        if c + 1 < KC:
                            scale(c + 1)
                        add(c)

            def ffn(n, after):
                u0, f0, t0, pj = U_FFN[n], n * FC, FFN_T0[n], X_OF_FFN[n]
                r_of_h(X_OF_FFN[n])
                if n == 0:
                    dve.wait_ge(vecs_t, 2)
                    dve.tensor_copy(vec_b[:, :], bank[6][:, 0:VB]).then_inc(vec_ready, 1)

                def scaled(m, it=0):
                    banks = ffn_banks(m)
                    b = m % 2
                    dve.wait_ge(gu_done, f0 + m + 1 + 4 * it)
                    if f0 + m >= 2:
                        dve.wait_ge(silu_done, f0 + m - 1 + 4 * it)
                    dve.tensor_tensor(gp[:, b, t0:L], bank[banks[0]][:, t0:L], r[:, t0:L], ALU.mult).then_inc(gate_scaled, 1)
                    dve.tensor_tensor(up[:, b, t0:L], bank[banks[1]][:, t0:L], r[:, t0:L], ALU.mult).then_inc(up_scaled, 1)

                def hidden(m, it=0):
                    b = m % 2
                    dve.wait_ge(silu_done, f0 + m + 1 + 4 * it)
                    dve.wait_ge(up_scaled, f0 + m + 1 + 4 * it)
                    if f0 + m >= 2:
                        dve.wait_ge(ah_ready, f0 + m - 1 + 4 * it)
                    dve.tensor_tensor(aa[:, b, t0:L], sl[:, b, t0:L], up[:, b, t0:L], ALU.mult).then_inc(a_full, 1)

                def tile_low(m, it=0):
                    b = m % 2
                    dve.wait_ge(ah_ready, f0 + m + 1 + 4 * it)
                    if isinstance(it, int):
                        d, s = al[:, m, t0:L], ah[:, m, t0:L].bitcast(F32)
                    else:
                        d = al[:, bass.ds(4 * it + m, 1), t0:L].rearrange("p a l -> p (a l)")
                        s = ah[:, bass.ds(4 * it + m, 1), t0:L].bitcast(F32).rearrange("p a l -> p (a l)")
                    dve.tensor_tensor(d, aa[:, b, t0:L], s, ALU.subtract).then_inc(a_ready, 1)

                def pair(p, it=0):
                    for j in range(2):
                        scaled(2 * p + j, it)
                        hidden(2 * p + j, it)
                        tile_low(2 * p + j, it)
                    for j in range(2):
                        out_unit = 2 * p + j + 4 - FFN_IN_UNITS
                        low(u0 + 2 * p + j + 4, it, OUT_K[out_unit] if out_unit >= 0 else KC)

                scaled(0)
                scaled(1)
                low(u0 + 4, 0)
                hidden(0)
                hidden(1)
                tile_low(0)
                tile_low(1)
                low(u0 + 5, 0)
                pair(1)
                with dve.Fori(0, 3) as it:
                    pair(2, it)
                    pair(3, it)
                pair(8)
                pair(9)
                pair(10)

                def next_unit(g, j, it):
                    if g < 3:
                        low(u0 + FFN_IN_UNITS + 4 * g + j + 4, it, OUT_K[j])
                    elif after:
                        low(u0 + FFN_UNITS + j, 0)

                def group(g, it=0):
                    for j in range(3):
                        next_unit(g, j, it)
                    if g < 3:
                        add_squares(pj, 2 * g, it)
                        add_squares(pj, 2 * g + 1, it)
                        next_unit(g, 3, it)

                group(0)
                if n == 0:
                    dve.wait_ge(vec_ready, 3)
                    softplus()
                with dve.Fori(0, 2) as it:
                    group(1, it)
                group(3)
                residual(pj)

            def projection(pj, u0):
                for g in range(4):
                    if g < 3:
                        add_squares(pj, 2 * g)
                        add_squares(pj, 2 * g + 1)
                        low(u0 + g + 4, 0)
                residual(pj)

            def attention():
                def head_root_in(t):
                    dve.wait_ge(q_sum, t + 1)
                    dve.tensor_tensor(hs[:, t], QSUM[0:KT, 0:6].rearrange("p (c g) -> p c g", g=2),
                                      rsq[:, :].rearrange("p (c o) -> p c o", o=1).broadcast_to([KT, 3, 2]), ALU.mult).then_inc(q_step, 1)

                def head_factor(t):
                    dve.wait_ge(q_root, t + 1)
                    dve.reciprocal(hs[:, t], hs[:, t]).then_inc(q_step, 1)
                    dve.wait_ge(q_step, 3 * t + 2)
                    dve.tensor_tensor(hs[:, t], hs[:, t], rc_pre[:, :].rearrange("p (c o) -> p c o", o=1).broadcast_to([KT, 3, 2]),
                                      ALU.mult).then_inc(q_step, 1)

                def times_sin(t):
                    dve.wait_ge(q_rot, t + 1)
                    if t >= 2:
                        dve.wait_ge(q_roped, t - 1)
                    dve.tensor_tensor(pad[:, t % 2, 0:L], ROTB[:, 0:L], sin, ALU.mult).then_inc(q_sin, 1)

                def final(t):
                    dve.wait_ge(q_roped, t + 1)
                    dve.wait_ge(q_spread, t + 1)
                    if t < KT_N:
                        dve.tensor_tensor(kd[:, 2 * t, :], qn[:, t % 2, :], QSCALE[:, 0:L], ALU.mult)
                        dve.tensor_tensor(kd[:, 2 * t + 1, :], qn[:, t % 2, :], QSCALE[:, 0:L], ALU.mult).then_inc(q_final, 1)
                    else:
                        dve.tensor_tensor(qt[:, t - KT_N, :], qn[:, t % 2, :], QSCALE[:, 0:L], ALU.mult).then_inc(q_final, 1)

                rc_of_h(1)
                dve.wait_ge(rc_ready, 2)
                dve.tensor_tensor(rsq[:, :], rc_pre[:, :], rc_pre[:, :], ALU.mult).then_inc(rsq_ready, 1)
                dve.wait_ge(v_done, 1)
                for c in range(3):
                    dve.tensor_scalar(vt[:, c, :], bank[2 + c][0:KT, 0:NKV * HD], rc_pre[:, c:c + 1], None, ALU.mult).then_inc(v_ready, 1)
                dve.wait_ge(v_ready, 3)
                dve.memset(vt[0:OVERLAP, 2, :], 0.0).then_inc(v_ready, 1)
                dve.wait_ge(rsq_ready, 1)
                head_root_in(0)
                times_sin(0)
                for t in range(KT_N, QKT):
                    head_factor(t - 2)
                    head_root_in(t - 1)
                    times_sin(t - 1)
                    final(t - 2)
                    if t < KT_N + 3:
                        low(U_QKV + 4 + t - KT_N, 0)
                    elif t % 2 and t < QKT - 1:
                        low(U_QKV + 2 + (t - KT_N) // 2 + 4, 0)
                head_factor(QKT - 2)
                head_root_in(QKT - 1)
                times_sin(QKT - 1)
                final(QKT - 2)
                head_factor(QKT - 1)
                final(QKT - 1)

                def maximum(a):
                    dve.wait_ge(s_done, a + 1)
                    dve.tensor_reduce(nmax[:, a:a + 1], S_BANK[a % 4][:, 0:L], AX_X, ALU.max, negate=True).then_inc(nmax_ready, 1)

                def normalise(a):
                    dve.wait_ge(p_exp, a + 1)
                    dve.reciprocal(rinv[:, a:a + 1], rsum[:, a:a + 1]).then_inc(p_inv, 1)
                    dve.wait_ge(p_inv, a + 1)
                    dve.tensor_scalar(prow[:, a % 4, :], prow[:, a % 4, :], rinv[:, a:a + 1], None, ALU.mult).then_inc(p_norm, 1)

                def out_low(pair):
                    dve.wait_ge(oh_ready, pair + 1)
                    dve.tensor_tensor(xl[:, pair, :], bank[4 + pair % 2][:, 0:L], xh[:, pair, :].bitcast(F32), ALU.subtract).then_inc(o_ready, 1)

                tiles = NKV * TILES_S
                maximum(0)
                maximum(1)
                for a in range(tiles):
                    normalise(a)
                    if a + 2 < tiles:
                        maximum(a + 2)
                    j, t = divmod(a - 3, TILES_S)
                    if a >= 3 and t in (4, 8):
                        out_low(2 * j + (t == 8))
                out_low(2 * NKV - 1)
                low(U_WO + 3, 0)

            def recurrent():
                def x_scaled(n):
                    for i in range(2):
                        m = 2 * n + i
                        dve.wait_ge(xr_done, m + 1)
                        if n:
                            dve.wait_ge(conv_step, 2 * CONVW * n)
                        dve.tensor_tensor(pad[:, i, CONVL:CONVL + L], REC_BANKS["x%d" % n][i][:, 0:L], r[:, :], ALU.mult).then_inc(xr_scaled, 1)

                def e_part(n):
                    for i in range(2):
                        m, t = 2 * n + i, slice(PROJ_T0[4], L)
                        dve.wait_ge(e_done, m + 1)
                        dve.tensor_tensor(mg[:, m, t], REC_BANKS["e%d" % n][i][:, t], r[:, t], ALU.mult).then_inc(e_scaled, 1)

                def split_next(what):
                    low(U_REC + REC_ORDER.index(what) + WEIGHT_SLOTS, 0)

                def conv(n):
                    dve.wait_ge(xr_scaled, 2 * n + 2)
                    if n >= 2:
                        dve.wait_ge(ix_done, 2 * n - 2)
                    for tap in range(CONVW):
                        for i in range(2):
                            m = 2 * n + i
                            v = V_CONVW + tap * KC + m
                            if tap == 0:
                                dve.tensor_scalar(xc[:, n % 2, i, :], pad[:, i, 0:L], vec_b[:, v:v + 1],
                                                  vec_b[:, V_CONVB + m:V_CONVB + m + 1], ALU.mult, ALU.add).then_inc(conv_step, 1)
                            else:
                                dve.wait_ge(conv_step, 2 * (CONVW * n + tap) + i - 1)
                                dve.scalar_tensor_tensor(xc[:, n % 2, i, :], pad[:, i, tap:tap + L], vec_b[:, v:v + 1], xc[:, n % 2, i, :],
                                                         ALU.mult, ALU.add).then_inc(conv_step, 1)

                flat = "p m l -> p (m l)"

                def decay(n, d):
                    fr, fw, fm = (v[:, n % 2, d].rearrange(flat) for v in (gr, gw, gm))
                    dve.wait_ge(tanh_done, 4 * n + 2 * d + 2)
                    if n >= 2:
                        dve.wait_ge(ysum_done, n - 1)
                    dve.scalar_tensor_tensor(fm, fw, 1.0, fr, ALU.add, ALU.mult).then_inc(rec_step, 1)
                    dve.wait_ge(rec_step, 6 * n + 3 * d + 1)
                    dve.scalar_tensor_tensor(fw, fm, 2.0, fm, ALU.subtract, ALU.mult).then_inc(rec_step, 1)
                    dve.tensor_scalar(fr, fm, -1.0, 1.0, ALU.mult, ALU.add).then_inc(rec_step, 1)

                def scans(n, d):
                    if (n, d) != (NB - 1, 1):
                        dve.wait_ge(b_done, 2 * n + d + 1)
                    for i in range(2):
                        a_, b_, o_ = (v[:, n % 2, d, i, :] for v in (gr, gi, gm))
                        if d:
                            a_, b_, o_ = a_[:, ::-1], b_[:, ::-1], o_[:, ::-1]
                        dve.tensor_tensor_scan(o_, a_, b_, 0.0, ALU.mult, ALU.add).then_inc(scan_done, 1)

                def y_low(n):
                    dve.wait_ge(yh_ready, n + 1)
                    s, t = slice(2 * n, 2 * n + 2), slice(PROJ_T0[4], L)
                    dve.tensor_tensor(xl[:, s, t], ys[:, s, t], xh[:, s, t].bitcast(F32), ALU.subtract).then_inc(y_ready, 1)

                r_of_h(4)
                x_scaled(0)
                conv(0)
                low(U_REC + 3, 0)
                x_scaled(1)
                conv(1)
                split_next("x0")
                e_part(0)
                split_next("x1")
                split_next("e0")
                split_next("g0")
                split_next("g1")
                x_scaled(2)
                conv(2)
                decay(0, 0)
                decay(0, 1)
                decay(1, 0)
                decay(1, 1)
                split_next("x2")
                scans(0, 0)
                scans(0, 1)
                x_scaled(3)
                conv(3)
                scans(1, 0)
                scans(1, 1)
                e_part(1)
                split_next("x3")
                split_next("e1")
                dve.wait_ge(wh_ready, U_ROUT)
                dve.wait_ge(landed[slot(U_ROUT)], landed_at[U_ROUT])
                dve.wait_ge(g_done, 8 * 2 + 8)
                dve.tensor_copy(wh[:, slot(U_ROUT), :], raw[:, slot(U_ROUT), :]).then_inc(wh_ready, 1)
                low(U_ROUT, 0)
                e_part(2)
                decay(2, 0)
                e_part(3)
                decay(2, 1)
                decay(3, 0)
                decay(3, 1)
                for n, d in ((2, 0), (2, 1), (3, 0)):
                    dve.wait_ge(root_done, 2 * n + d + 1)
                    dve.wait_ge(ix_done, 2 * n + d + 1)
                    fi, fw = gi[:, n % 2, d].rearrange(flat), gw[:, n % 2, d].rearrange(flat)
                    dve.tensor_tensor(fi, fi, fw, ALU.mult).then_inc(b_done, 1)
                    scans(n, d)
                dve.wait_ge(last_b_done, 1)
                scans(3, 1)
                last = NB - 1
                dve.wait_ge(scan_done, 4 * NB)
                dve.wait_ge(ysum_done, last)
                s, t = slice(2 * last, 2 * last + 2), slice(PROJ_T0[4], L)
                dve.tensor_tensor(ys[:, s, :], gm[:, last % 2, 0], gm[:, last % 2, 1], ALU.add).then_inc(ysum_done, 1)
                dve.wait_ge(ysum_done, NB)
                dve.wait_ge(gelu_done, NB)
                dve.wait_ge(y_full, last)
                dve.tensor_tensor(ys[:, s, t], ys[:, s, t], mg[:, s, t], ALU.mult).then_inc(y_full, 1)
                y_low(2)
                y_low(3)
                split_next("g3")
                split_next("e2")
                split_next("e3")

            def softplus():
                steps = [0]

                def link(ins):
                    steps[0] += 1
                    ins.then_inc(lam_v, 1)
                    dve.wait_ge(lam_v, steps[0])

                e, w, z, zz, p, m0 = (small[:, i, :] for i in (1, 2, 3, 4, 5, 6))
                dve.wait_ge(lam_a, 2)
                link(dve.tensor_scalar(w, e, 2.0, None, ALU.add))
                link(dve.reciprocal(w, w))
                link(dve.tensor_tensor(z, e, w, ALU.mult))
                link(dve.tensor_tensor(zz, z, z, ALU.mult))
                link(dve.tensor_scalar(p, zz, 1.0 / 15, None, ALU.mult))
                for k in (13, 11, 9, 7, 5, 3):
                    link(dve.scalar_tensor_tensor(p, p, 1.0 / k, zz, ALU.add, ALU.mult))
                link(dve.scalar_tensor_tensor(p, p, 1.0, z, ALU.add, ALU.mult))
                link(dve.tensor_scalar(m0, vec_b[:, V_LAM:V_QG], -1.0, 0.0, ALU.mult, ALU.max))
                link(dve.scalar_tensor_tensor(m0, p, 2.0, m0, ALU.mult, ALU.add))
                link(dve.tensor_scalar(c4[:, :, :].rearrange("p d c -> p (d c)"), m0, 4.0, None, ALU.mult))
                link(dve.tensor_scalar(c8[:, :, :].rearrange("p d c -> p (d c)"), m0, -8.0, None, ALU.mult))
                link(dve.tensor_scalar(qg[:, 0:1], vec_b[:, V_QG:V_QG + 1], HD ** -0.5, None, ALU.mult))
                link(dve.tensor_copy(qg[:, 1:2], vec_b[:, V_KG:V_KG + 1]))

            dve.memset(warm[:, :], 1.0).then_inc(warm_set, 1)
            dve.memset(acc[:, :], 0.0).then_inc(acc_step, 2)
            dve.memset(pad[:, :, :], 0.0).then_inc(pad_zero, 1)
            dve.wait_ge(vecs_t, 1)
            dve.tensor_copy(vec_a[:, :], bank[4][:, 0:96]).then_inc(vec_ready, 1)
            dve.tensor_scalar(vec_h[:, :], bank[4][:, 0:96], 0.5, None, ALU.mult).then_inc(vec_ready, 1)
            dve.wait_ge(vec_ready, 2)
            for c in range(KC):
                dve.wait_ge(x_trans, c + 1)
                dve.tensor_copy(h[:, c, :], bank[4 + c % 4][:, 0:L]).then_inc(h_ready, 1)
            for u in range(2):
                for c in range(KC // 2 * u, KC // 2 * (u + 1)):
                    low_x(0, c)
                low(u, 0)
            low(2, 0)
            low(3, 0)

            ffn(0, True)
            low(U_FFN[0] + FFN_UNITS + 3, 0)
            clear_sum()
            attention()
            projection(1, U_WO)
            low(U_WO + 3 + 4, 0)
            clear_sum()
            ffn(1, True)
            low(U_FFN[1] + FFN_UNITS + 3, 0)
            clear_sum()
            ffn(2, True)
            clear_sum()
            dve.memset(pad[:, :, 0:CONVL], 0.0).then_inc(pad_zero, 1)
            dve.memset(pad[:, :, CONVL + L:], 0.0).then_inc(pad_zero, 1)
            recurrent()
            projection(4, U_ROUT)
            low(U_ROUT + 3 + 4, 0)
            clear_sum()
            ffn(3, False)
            dve.wait_ge(out_t, 3)
            dve.wait_ge(out_copied[0], 1)
            dve.tensor_copy(tok_out[:, 0, 512:1024], bank[1][:, :]).then_inc(out_copied[0], 1)

        @block.gpsimd
        def _(pool):
            def sum_squares(n):
                t0 = PROJ_T0[n - 1] if n else 0
                if n:
                    pool.wait_ge(pre_sum, n)
                for c in range(KC):
                    pool.wait_ge(hsq_ready, 8 * n + c + 1)
                    if c == 0:
                        pool.tensor_copy(hacc[:, t0:L], sqh[:, 0, t0:L]).then_inc(hacc_step, 1)
                    else:
                        pool.wait_ge(hacc_step, 8 * n + c)
                        pool.tensor_tensor(hacc[:, t0:L], hacc[:, t0:L], sqh[:, c % 2, t0:L], ALU.add).then_inc(hacc_step, 1)

            def rotary():
                def times_cos(t):
                    pool.wait_ge(q_gained, t + 1)
                    if t >= 2:
                        pool.wait_ge(q_roped, t - 1)
                    pool.tensor_tensor(qc[:, t % 2, :], qp[:, t % 2, :], cos, ALU.mult).then_inc(q_cos, 1)

                def roped(t):
                    pool.wait_ge(q_sin, t + 1)
                    pool.wait_ge(q_cos, t + 1)
                    if t >= 2:
                        pool.wait_ge(q_final, t - 1)
                    pool.tensor_tensor(qn[:, t % 2, :], qc[:, t % 2, :], pad[:, t % 2, 0:L], ALU.add).then_inc(q_roped, 1)

                pool.wait_ge(s_rope, 16)
                times_cos(0)
                for t in range(1, QKT):
                    times_cos(t)
                    roped(t - 1)
                    if t == KT_N + 1:
                        pool.wait_ge(q_final, KT_N)
                        pool.dma_start(kd[HD:P, 0:NKV:2, :], kd[0:HD, 0:NKV:2, :]).then_inc(k_dup, 16)
                        pool.dma_start(kd[0:HD, 1:NKV:2, :], kd[HD:P, 1:NKV:2, :]).then_inc(k_dup, 16)
                roped(QKT - 1)

            def recurrent():
                def conv_low(n):
                    for i in range(2):
                        pool.wait_ge(xch_ready, 2 * n + i + 1)
                        pool.tensor_tensor(xcl[:, n % 2, i, :], xc[:, n % 2, i, :], xch[:, n % 2, i, :].bitcast(F32),
                                           ALU.subtract).then_inc(xcl_ready, 1)

                def gated_input(n):
                    for d in range(2):
                        pool.wait_ge(sig_done, 8 * n + 4 * d + 4)
                        pool.tensor_tensor(gi[:, n % 2, d], gi[:, n % 2, d], xc[:, n % 2], ALU.mult).then_inc(ix_done, 1)

                def scan_input(n):
                    for d in range(2):
                        pool.wait_ge(root_done, 2 * n + d + 1)
                        pool.wait_ge(ix_done, 2 * n + d + 1)
                        pool.tensor_tensor(gi[:, n % 2, d], gi[:, n % 2, d], gw[:, n % 2, d], ALU.mult).then_inc(b_done, 1)

                def y_sum(n):
                    pool.wait_ge(scan_done, 4 * n + 4)
                    pool.tensor_tensor(ys[:, 2 * n:2 * n + 2, :], gm[:, n % 2, 0], gm[:, n % 2, 1], ALU.add).then_inc(ysum_done, 1)

                def y_gated(n):
                    pool.wait_ge(gelu_done, n + 1)
                    pool.wait_ge(ysum_done, n + 1)
                    s, t = slice(2 * n, 2 * n + 2), slice(PROJ_T0[4], L)
                    pool.tensor_tensor(ys[:, s, t], ys[:, s, t], mg[:, s, t], ALU.mult).then_inc(y_full, 1)

                conv_low(0)
                conv_low(1)
                gated_input(0)
                gated_input(1)
                conv_low(2)
                scan_input(0)
                scan_input(1)
                conv_low(3)
                y_sum(0)
                y_sum(1)
                gated_input(2)
                gated_input(3)
                y_gated(0)
                y_gated(1)
                for n in range(2):
                    pool.wait_ge(yh_ready, n + 1)
                    t = slice(PROJ_T0[4], L)
                    pool.tensor_tensor(xcl[:, n, :, t], ys[:, 2 * n:2 * n + 2, t], xch[:, n, :, t].bitcast(F32), ALU.subtract).then_inc(y_ready, 1)
                pool.wait_ge(root_done, 2 * NB)
                pool.wait_ge(ix_done, 2 * NB)
                pool.tensor_tensor(gi[:, 1, 1], gi[:, 1, 1], gw[:, 1, 1], ALU.mult).then_inc(last_b_done, 1)
                y_sum(2)
                y_gated(2)

            sum_squares(0)
            sum_squares(1)
            rotary()
            sum_squares(2)
            sum_squares(3)
            sum_squares(4)
            recurrent()
            sum_squares(5)


_INS = ["x", "meta_tokens", "norm_gains", "ffn_w_in", "ffn_w_out", "attn_w_qkv", "attn_q_gain", "attn_k_gain",
        "attn_w_o", "rec_w_in", "rec_conv_w", "rec_conv_b", "rec_gate_w", "rec_gate_b", "rec_lambda", "rec_w_out"]
_LAYERED = _INS[5:]
_OUT = (1, SEQ, D)


def kernel(**inputs):
    import concourse.bacc as _bacc
    from concourse.bass_utils import run_bass_kernel_spmd as _run

    nc = _bacc.Bacc("TRN2", target_bir_lowering=False, num_devices=1)
    arrays, args = {}, []
    for name in _INS:
        a = np.ascontiguousarray(inputs[name])
        arrays[f"in_{name}"] = a
        ap = nc.dram_tensor(f"in_{name}", a.shape, mybir.dt.from_np(a.dtype), kind="ExternalInput").ap()
        args.append(ap[0] if name == "x" or name in _LAYERED else ap)
    arrays["in_consts"] = shape_constants()
    args.append(nc.dram_tensor("in_consts", (P, C_N), F32, kind="ExternalInput").ap())
    out = nc.dram_tensor("out_0", _OUT, F32, kind="ExternalOutput").ap()
    build(nc, *args, out[0])
    r = _run(nc, [arrays], core_ids=[0])
    return r.results[0]["out_0"]
```
